# Optimizing a Trainium2 kernel written in Bass

```python
import jax, jax.numpy as jnp
from jax import lax
import numpy as np
import math

D_MODEL = 1024
BATCH = 1
SEQ = 512
DEPTH = 2

CHUNK = 64
HEAD_DIM = 64
ROT_DIM = HEAD_DIM // 4
ROPE_THETA = 500000.0
N_HEADS_A = 6
N_HEADS_B = 5
N_HEADS_C = 5
WIDTH_A = N_HEADS_A * HEAD_DIM
WIDTH_B = N_HEADS_B * HEAD_DIM
WIDTH_C = N_HEADS_C * HEAD_DIM
MIX_WIDTH = WIDTH_A + WIDTH_B + WIDTH_C
IDX_HEADS = 8
IDX_DIM = 64
TOPK_MAX = 256
PREV_CHUNKS = 8
BAND = (PREV_CHUNKS + 1) * CHUNK
REL_CLIP = 128
Q_BLOCK = 128
N_BRANCH = 3
FFN_HIDDEN = -(-8 * D_MODEL // (3 * 256)) * 256
RMS_EPS = 1e-6
FORGET_BIAS_LO = 2.0
FORGET_BIAS_HI = 6.0
SPLIT_SIZES = (WIDTH_A, WIDTH_A, WIDTH_A, IDX_HEADS * IDX_DIM, IDX_DIM, IDX_HEADS,
               3 * WIDTH_B, 3 * WIDTH_C, N_HEADS_C, N_BRANCH * D_MODEL)
IN_WIDTH = sum(SPLIT_SIZES)


def rmsnorm(x, g):
    xf = x.astype(jnp.float32)
    y = xf * lax.rsqrt(jnp.mean(xf * xf, axis=-1, keepdims=True) + RMS_EPS)
    return (y * g.astype(jnp.float32)).astype(x.dtype)

def rope_tables(positions):
    inv = ROPE_THETA ** (-jnp.arange(0, ROT_DIM, 2, dtype=jnp.float32) / ROT_DIM)
    ang = positions.astype(jnp.float32)[..., None] * inv
    return jnp.cos(ang), jnp.sin(ang)

def partial_rope(t, cos, sin):
    half = ROT_DIM // 2
    cs = cos[:, :, None, :].astype(t.dtype)
    sn = sin[:, :, None, :].astype(t.dtype)
    x1 = t[..., :half]
    x2 = t[..., half:ROT_DIM]
    return jnp.concatenate([x1 * cs - x2 * sn, x2 * cs + x1 * sn, t[..., ROT_DIM:]], axis=-1)

def dsa_attention(q, k, v, q_idx, k_idx, w_idx):
    B, S = q.shape[0], q.shape[1]
    topk = min(TOPK_MAX, S // 4)
    n_blk = S // Q_BLOCK
    key_chunk = jnp.arange(S) // CHUNK
    scale = HEAD_DIM ** -0.5
    kf = k_idx.astype(jnp.float32)
    gather = jax.vmap(lambda arr, ix: arr[ix])

    def block(i):
        start = i * Q_BLOCK
        qs = lax.dynamic_slice_in_dim(q, start, Q_BLOCK, axis=1)
        qis = lax.dynamic_slice_in_dim(q_idx, start, Q_BLOCK, axis=1).astype(jnp.float32)
        ws = lax.dynamic_slice_in_dim(w_idx, start, Q_BLOCK, axis=1).astype(jnp.float32)
        q_chunk = (start + jnp.arange(Q_BLOCK)) // CHUNK
        idx_scores = jnp.einsum('bqhs,bqh->bqs',
                                jax.nn.relu(jnp.einsum('bqhd,bsd->bqhs', qis, kf)), ws)
        adm = key_chunk[None, :] <= q_chunk[:, None]
        idx_scores = jnp.where(adm[None], idx_scores, -jnp.inf)
        _, sel = lax.top_k(idx_scores, topk)
        valid = (sel // CHUNK) <= q_chunk[None, :, None]
        k_sel = gather(k, sel)
        v_sel = gather(v, sel)
        logits = jnp.einsum('bqhd,bqkhd->bhqk', qs, k_sel).astype(jnp.float32) * scale
        logits = jnp.where(valid[:, None], logits, -jnp.inf)
        p = jax.nn.softmax(logits, axis=-1).astype(v.dtype)
        return jnp.einsum('bhqk,bqkhd->bqhd', p, v_sel)

    out = lax.map(block, jnp.arange(n_blk))
    return jnp.moveaxis(out, 0, 1).reshape(B, S, -1)

def chunk_band_attention(q, k, v, rel_bias):
    B, S, H, Dh = q.shape
    n_c = S // CHUNK
    pad = PREV_CHUNKS * CHUNK
    qc = q.reshape(B, n_c, CHUNK, H, Dh)
    kp = jnp.pad(k, ((0, 0), (pad, 0), (0, 0), (0, 0))).reshape(B, n_c + PREV_CHUNKS, CHUNK, H, Dh)
    vp = jnp.pad(v, ((0, 0), (pad, 0), (0, 0), (0, 0))).reshape(B, n_c + PREV_CHUNKS, CHUNK, H, Dh)
    kband = jnp.concatenate([kp[:, j:j + n_c] for j in range(PREV_CHUNKS + 1)], axis=2)
    vband = jnp.concatenate([vp[:, j:j + n_c] for j in range(PREV_CHUNKS + 1)], axis=2)
    logits = jnp.einsum('bcqhd,bckhd->bchqk', qc, kband).astype(jnp.float32) * (Dh ** -0.5)
    qi = jnp.arange(CHUNK)
    kj = jnp.arange(BAND)
    dist = jnp.clip(qi[:, None] + pad - kj[None, :], -REL_CLIP, REL_CLIP) + REL_CLIP
    bias = rel_bias[:, dist].astype(jnp.float32)
    band_chunk = jnp.arange(n_c)[:, None] - PREV_CHUNKS + kj[None, :] // CHUNK
    valid = band_chunk >= 0
    logits = jnp.where(valid[None, :, None, None, :], logits + bias[None, None], -jnp.inf)
    p = jax.nn.softmax(logits, axis=-1).astype(v.dtype)
    out = jnp.einsum('bchqk,bckhd->bcqhd', p, vband)
    return out.reshape(B, S, H * Dh)

def forgetting_attention(q, k, v, f_logit):
    B, S, H, Dh = q.shape
    n_blk = S // Q_BLOCK
    log_f = jax.nn.log_sigmoid(f_logit.astype(jnp.float32))
    F = jnp.moveaxis(jnp.cumsum(log_f, axis=1), 1, 2)
    key_pos = jnp.arange(S)
    scale = Dh ** -0.5

    def block(i):
        start = i * Q_BLOCK
        qs = lax.dynamic_slice_in_dim(q, start, Q_BLOCK, axis=1)
        Fq = lax.dynamic_slice_in_dim(F, start, Q_BLOCK, axis=2)
        logits = (jnp.einsum('bqhd,bshd->bhqs', qs, k).astype(jnp.float32) * scale
                  + Fq[..., :, None] - F[:, :, None, :])
        qpos = start + jnp.arange(Q_BLOCK)
        logits = jnp.where((key_pos[None, :] <= qpos[:, None])[None, None], logits, -jnp.inf)
        p = jax.nn.softmax(logits, axis=-1).astype(v.dtype)
        return jnp.einsum('bhqs,bshd->bqhd', p, v)

    out = lax.map(block, jnp.arange(n_blk))
    return jnp.moveaxis(out, 0, 1).reshape(B, S, H * Dh)

def hybrid_mixer(h, cos, sin, w_in, b_in, rel_bias, w_branch, w_out):
    B, S, D = h.shape
    proj = h @ w_in + b_in
    parts = []
    off = 0
    for size in SPLIT_SIZES:
        parts.append(proj[..., off:off + size])
        off += size
    qa, ka, va, qi, ki, wi, qkv_b, qkv_c, f_c, gate_logits = parts
    qa = partial_rope(qa.reshape(B, S, N_HEADS_A, HEAD_DIM), cos, sin)
    ka = partial_rope(ka.reshape(B, S, N_HEADS_A, HEAD_DIM), cos, sin)
    va = va.reshape(B, S, N_HEADS_A, HEAD_DIM)
    qi = partial_rope(qi.reshape(B, S, IDX_HEADS, IDX_DIM), cos, sin)
    ki = partial_rope(ki[:, :, None, :], cos, sin)[:, :, 0, :]
    wi = wi * (IDX_HEADS ** -0.5 * IDX_DIM ** -0.5)
    o_a = dsa_attention(qa, ka, va, qi, ki, wi)
    qkv_b = qkv_b.reshape(B, S, 3, N_HEADS_B, HEAD_DIM)
    o_b = chunk_band_attention(qkv_b[:, :, 0], qkv_b[:, :, 1], qkv_b[:, :, 2], rel_bias)
    qkv_c = qkv_c.reshape(B, S, 3, N_HEADS_C, HEAD_DIM)
    o_c = forgetting_attention(qkv_c[:, :, 0], qkv_c[:, :, 1], qkv_c[:, :, 2], f_c)
    gates = jax.nn.sigmoid(gate_logits.reshape(B, S, N_BRANCH, D))
    y = (gates[:, :, 0] * (o_a @ w_branch[:WIDTH_A])
         + gates[:, :, 1] * (o_b @ w_branch[WIDTH_A:WIDTH_A + WIDTH_B])
         + gates[:, :, 2] * (o_c @ w_branch[WIDTH_A + WIDTH_B:]))
    return y @ w_out

def swiglu(h, w_ffn_in, w_ffn_out):
    gu = h @ w_ffn_in
    g, u = gu[..., :FFN_HIDDEN], gu[..., FFN_HIDDEN:]
    return (jax.nn.silu(g) * u) @ w_ffn_out

def first_inputs(seed: int = 0) -> dict:
    key = jax.random.key(seed)
    ks = jax.random.split(key, 16)
    f32 = jnp.float32
    D = D_MODEL
    nrm = jax.random.normal
    x = nrm(ks[0], (BATCH, SEQ, D), f32)
    c = nrm(ks[1], (BATCH, D), f32)
    offset = jax.random.randint(ks[2], (BATCH, 1), 0, 4096, dtype=jnp.int32)
    positions = offset + jnp.arange(SEQ, dtype=jnp.int32)[None, :]
    ada_w = 0.5 * D ** -0.5 * nrm(ks[3], (DEPTH, D, 6 * D), f32)
    ada_b = 0.01 * nrm(ks[4], (DEPTH, 6 * D), f32)
    norm1_g = 1.0 + 0.05 * nrm(ks[5], (DEPTH, D), f32)
    w_in = D ** -0.5 * nrm(ks[6], (DEPTH, D, IN_WIDTH), f32)
    f_off = sum(SPLIT_SIZES[:8])
    forget_b = jax.random.uniform(ks[7], (DEPTH, N_HEADS_C), f32, FORGET_BIAS_LO, FORGET_BIAS_HI)
    b_in = (0.01 * nrm(ks[8], (DEPTH, IN_WIDTH), f32)).at[:, f_off:f_off + N_HEADS_C].add(forget_b)
    rel_bias = 0.5 * nrm(ks[9], (DEPTH, N_HEADS_B, 2 * REL_CLIP + 1), f32)
    w_branch = WIDTH_B ** -0.5 * nrm(ks[10], (DEPTH, MIX_WIDTH, D), f32)
    w_out = D ** -0.5 * nrm(ks[11], (DEPTH, D, D), f32)
    norm2_g = 1.0 + 0.05 * nrm(ks[12], (DEPTH, D), f32)
    w_ffn_in = D ** -0.5 * nrm(ks[13], (DEPTH, D, 2 * FFN_HIDDEN), f32)
    w_ffn_out = FFN_HIDDEN ** -0.5 * nrm(ks[14], (DEPTH, FFN_HIDDEN, D), f32)
    final_g = 1.0 + 0.05 * nrm(ks[15], (D,), f32)
    return {'x': x, 'c': c, 'positions': positions, 'ada_w': ada_w, 'ada_b': ada_b,
            'norm1_g': norm1_g, 'w_in': w_in, 'b_in': b_in, 'rel_bias': rel_bias,
            'w_branch': w_branch, 'w_out': w_out, 'norm2_g': norm2_g,
            'w_ffn_in': w_ffn_in, 'w_ffn_out': w_ffn_out, 'final_g': final_g}

def first_block(x, c, positions, ada_w, ada_b, norm1_g, w_in, b_in, rel_bias,
              w_branch, w_out, norm2_g, w_ffn_in, w_ffn_out, final_g):
    cos, sin = rope_tables(positions)
    cond = jax.nn.silu(c)
    for l in range(DEPTH):
        mod = (cond @ ada_w[l] + ada_b[l])[:, None, :]
        sh1, sc1, g1, sh2, sc2, g2 = jnp.split(mod, 6, axis=-1)
        h = rmsnorm(x, norm1_g[l]) * (1 + sc1) + sh1
        x = x + g1 * hybrid_mixer(h, cos, sin, w_in[l], b_in[l], rel_bias[l], w_branch[l], w_out[l])
        h = rmsnorm(x, norm2_g[l]) * (1 + sc2) + sh2
        x = x + g2 * swiglu(h, w_ffn_in[l], w_ffn_out[l])
    return rmsnorm(x, final_g)


CTX_LEN = 256
GRID_W = 64
POOL_WIDTH = 512
POOL_WINDOWS = (2, 4, 8, 16)
POOL_GROUPS = len(POOL_WINDOWS)
POOL_GC = POOL_WIDTH // POOL_GROUPS
N_HEADS = 4
V_DIM = 2 * HEAD_DIM
QK_WIDTH = N_HEADS * 2 * HEAD_DIM
ATTN_WIDTH = N_HEADS * V_DIM
MIX_WIDTH_2 = POOL_WIDTH + ATTN_WIDTH
IN_WIDTH_2 = POOL_WIDTH + 2 * QK_WIDTH + ATTN_WIDTH
ROT_AXIS = HEAD_DIM // 2
ROPE_BASE = 10000.0
D_FF = 4 * D_MODEL
N_ADA = 6
EPS = 1e-6


def rms_norm(x, g):
    xf = x.astype(jnp.float32)
    y = xf * lax.rsqrt(jnp.mean(xf * xf, axis=-1, keepdims=True) + EPS)
    return (y * g.astype(jnp.float32)).astype(x.dtype)

def modulate(h, shift, scale):
    return h * (1 + scale) + shift

def ada_params(cvec, w_ada, b_ada):
    return jnp.split(jax.nn.silu(cvec) @ w_ada + b_ada, N_ADA, axis=-1)

def axial_rope(n, dtype):
    rows = n // GRID_W
    row = jnp.repeat(jnp.arange(rows), GRID_W).astype(jnp.float32)
    col = jnp.tile(jnp.arange(GRID_W), rows).astype(jnp.float32)
    inv = ROPE_BASE ** (-jnp.arange(0, ROT_AXIS, 2, dtype=jnp.float32) / ROT_AXIS)
    ang = jnp.concatenate([row[:, None] * inv, col[:, None] * inv], axis=-1)
    return jnp.cos(ang).astype(dtype), jnp.sin(ang).astype(dtype)

def apply_rope(x, cos, sin):
    x1, x2 = x[..., :HEAD_DIM // 2], x[..., HEAD_DIM // 2:]
    return jnp.concatenate([x1 * cos - x2 * sin, x1 * sin + x2 * cos], axis=-1)

def centred_mean(x, w):
    b, n, ch = x.shape
    xf = x.astype(jnp.float32)
    cs = jnp.concatenate([jnp.zeros((b, 1, ch), jnp.float32), jnp.cumsum(xf, axis=1)], axis=1)
    t = jnp.arange(n)
    lo = jnp.clip(t - w // 2, 0, n)
    hi = jnp.clip(t + w - w // 2, 0, n)
    s = cs[:, hi] - cs[:, lo]
    cnt = (hi - lo).astype(jnp.float32)
    return (s / cnt[None, :, None]).astype(x.dtype)

def pool_mixer(u, w_pool, s_pool):
    b, n, _ = u.shape
    groups = jnp.split(u, POOL_GROUPS, axis=-1)
    y = jnp.stack([centred_mean(g, w) - g for g, w in zip(groups, POOL_WINDOWS)], axis=2)
    y = jnp.einsum('bngc,gcd->bngd', y, w_pool).reshape(b, n, POOL_WIDTH)
    return y * s_pool

def split_heads(z):
    b, n, _ = z.shape
    u, q, k, v = jnp.split(z, [POOL_WIDTH, POOL_WIDTH + QK_WIDTH, POOL_WIDTH + 2 * QK_WIDTH], axis=-1)
    q = q.reshape(b, n, 2 * N_HEADS, HEAD_DIM).transpose(0, 2, 1, 3)
    k = k.reshape(b, n, 2 * N_HEADS, HEAD_DIM).transpose(0, 2, 1, 3)
    v = v.reshape(b, n, N_HEADS, V_DIM).transpose(0, 2, 1, 3)
    return u, q, k, v

def diff_attn(q, k, v, lam):
    b, _, nq, _ = q.shape
    nk = k.shape[2]
    s = jnp.einsum('bhqd,bhkd->bhqk', q, k).astype(jnp.float32) * (HEAD_DIM ** -0.5)
    a = jax.nn.softmax(s, axis=-1).reshape(b, N_HEADS, 2, nq, nk)
    w = a[:, :, 0] - lam * a[:, :, 1]
    return jnp.einsum('bhqk,bhkd->bhqd', w.astype(v.dtype), v)

def diff_attn_blocks(q, k, v, lam):
    b, hh, n, d = q.shape
    nb = n // Q_BLOCK
    qb = q.reshape(b, hh, nb, Q_BLOCK, d).transpose(2, 0, 1, 3, 4)
    o = lax.map(lambda qblk: diff_attn(qblk, k, v, lam), qb)
    return o.transpose(1, 2, 0, 3, 4).reshape(b, N_HEADS, n, V_DIM)

def head_out(o, g_sub, lam_init):
    o = rms_norm(o, g_sub) * (1.0 - lam_init)
    b, h, n, d = o.shape
    return o.transpose(0, 2, 1, 3).reshape(b, n, h * d)

def sq_relu_mlp(h, w1, w2):
    return jnp.square(jax.nn.relu(h @ w1)) @ w2

def second_inputs(seed: int = 0) -> dict:
    key = jax.random.key(seed)
    ks = jax.random.split(key, 24)
    f = jnp.float32
    nrm = lambda k, shape, s: jax.random.normal(k, shape, f) * s
    L = DEPTH
    return {
        "x": nrm(ks[0], (BATCH, SEQ, D_MODEL), 1.0),
        "c": nrm(ks[1], (BATCH, D_MODEL), 1.0),
        "ctx": nrm(ks[2], (BATCH, CTX_LEN, D_MODEL), 1.0),
        "c_ctx": nrm(ks[3], (D_MODEL,), 1.0),
        "w_ada": nrm(ks[4], (L, D_MODEL, N_ADA * D_MODEL), 0.02),
        "b_ada": nrm(ks[5], (L, N_ADA * D_MODEL), 0.01),
        "g_mix": 1.0 + nrm(ks[6], (L, D_MODEL), 0.02),
        "g_mlp": 1.0 + nrm(ks[7], (L, D_MODEL), 0.02),
        "w_in": nrm(ks[8], (L, D_MODEL, IN_WIDTH_2), D_MODEL ** -0.5),
        "w_pool": nrm(ks[9], (L, POOL_GROUPS, POOL_GC, POOL_GC), POOL_GC ** -0.5),
        "s_pool": 1.0 + nrm(ks[10], (L, POOL_WIDTH), 0.1),
        "lam_q1": nrm(ks[11], (L, HEAD_DIM), 0.1),
        "lam_k1": nrm(ks[12], (L, HEAD_DIM), 0.1),
        "lam_q2": nrm(ks[13], (L, HEAD_DIM), 0.1),
        "lam_k2": nrm(ks[14], (L, HEAD_DIM), 0.1),
        "g_subln": 1.0 + nrm(ks[15], (L, V_DIM), 0.02),
        "w_out": nrm(ks[16], (L, MIX_WIDTH_2, D_MODEL), MIX_WIDTH_2 ** -0.5),
        "w_mlp1": nrm(ks[17], (L, D_MODEL, D_FF), D_MODEL ** -0.5),
        "w_mlp2": nrm(ks[18], (L, D_FF, D_MODEL), D_FF ** -0.5),
        "g_final": 1.0 + nrm(ks[19], (D_MODEL,), 0.02),
    }

def second_block(x, c, ctx, c_ctx, w_ada, b_ada, g_mix, g_mlp, w_in, w_pool, s_pool,
              lam_q1, lam_k1, lam_q2, lam_k2, g_subln, w_out, w_mlp1, w_mlp2, g_final):
    n = x.shape[1]
    cos, sin = axial_rope(n, x.dtype)
    c_lat = c[:, None, :]
    c_cx = c_ctx[None, None, :]
    for l in range(DEPTH):
        last = l == DEPTH - 1
        sa, ca, ga, sm, cm, gm = ada_params(c_lat, w_ada[l], b_ada[l])
        sa_c, ca_c, ga_c, sm_c, cm_c, gm_c = ada_params(c_cx, w_ada[l], b_ada[l])
        lam_init = 0.8 - 0.6 * math.exp(-0.3 * l)
        lam = (jnp.exp(jnp.sum(lam_q1[l].astype(jnp.float32) * lam_k1[l].astype(jnp.float32)))
               - jnp.exp(jnp.sum(lam_q2[l].astype(jnp.float32) * lam_k2[l].astype(jnp.float32)))
               + lam_init)

        h = modulate(rms_norm(x, g_mix[l]), sa, ca)
        hc = modulate(rms_norm(ctx, g_mix[l]), sa_c, ca_c)
        u, q, k, v = split_heads(h @ w_in[l])
        uc, qc, kc, vc = split_heads(hc @ w_in[l])
        q = apply_rope(q, cos, sin)
        k = apply_rope(k, cos, sin)
        k_all = jnp.concatenate([kc, k], axis=2)
        v_all = jnp.concatenate([vc, v], axis=2)
        o_att = diff_attn_blocks(q, k_all, v_all, lam)
        mix = jnp.concatenate([pool_mixer(u, w_pool[l], s_pool[l]),
                               head_out(o_att, g_subln[l], lam_init)], axis=-1)
        x = x + ga * (mix @ w_out[l])

        x = x + gm * sq_relu_mlp(modulate(rms_norm(x, g_mlp[l]), sm, cm), w_mlp1[l], w_mlp2[l])

        if not last:
            o_c = diff_attn(qc, kc, vc, lam)
            mix_c = jnp.concatenate([pool_mixer(uc, w_pool[l], s_pool[l]),
                                     head_out(o_c, g_subln[l], lam_init)], axis=-1)
            ctx = ctx + ga_c * (mix_c @ w_out[l])
            ctx = ctx + gm_c * sq_relu_mlp(modulate(rms_norm(ctx, g_mlp[l]), sm_c, cm_c),
                                           w_mlp1[l], w_mlp2[l])
    return rms_norm(x, g_final)


def setup_inputs(seed=0):
    out = dict(first_inputs(seed))
    for name, value in second_inputs(seed + 1).items():
        if name != "x":
            out[name + "_2"] = value
    return out


def reference(
    x, c, positions, ada_w, ada_b, norm1_g, w_in, b_in, rel_bias, w_branch, w_out, norm2_g,
    w_ffn_in, w_ffn_out, final_g, c_2, ctx_2, c_ctx_2, w_ada_2, b_ada_2, g_mix_2, g_mlp_2,
    w_in_2, w_pool_2, s_pool_2, lam_q1_2, lam_k1_2, lam_q2_2, lam_k2_2, g_subln_2, w_out_2,
    w_mlp1_2, w_mlp2_2, g_final_2,
):
    x = first_block(
        x, c, positions, ada_w, ada_b, norm1_g, w_in, b_in, rel_bias, w_branch, w_out, norm2_g,
        w_ffn_in, w_ffn_out, final_g,
    )
    return second_block(
        x, c_2, ctx_2, c_ctx_2, w_ada_2, b_ada_2, g_mix_2, g_mlp_2, w_in_2, w_pool_2, s_pool_2,
        lam_q1_2, lam_k1_2, lam_q2_2, lam_k2_2, g_subln_2, w_out_2, w_mlp1_2, w_mlp2_2,
        g_final_2,
    )


_drawn_inputs = setup_inputs


def setup_inputs(seed=0):
    import zlib

    import numpy as np

    out = dict(_drawn_inputs(seed))
    spreads = {}
    factors = {'ada_b': 3.679,
     'norm1_g': 4.099,
     'rel_bias': 3.373,
     'g_mix_2': 7.047,
     'g_mlp_2': 3.836,
     'lam_q2_2': 5.216,
     'g_subln_2': 8.0}
    for name, (base, spread) in spreads.items():
        noise = np.random.default_rng([zlib.crc32(name.encode()), seed]).standard_normal(out[name].shape)
        drawn = base * np.exp(spread * noise) if base else spread * noise
        out[name] = __import__('jax').numpy.asarray(drawn.astype(out[name].dtype))
    for name, factor in factors.items():
        out[name] = (out[name] * factor).astype(out[name].dtype)
    return out
```

```python
from contextlib import ExitStack, contextmanager

import numpy as np

import concourse.bass as bass
from concourse import mybir
from concourse.alu_op_type import AluOpType as ALU

F32 = mybir.dt.float32
F32R = mybir.dt.float32r
BF16 = mybir.dt.bfloat16
I32 = mybir.dt.int32
ACT = mybir.ActivationFunctionType
AX = mybir.AxisListType

P = 128
D = 1024
KT = D // P
T = 512
TT = T // P
TC = 256
TA = TC + T
HD = 64
CHUNK = 64
EPS = 1e-6
NEG = -1.0e30
TAKEN = -3.0e38
TOPK = min(256, T // 4)

HA, HB, HC, HI = 6, 5, 5, 8
WA, WB, WC = HA * HD, HB * HD, HC * HD
OQA, OKA, OVA = 0, WA, 2 * WA
OQI = 3 * WA
OKI = OQI + HI * HD
OWI = OKI + HD
OB = OWI + HI
OC = OB + 3 * WB
OF = OC + 3 * WC
OG = OF + HC
INW = OG + 3 * D
FFN = -(-8 * D // 768) * 256
TILES = ([OQA + P * i for i in range(6)] + [OQI + P * i for i in range(4)] + [OKI]
         + [o + P * i for o in (OB, OB + WB, OC, OC + WC) for i in range(3)] + [OF])
TA0, TQI, TKI, TB0, TC0, TF = 0, 6, 10, 11, 17, 23
REL = 128

NH2 = 4
POOLW = 512
WINDOWS = (2, 4, 8, 16)
INW2 = 2048
DFF = 4 * D

DEPTH = 2
PAD = 8
UPAD = TA + 4 * PAD
REL_ROW = 512

SLOT = 9 * 2 * P
CREDIT = 4096


class Progress:

    def __init__(self, nc, sem, engine=None, step=1):
        self.sem, self.step, self.steps = sem, step, 0
        self.count = CREDIT
        (engine or nc.sync).sem_inc(sem, self.count)

    def after(self, instruction):
        instruction.then_inc(self.sem, self.step)
        self.builder.waiting.pop(id(self.engine), None)
        self.count = self.count + self.step
        self.steps += self.step
        return (self, self.count, self.steps)


class Buffer:

    def __init__(self, writer):
        self.writer, self.last = writer, []


class Builder:

    def __init__(self, nc, plan):
        self.nc, self.plan, self.n_loops = nc, plan, 0
        self.ctx = ExitStack()
        self.counters, self.seen, self.waiting = [], {}, {}
        self.pe = self.counter("pe_done", nc.tensor)
        self.act = self.counter("act_done", nc.scalar)
        self.dve = self.counter("dve_done", nc.vector)
        self.pool = self.counter("pool_done", nc.gpsimd)
        self.held = self.ctx.enter_context(nc.semaphore("held"))

    def counter(self, name, engine=None, step=1):
        c = Progress(self.nc, self.ctx.enter_context(self.nc.semaphore(name)), engine, step)
        c.engine, c.builder = engine, self
        self.counters.append(c)
        return c

    def wait(self, engine, *tokens):
        for token in tokens:
            if token is None:
                continue
            if isinstance(token, list):
                self.wait(engine, *token)
                continue
            counter, count, steps = token
            key = (id(engine), id(counter))
            if steps is not None and self.seen.get(key, -1) >= steps:
                continue
            waiting = self.waiting.setdefault(id(engine), set())
            if not isinstance(count, int) and id(counter) in waiting:
                self.hold(engine)
                waiting.clear()
            engine.wait_ge(counter.sem, count)
            waiting.add(id(counter))
            if not isinstance(count, int) and engine not in (self.nc.tensor, self.nc.scalar):
                self.hold(engine)
                waiting.clear()
            if steps is not None:
                self.seen[key] = steps

    def hold(self, engine):
        engine.sem_inc(self.held, 1)

    def acquire(self, buffer):
        self.wait(buffer.writer, *buffer.last)

    @contextmanager
    def loop(self, trips, buffers, engines=None):
        key = self.n_loops
        self.n_loops += 1
        plan = self.plan.get(key, {})
        for b in buffers:
            self.acquire(b)
        if engines is None:
            self.hold(self.nc.tensor)
        start = [(c, c.count, c.steps) for c in self.counters]
        at = {id(c): n for n, (c, _, _) in enumerate(start)}
        before = [b.last for b in buffers]
        seen = dict(self.seen)
        delta = plan.get("delta", [0] * len(start))
        ends = plan.get("ends", [None] * len(buffers))
        kw = {} if engines is None else {"engines": engines}
        with self.nc.Fori(0, trips, **kw) as i:
            self.seen = {}
            for (c, count, _), d in zip(start, delta):
                if d:
                    c.count = count + i * d
            carried = []
            for b, end in zip(buffers, ends):
                if end is not None:
                    b.last = [(start[n][0], start[n][1] + i * delta[n] + (off - delta[n]), None)
                              for n, off in end]
                else:
                    b.last = list(b.last)
                carried.append(b.last)
            yield i
            found = [c.steps - s for c, _, s in start]
            now = []
            for b, was in zip(buffers, carried):
                now.append(None if b.last is was else
                           [(at[id(c)], steps - start[at[id(c)]][2]) for c, _, steps in b.last])
            self.plan[key] = {"delta": found, "ends": now}
        for (c, count, steps), d in zip(start, found):
            c.count = count + trips * d
            c.steps = steps + trips * d
        for b, end, was in zip(buffers, now, before):
            b.last = was if end is None else [
                (start[n][0], start[n][1] + (trips - 1) * found[n] + off,
                 start[n][2] + (trips - 1) * found[n] + off) for n, off in end]
        self.seen = seen


def dyn(ap, index):
    if isinstance(index, int):
        return ap[:, index]
    got = ap[:, bass.ds(index, 1)]
    if len(got.shape) == 3:
        return got.rearrange("p a n -> p (a n)")
    return got


def program(nc, plan, a, n_first=2, n_second=2):
    b = Builder(nc, plan)
    tensor, vector, scalar, gpsimd, sync = nc.tensor, nc.vector, nc.scalar, nc.gpsimd, nc.sync
    pe, act, dve, pool = b.pe, b.act, b.dve, b.pool

    names = {}

    def sb(scope, name, shape, dt=F32):
        names[name] = names.get(name, 0) + 1
        if names[name] > 1:
            name = f"{name}_{names[name]}"
        return scope.enter_context(nc.sbuf_tensor(name, shape, dt))

    top = b.ctx
    X = sb(top, "x", [P, KT, TA])
    raw = sb(top, "raw_weights", [P, 2, SLOT])
    whi = sb(top, "weights_hi", [P, 2, SLOT], F32R)
    wlo = sb(top, "weights_lo", [P, 2, SLOT], F32R)
    cst = sb(top, "constants", [P, 6, P])
    ident, perm, meanm, dup, dupperm, sel = (cst[:, n, :] for n in range(6))
    identb = sb(top, "identity_bf16", [P, P], BF16)
    causal = sb(top, "causal_bf16", [P, P], BF16)
    eps = sb(top, "eps", [P, 1])
    cond = sb(top, "cond", [P, KT, 32])
    mod = sb(top, "mod", [P, 48, 2])
    col = sb(top, "norm_columns", [P, 2, KT, 2])
    small = sb(top, "small", [P, 16, 4])
    psum = top.enter_context(nc.psum_tensor("psum", [P, 8 * 512], F32))
    bank = [psum[:, 512 * n:512 * n + 512] for n in range(8)]
    bank_use = [Buffer(tensor) for _ in range(8)]

    arrived = [b.counter(f"weights_arrived{r}", step=16) for r in range(2)]
    loaded = [b.counter(f"small_load{n}", step=16) for n in range(8)]
    loads = [0]
    raw_use = [Buffer(sync), Buffer(sync)]
    split_use = [Buffer(gpsimd), Buffer(gpsimd)]
    ring = [0]

    def load(dst, src):
        loads[0] += 1
        return loaded[loads[0] % 8].after(sync.dma_start(dst, src))

    def fetch(kt, cols, pieces):
        r = ring[0] % 2
        ring[0] += 1
        view = raw[:, r, 0:kt * cols].rearrange("p (k n) -> p k n", k=kt)
        b.acquire(raw_use[r])
        for ks, cs, rows, src in pieces:
            token = arrived[r].after(sync.dma_start(view[0:rows, ks, cs], src))
        return r, view, token

    def weights(kt, cols, pieces):
        r, _, token = fetch(kt, cols, pieces)
        n = kt * cols
        b.acquire(split_use[r])
        b.wait(gpsimd, token)
        hi_done = pool.after(gpsimd.tensor_scalar(whi[:, r, 0:n], raw[:, r, 0:n], 1.0, 1.0, ALU.mult, ALU.mult))
        b.wait(gpsimd, hi_done)
        done = pool.after(gpsimd.tensor_tensor(wlo[:, r, 0:n], raw[:, r, 0:n], whi[:, r, 0:n].bitcast(F32),
                                               ALU.subtract))
        raw_use[r].last = [done]
        hi = whi[:, r, 0:n].rearrange("p (k n) -> p k n", k=kt)
        lo = wlo[:, r, 0:n].rearrange("p (k n) -> p k n", k=kt)
        return r, hi, lo, done

    def rows_of(w, l, r0, kt, c0, cols):
        if l is None:
            v = w[r0:r0 + kt * P] if isinstance(r0, int) else w[bass.ds(r0, kt * P)]
        else:
            v = w[bass.ds(l, 1)].rearrange("l r c -> (l r) c") if not isinstance(l, int) else w[l]
            v = v[r0:r0 + kt * P] if isinstance(r0, int) else v[bass.ds(r0, kt * P)]
        v = v.rearrange("(k p) c -> p k c", p=P)
        return v[:, :, c0:c0 + cols] if isinstance(c0, int) else v[:, :, bass.ds(c0, cols)]

    def matrix(w, l, c0, cols, kt=KT, r0=0):
        return weights(kt, cols, [(slice(0, kt), slice(0, cols), P, rows_of(w, l, r0, kt, c0, cols))])

    def product(out, stationary, moving, first, last):
        (sh, sl), (mh, ml) = stationary, moving
        tensor.matmul(out, sh, mh, start=first, stop=False)
        tensor.matmul(out, sh, ml, start=False, stop=False)
        return tensor.matmul(out, sl, mh, start=False, stop=last)

    small_use = {}
    t_const = load(cst[:], a["consts"])
    t_x = load(X[:, :, TC:TA], a["x_t"].rearrange("(k p) t -> p k t", p=P))
    t_ctx = load(X[:, :, 0:TC], a["ctx_t"].rearrange("(k p) t -> p k t", p=P))
    with ExitStack() as s:
        cm = sb(s, "causal_f32", [P, P])
        t_cm = load(cm[:], a["causal"])
        b.wait(vector, t_cm, t_const, t_x)
        dve.after(vector.tensor_copy(identb[:], ident))
        dve.after(vector.tensor_copy(causal[:], cm[:]))
        dve.after(vector.memset(eps[:], EPS))
        dve.after(vector.memset(small[:], 0.0))
        t_init = dve.after(vector.memset(raw[:], 0.0))
        raw_use[0].last = [t_init]
        raw_use[1].last = [t_init]
        for e in (sync, tensor, scalar):
            b.wait(e, t_init, t_const, t_x, t_ctx)
    START = t_init

    def all_done(*engines):
        for e in engines:
            for c in (pe, act, dve):
                if c.steps:
                    b.wait(e, (c, c.count, c.steps))

    def condition(sources):
        with ExitStack() as s:
            cin = sb(s, "cond_in", [P, 2, KT])
            sg = sb(s, "cond_sigmoid", [P, 2, KT])
            all_done(sync, vector)
            t = [load(cin[:, m, :], src) for m, src in enumerate(sources)]
            z = dve.after(vector.memset(cond[:], 0.0))
            m = len(sources)
            b.wait(scalar, t)
            t = act.after(scalar.activation(sg[:, 0:m, :], cin[:, 0:m, :], ACT.Sigmoid))
            b.wait(vector, t, z)
            for n in range(m):
                dve.after(vector.tensor_tensor(cond[:, :, n], cin[:, n, :], sg[:, n, :], ALU.mult))
            all_done(sync)

    def ada(w, bias, l, m):
        with ExitStack() as s:
            rows = sb(s, "ada_rows", [P, 2, 512])
            bcol = sb(s, "ada_bias", [P, 48])
            row_use = Buffer(scalar)
            all_done(sync, scalar, vector, tensor)
            t_b = load(bcol[:], bias)
            b.wait(vector, t_b)
            with b.loop(6, [*raw_use, *bank_use[0:4], row_use]) as i:
                for half in range(2):
                    b.acquire(bank_use[half])
                    for q in range(2):
                        c0 = i * 1024 + (half * 2 + q) * 256
                        r, view, t = fetch(KT, 256, [(slice(0, KT), slice(0, 256), P,
                                                      rows_of(w, l, 0, KT, c0, 256))])
                        b.wait(tensor, t)
                        for kk in range(2):
                            for g in range(4):
                                ins = tensor.matmul(bank[half][32 * g:32 * g + 32, 256 * q:256 * q + 256],
                                                    cond[:, 4 * kk + g, :], view[:, 4 * kk + g, :],
                                                    start=kk == 0, stop=kk == 1, tile_position=(0, 32 * g))
                        t_rows = pe.after(ins)
                        raw_use[r].last = [t_rows]
                    b.wait(scalar, t_rows)
                    if half == 0:
                        b.acquire(row_use)
                    t_copy = act.after(scalar.copy(rows[:, half, :], bank[half][:, :]))
                    bank_use[half].last = [t_copy]
                    b.acquire(bank_use[2 + half])
                    b.wait(tensor, t_copy)
                    for n in range(4):
                        ins = tensor.matmul(bank[2 + half][:, n * m:n * m + m], rows[:, half, n * P:n * P + P],
                                            sel[:, 0:m], start=n == 0, stop=n == 3, skip_group_check=True)
                    t_cols = pe.after(ins)
                    b.wait(vector, t_cols)
                    bc = bcol[:, bass.ds(i * 8 + half * 4, 4)]
                    for mm in range(m):
                        t_mod = dve.after(vector.tensor_tensor(
                            mod[:, bass.ds(i * 8 + half * 4, 4), mm],
                            bank[2 + half][:, 0:4 * m].rearrange("p (n m) -> p n m", m=m)[:, :, mm], bc, ALU.add))
                    bank_use[2 + half].last = [t_mod]
                    if half == 1:
                        row_use.last = [t_cols]
            all_done(vector, scalar, tensor, sync)

    def norm_scales(g, sc, sh, m):
        b.wait(vector, (dve, dve.count, dve.steps))
        t = dve.after(vector.scalar_tensor_tensor(out=col[:, 0, :, m], in0=mod[:, sc * 8:sc * 8 + 8, m], scalar=1.0,
                                                  in1=g, op0=ALU.add, op1=ALU.mult))
        t = dve.after(vector.tensor_copy(col[:, 1, :, m], mod[:, sh * 8:sh * 8 + 8, m]))
        return t

    def mean_square(s, x0, x1, tmp, sq_use, src=None):
        n = x1 - x0
        rstd = tmp["rstd"][:, 0:n]
        b.acquire(bank_use[7])
        for k in range(KT):
            q = k % 2
            b.acquire(sq_use[q])
            t = act.after(scalar.activation(tmp["sq"][:, q, 0:n], X[:, k, x0:x1], ACT.Square))
            b.wait(tensor, t)
            t = pe.after(tensor.matmul(bank[7][:, 0:n], meanm, tmp["sq"][:, q, 0:n], start=k == 0, stop=k == KT - 1))
            sq_use[q].last = [t]
        b.wait(scalar, t)
        t = act.after(scalar.activation(rstd, bank[7][:, 0:n], ACT.Sqrt, bias=eps[:, 0:1]))
        bank_use[7].last = [t]
        b.wait(vector, t)
        t = dve.after(vector.reciprocal(rstd, rstd))
        b.wait(vector, t)
        return rstd

    def norm(segments, hh, hl):
        with ExitStack() as s:
            tmp = {"rstd": sb(s, "rstd", [P, 512]), "sq": sb(s, "squares", [P, 2, 512])}
            sq_use = [Buffer(scalar), Buffer(scalar)]
            all_done(scalar, vector, tensor)
            for x0, x1, h0, m in segments:
                n = x1 - x0
                rstd = mean_square(s, x0, x1, tmp, sq_use)
                all_done(vector)
                free = [None, None]
                for k in range(KT):
                    q = k % 2
                    u = tmp["sq"][:, q, 0:n]
                    b.wait(vector, free[q])
                    t = dve.after(vector.scalar_tensor_tensor(out=u, in0=X[:, k, x0:x1], scalar=col[:, 0, k, m:m + 1],
                                                              in1=rstd, op0=ALU.mult, op1=ALU.mult))
                    b.wait(scalar, t)
                    th = act.after(scalar.activation(hh[:, k, h0:h0 + n], u, ACT.Identity, bias=col[:, 1, k, m:m + 1]))
                    b.wait(vector, th)
                    free[q] = dve.after(vector.scalar_tensor_tensor(
                        out=hl[:, k, h0:h0 + n], in0=u, scalar=col[:, 1, k, m:m + 1],
                        in1=hh[:, k, h0:h0 + n].bitcast(F32), op0=ALU.add, op1=ALU.subtract))
                all_done(scalar, vector, tensor)

    def split_out(hi, lo, value, token):
        b.wait(scalar, token)
        t = act.after(scalar.copy(hi, value))
        b.wait(vector, t, token)
        return dve.after(vector.tensor_tensor(lo, value, hi.bitcast(F32), ALU.subtract))

    def transposed(slot, c, h, chunks, banks, k_rows=None):
        r, hi, lo, ready = slot
        b.wait(tensor, ready)
        for (c0, c1), bk in zip(chunks, banks):
            b.acquire(bank_use[bk])
            kt = hi.shape[1]
            for k in range(kt):
                n = P if k_rows is None else k_rows[k]
                xh, xl = h(k)
                ins = product(bank[bk][:, 0:c1 - c0], (hi[0:n, k, c:c + P], lo[0:n, k, c:c + P]),
                              (xh[0:n, c0:c1], xl[0:n, c0:c1]), k == 0, k == kt - 1)
        t = pe.after(ins)
        split_use[r].last = [t]
        return t

    def natural(slot, c, n, h, tok0, bk, o0=0):
        r, hi, lo, ready = slot
        b.wait(tensor, ready)
        b.acquire(bank_use[bk])
        for k in range(KT):
            xh, xl = h(k)
            ins = product(bank[bk][:, o0:o0 + n], (xh[:, tok0:tok0 + P], xl[:, tok0:tok0 + P]),
                          (hi[:, k, c:c + n], lo[:, k, c:c + n]), k == 0, k == KT - 1)
        t = pe.after(ins)
        split_use[r].last = [t]
        return t

    ALLBUF = [*raw_use, *split_use, *bank_use]

    first = ExitStack()
    hh = sb(first, "h_hi", [P, KT, T], F32R)
    hl = sb(first, "h_lo", [P, KT, T], F32R)
    ropec = sb(first, "rope_cos", [P, T])
    ropes = sb(first, "rope_sin", [P, T])
    pcol = sb(first, "layer_columns", [P, 2 * KT + len(TILES) + 3 * KT])
    wicol = sb(first, "index_weights", [P, TT, HI])
    stat = sb(first, "softmax_stats", [P, 4, 4])

    def h1(k):
        return hh[:, k, :], hl[:, k, :]

    def rope_tables():
        with ExitStack() as s:
            pi_ = sb(s, "pos_int", [P, T], I32)
            ang = sb(s, "angle", [P, T])
            turns = sb(s, "turns", [P, T])
            red = sb(s, "reduced", [P, T])
            ti = load(pi_[:], a["positions"].to_broadcast((P, T)))
            tc = load(small[:, 0, 0:2], a["rope_cols"])
            b.wait(vector, tc, ti)

            def step(ins):
                t = dve.after(ins)
                b.wait(vector, t)
                return t
            step(vector.tensor_copy(ang[:], pi_[:]))
            step(vector.tensor_scalar(ang[:], ang[:], small[:, 0, 0:1], None, ALU.mult))
            magic = 1.5 * 2.0 ** 23
            tau = 2.0 * np.pi
            parts = [6.28125]
            parts.append(float(np.float32(np.round((tau - parts[0]) * 2 ** 21) / 2 ** 21)))
            parts.append(float(tau - parts[0] - parts[1]))
            for quarter, out in ((0.25, ropec), (0.0, ropes)):
                step(vector.tensor_scalar(turns[:], ang[:], float(1.0 / tau), quarter, ALU.mult, ALU.add))
                step(vector.tensor_scalar(turns[:], turns[:], magic, None, ALU.add))
                step(vector.tensor_scalar(turns[:], turns[:], magic, None, ALU.subtract))
                src = ang
                for part in parts:
                    step(vector.scalar_tensor_tensor(out=red[:], in0=turns[:], scalar=-part, in1=src[:],
                                                     op0=ALU.mult, op1=ALU.add))
                    src = red
                if quarter:
                    step(vector.tensor_scalar(red[:], red[:], float(np.pi / 2), None, ALU.add))
                t = step(vector.tensor_scalar(red[:], red[:], 3.14159, -3.14159, ALU.min, ALU.max))
                b.wait(scalar, t)
                t = act.after(scalar.activation(out[:], red[:], ACT.Sin))
                b.wait(vector, t)
            step(vector.tensor_scalar(ropes[:], ropes[:], small[:, 0, 1:2], None, ALU.mult))
            all_done(sync, scalar, tensor)

    def rope(t_in, x, cos, sin, tmp, tmp_use, bk, perm=perm):
        b.wait(tensor, t_in)
        b.acquire(bank_use[bk])
        t = pe.after(tensor.matmul(bank[bk][:, 0:x.shape[1]], perm, x, start=True, stop=True))
        b.wait(vector, t)
        b.acquire(tmp_use)
        t1 = dve.after(vector.tensor_tensor(tmp, bank[bk][:, 0:x.shape[1]], sin, ALU.mult))
        bank_use[bk].last = [t1]
        t2 = dve.after(vector.tensor_tensor(x, x, cos, ALU.mult))
        b.wait(vector, t1, t2)
        t3 = dve.after(vector.tensor_tensor(x, x, tmp, ALU.add))
        tmp_use.last = [t3]
        return t3

    def first_layer(l):
        wi = a["w_in"]
        all_done(sync)
        t_cols = load(pcol[:], a["cols1"][bass.ds(l, 1)].rearrange("l p n -> (l p) n"))
        ada(a["ada_w"], a["ada_b_cols"][bass.ds(l, 1)].rearrange("l p n -> (l p) n"), l, 1)
        bt = pcol[:, 2 * KT:2 * KT + len(TILES)]
        bg = pcol[:, 2 * KT + len(TILES):]
        b.wait(vector, t_cols)
        b.wait(scalar, t_cols)
        norm_scales(pcol[:, 0:KT], 1, 0, 0)
        norm([(TC, TA, 0, 0)], hh, hl)

        mix = ExitStack()
        oh = sb(mix, "o_hi", [P, 9, T], F32R)
        ol = sb(mix, "o_lo", [P, 9, T], F32R)
        att = ExitStack()
        maska = sb(att, "select_mask", [P, TT, T], BF16)

        with ExitStack() as s:
            work = sb(s, "index_scores", [P, 3, T])
            qi = sb(s, "index_q", [P, 4, T])
            ki = sb(s, "index_k", [P, T])
            relu = sb(s, "relu_scores", [P, 3, T])
            tmp = relu[:, 2, :]
            tmp_use = Buffer(vector)
            all_done(tensor, vector, scalar)
            t_q = []
            for half in range(2):
                slot = matrix(wi, l, OQI + 256 * half, 256)
                for q in range(2):
                    n = 2 * half + q
                    t = transposed(slot, q * P, h1, [(0, T)], [n])
                    b.wait(scalar, t)
                    t = act.after(scalar.activation(qi[:, n, :], bank[n][:, :], ACT.Identity, bias=bt[:, TQI + n:TQI + n + 1]))
                    bank_use[n].last = [t]
                    t_q.append(t)
            slot = matrix(wi, l, OKI, P)
            t = transposed(slot, 0, h1, [(0, T)], [4])
            b.wait(scalar, t)
            t_k = act.after(scalar.activation(ki[:], bank[4][:, :], ACT.Identity, bias=bt[:, TKI:TKI + 1]))
            bank_use[4].last = [t_k]
            for n in range(4):
                t_q[n] = rope(t_q[n], qi[:, n, :], ropec[:], ropes[:], tmp, tmp_use, 5 + n % 2)
            b.wait(tensor, t_k)
            b.acquire(bank_use[7])
            for n in range(TT):
                ins = tensor.transpose(bank[7][:, n * P:n * P + P], ki[:, n * P:n * P + P], ident)
            t = pe.after(ins)
            b.wait(vector, t)
            t_w = dve.after(vector.tensor_scalar(
                wicol[:], bank[7][:, :].rearrange("p (n c) -> p n c", n=TT)[:, :, HD:HD + HI],
                float(HI ** -0.5 * HD ** -0.5), None, ALU.mult))
            bank_use[7].last = [t_w]
            b.acquire(bank_use[5])
            b.acquire(bank_use[6])
            tensor.matmul(bank[5][:, :], dup, ki[:], start=True, stop=True)
            t = pe.after(tensor.matmul(bank[6][:, :], dupperm, ki[:], start=True, stop=True))
            b.wait(vector, t)
            b.acquire(tmp_use)
            t1 = dve.after(vector.tensor_tensor(ki[:], bank[5][:, :], ropec[:], ALU.mult))
            t2 = dve.after(vector.tensor_tensor(tmp, bank[6][:, :], ropes[:], ALU.mult))
            bank_use[5].last = [t1]
            bank_use[6].last = [t2]
            b.wait(vector, t1, t2)
            t_k = dve.after(vector.tensor_tensor(ki[:], ki[:], tmp, ALU.add))
            b.wait(tensor, t_k)
            b.wait(scalar, t_k)
            relu_use = [Buffer(scalar), Buffer(scalar)]
            n = 0
            done = [None] * 3
            for i in range(1, TT):
                w = (i + 1) * P
                for h in range(HI):
                    bk, q = n % 4, n % 2
                    n += 1
                    p0 = HD * (h % 2)
                    b.acquire(bank_use[bk])
                    t = pe.after(tensor.matmul(bank[bk][:, 0:w], qi[p0:p0 + HD, h // 2, i * P:i * P + P],
                                               ki[p0:p0 + HD, 0:w], start=True, stop=True))
                    b.wait(scalar, t)
                    b.acquire(relu_use[q])
                    t = act.after(scalar.activation(relu[:, q, 0:w], bank[bk][:, 0:w], ACT.Relu))
                    bank_use[bk].last = [t]
                    b.wait(vector, t, t_w, done[i - 1])
                    wc = wicol[:, i, h:h + 1]
                    if h == 0:
                        t = dve.after(vector.tensor_scalar(work[:, i - 1, 0:w], relu[:, q, 0:w], wc, None, ALU.mult))
                    else:
                        t = dve.after(vector.scalar_tensor_tensor(out=work[:, i - 1, 0:w], in0=relu[:, q, 0:w], scalar=wc,
                                                                  in1=work[:, i - 1, 0:w], op0=ALU.mult, op1=ALU.add))
                    done[i - 1] = t
                    relu_use[q].last = [t]
            for i in range(1, TT):
                b.wait(vector, done[i - 1])
                done[i - 1] = dve.after(vector.memset(work[0:CHUNK, i - 1, (i + 1) * P - CHUNK:(i + 1) * P], NEG))
            top8 = small[:, 1:7, :].rearrange("p a c -> p (a c)")
            b.wait(vector, *done)
            chain = [Buffer(vector) for _ in range(3)]
            for i in range(3):
                chain[i].last = [done[i]]
            with b.loop(TOPK // 8, chain, engines=[mybir.EngineType.DVE]) as _:
                tops = []
                for i in range(3):
                    b.acquire(chain[i])
                    tops.append(dve.after(vector.max(top8[:, 8 * i:8 * i + 8], work[:, i, 0:(i + 2) * P])))
                for i in range(3):
                    w = work[:, i, 0:(i + 2) * P]
                    b.wait(vector, tops[i])
                    chain[i].last = [dve.after(vector.match_replace(
                        out=w, in_to_replace=top8[:, 8 * i:8 * i + 8], in_values=w, imm_value=TAKEN))]
            for i in range(3):
                b.acquire(chain[i])
                dve.after(vector.tensor_scalar(maska[:, i + 1, 0:(i + 2) * P], work[:, i, 0:(i + 2) * P],
                                               -2.9e38, NEG, ALU.is_gt, ALU.mult))
            t = dve.after(vector.memset(maska[:, 0, 0:P], 0.0))
            b.wait(vector, t)
            dve.after(vector.memset(maska[0:CHUNK, 0, CHUNK:P], NEG))
            all_done(tensor, vector, scalar, sync)

        qk = sb(att, "qk", [P, 6, T])
        val = sb(att, "values", [P, TT, WA])
        bval = sb(att, "value_bias", [P, WA])
        logit = sb(att, "logits", [P, 2, T])
        prob = sb(att, "probabilities", [P, 2, T])
        probt = sb(att, "probabilities_t", [P, 2, T])
        biast = sb(att, "bias_tile", [P, 2, T])
        relt = sb(att, "bias_diagonals", [P, 384])
        frow = sb(att, "forget", [P, 3, T])
        fcol = sb(att, "forget_columns", [P, TT, HC])

        def project(o_q, o_k, o_v, n_heads, tile0, with_rope, extra=0):
            nt = 3
            all_done(sync, vector, scalar, tensor)
            t_b = load(bval[:, 0:n_heads * HD], a["b_in"][bass.ds(l, 1), o_v:o_v + n_heads * HD].to_broadcast((P, n_heads * HD)))
            tmp_use = Buffer(vector)
            n = 0
            ts = []
            for which, o in ((0, o_q), (1, o_k)):
                for c0, cols in ((0, 256), (256, 128)):
                    slot = matrix(wi, l, o + c0, cols)
                    for q in range(cols // P):
                        tile = which * 3 + (c0 // P) + q
                        bk = n % 4
                        n += 1
                        t = transposed(slot, q * P, h1, [(0, T)], [bk])
                        b.wait(vector, t)
                        t = dve.after(vector.tensor_scalar(qk[:, tile, :], bank[bk][:, :], bt[:, tile0 + tile:tile0 + tile + 1],
                                                           HD ** -0.5 if which == 0 else 1.0, ALU.add, ALU.mult))
                        bank_use[bk].last = [t]
                        if with_rope:
                            ts.append((t, tile))
            if with_rope:
                for t, tile in ts:
                    b.wait(vector, t)
                    rope(t, qk[:, tile, :], ropec[:], ropes[:], biast[:, 0, :], tmp_use, 5 + tile % 2)
            wv = n_heads * HD
            b.wait(vector, t_b)
            for c0 in (0, 256):
                cols = min(256, wv - c0) + (extra if c0 else 0)
                nv = min(256, wv - c0)
                slot = matrix(wi, l, o_v + c0, cols)
                for n in range(TT):
                    t = natural(slot, 0, nv, h1, n * P, n)
                    b.wait(vector, t)
                    t = dve.after(vector.tensor_tensor(val[:, n, c0:c0 + nv], bank[n][:, 0:nv], bval[:, c0:c0 + nv], ALU.add))
                    bank_use[n].last = [t]
            return slot, nv

        def attend(n_heads, tile0, kind):
            all_done(tensor, vector, scalar, sync)
            logit_use = [Buffer(vector), Buffer(vector)]
            prob_use = [Buffer(scalar), Buffer(scalar)]
            probt_use = [Buffer(scalar), Buffer(scalar)]
            bias_use = [Buffer(vector if kind == "B" else scalar) for _ in range(2)]
            relt_use = Buffer(sync)
            units = [(h, i) for h in range(n_heads) for i in range(TT)]
            st = {}

            def prepare(h):
                if kind == "B":
                    b.acquire(relt_use)
                    src = a["rel"]
                    t = load(relt[:], bass.AP(src.tensor, l * (HB * REL_ROW) + h * REL_ROW, [[1, P], [1, 384]]))
                    b.wait(vector, t)
                    b.acquire(bias_use[h % 2])
                    bt_ = biast[:, h % 2, :]
                    t1 = dve.after(vector.tensor_copy(bt_[:, 256:512], relt[:, 256:0:-1]))
                    t2 = dve.after(vector.tensor_copy(bt_[:, 0:256], relt[:, 383:384].to_broadcast((P, 256))))
                    b.wait(vector, t1, t2)
                    t = dve.after(vector.memset(bt_[0:CHUNK, 448:512], NEG))
                    b.wait(vector, t)
                    relt_use.last = [t]
                if kind == "C":
                    b.acquire(bank_use[6 + h % 2])
                    st["nf", h] = pe.after(tensor.matmul(bank[6 + h % 2][:, :], negsel[0:HC, h, :], frow[0:HC, 2, :],
                                                         start=True, stop=True))

            def scores(u):
                h, i = units[u]
                if i == 0:
                    prepare(h)
                w = (i + 1) * P
                p0 = HD * (h % 2)
                bk = u % 2
                b.acquire(bank_use[bk])
                if kind == "A":
                    tensor.matmul(bank[bk][:, 0:w], identb[:], maska[:, i, 0:w], start=True, stop=False)
                if kind == "C":
                    tensor.matmul(bank[bk][:, w - P:w], identb[:], causal[:], start=True, stop=False)
                q_ = qk[p0:p0 + HD, h // 2, i * P:i * P + P]
                k_ = qk[p0:p0 + HD, 3 + h // 2, 0:w]
                if kind == "C":
                    ins = tensor.matmul(bank[bk][:, w - P:w], q_, k_[:, w - P:w], start=False, stop=True)
                    if i:
                        ins = tensor.matmul(bank[bk][:, 0:w - P], q_, k_[:, 0:w - P], start=True, stop=True)
                else:
                    ins = tensor.matmul(bank[bk][:, 0:w], q_, k_, start=kind == "B", stop=True)
                st["s", u] = pe.after(ins)

            def soften(u):
                h, i = units[u]
                w = (i + 1) * P
                bk, q = u % 2, u % 2
                nm, rs = stat[:, u % 4, 0:1], stat[:, u % 4, 1:2]
                if kind == "A":
                    b.wait(vector, st["s", u])
                    t = dve.after(vector.tensor_reduce(nm, bank[bk][:, 0:w], AX.X, ALU.max, negate=True))
                    src, scale = bank[bk][:, 0:w], 1.0
                else:
                    if kind == "B":
                        extra_logit = biast[:, h % 2, T - w:T]
                    else:
                        b.wait(scalar, st["nf", h])
                        b.acquire(bias_use[q])
                        extra_logit = biast[:, q, 0:w]
                        t = act.after(scalar.activation(extra_logit, bank[6 + h % 2][:, 0:w], ACT.Identity,
                                                        bias=fcol[:, i, h:h + 1]))
                        if i == TT - 1:
                            bank_use[6 + h % 2].last = [t]
                        b.wait(vector, t)
                    b.wait(vector, st["s", u])
                    b.acquire(logit_use[q])
                    t = dve.after(vector.tensor_tensor_reduce(
                        out=logit[:, q, 0:w], in0=bank[bk][:, 0:w], in1=extra_logit, scale=-1.0, scalar=3e38,
                        op0=ALU.add, op1=ALU.min, accum_out=nm))
                    bank_use[bk].last = [t]
                    if kind == "C":
                        bias_use[q].last = [t]
                    elif i == TT - 1:
                        bias_use[h % 2].last = [t]
                    src, scale = logit[:, q, 0:w], -1.0
                b.wait(scalar, t)
                b.acquire(prob_use[q])
                t = act.after(scalar.activation(prob[:, q, 0:w], src, ACT.Exp, bias=nm, scale=scale, accum_out=rs))
                if kind == "A":
                    bank_use[bk].last = [t]
                else:
                    logit_use[q].last = [t]
                st["e", u] = t

            def normalise(u):
                h, i = units[u]
                w = (i + 1) * P
                q = u % 2
                rs, rr = stat[:, u % 4, 1:2], stat[:, u % 4, 2:3]
                b.wait(vector, st["e", u])
                t = dve.after(vector.reciprocal(rr, rs))
                b.wait(vector, t)
                t = dve.after(vector.tensor_scalar(prob[:, q, 0:w], prob[:, q, 0:w], rr, None, ALU.mult))
                b.wait(tensor, t)
                bk = 2 + q
                b.acquire(bank_use[bk])
                for j in range(i + 1):
                    ins = tensor.transpose(bank[bk][:, j * P:j * P + P], prob[:, q, j * P:j * P + P], ident)
                t = pe.after(ins)
                prob_use[q].last = [t]
                b.wait(scalar, t)
                b.acquire(probt_use[q])
                t = act.after(scalar.copy(probt[:, q, 0:w], bank[bk][:, 0:w]))
                bank_use[bk].last = [t]
                st["t", u] = t

            def values(u):
                h, i = units[u]
                q = u % 2
                p0 = HD * (h % 2)
                ob = 4 + (h // 2) % 2
                b.wait(tensor, st["t", u])
                if h % 2 == 0 and i == 0:
                    b.acquire(bank_use[ob])
                for j in range(i + 1):
                    ins = tensor.matmul(bank[ob][p0:p0 + HD, i * P:i * P + P], val[:, j, h * HD:h * HD + HD],
                                        probt[:, q, j * P:j * P + P], start=j == 0, stop=j == i)
                t = pe.after(ins)
                probt_use[q].last = [t]
                if i == TT - 1 and (h % 2 == 1 or h == n_heads - 1):
                    n = p0 + HD
                    tile = tile0 + h // 2
                    t = split_out(oh[0:n, tile, :], ol[0:n, tile, :], bank[ob][0:n, :], t)
                    bank_use[ob].last = [t]

            for u in range(len(units) + 2):
                if u < len(units):
                    scores(u)
                    soften(u)
                if 1 <= u <= len(units):
                    normalise(u - 1)
                if u >= 2:
                    values(u - 2)
            all_done(tensor, vector, scalar, sync)

        project(OQA, OKA, OVA, HA, TA0, True)
        attend(HA, 0, "A")
        project(OB, OB + WB, OB + 2 * WB, HB, TB0, False)
        attend(HB, 3, "B")
        slot, c_f = project(OC, OC + WC, OC + 2 * WC, HC, TC0, False, extra=P)
        t = transposed(slot, c_f, h1, [(0, T)], [4])
        z, m, F = (frow[0:HC, n, :] for n in range(3))
        b.wait(scalar, t)
        t = act.after(scalar.activation(z, bank[4][0:HC, :], ACT.Identity, bias=bt[0:HC, TF:TF + 1]))
        bank_use[4].last = [t]
        b.wait(vector, t)
        t = dve.after(vector.scalar_tensor_tensor(out=m, in0=z, scalar=-1.0, in1=z, op0=ALU.mult, op1=ALU.max))
        b.wait(scalar, t)
        t = act.after(scalar.activation(m, m, ACT.Exp, scale=-1.0))
        b.wait(scalar, t)
        t = act.after(scalar.activation(m, m, ACT.Ln, bias=1.0))
        b.wait(vector, t)
        t = dve.after(vector.scalar_tensor_tensor(out=z, in0=z, scalar=0.0, in1=m, op0=ALU.min, op1=ALU.subtract))
        t1 = dve.after(vector.memset(logit[0:HC, 0, :], 1.0))
        b.wait(vector, t, t1)
        t = dve.after(vector.tensor_tensor_scan(F, logit[0:HC, 0, :], z, 0.0, ALU.mult, ALU.add))
        b.wait(tensor, t)
        b.acquire(bank_use[7])
        for n in range(TT):
            ins = tensor.matmul(bank[7][:, n * HC:n * HC + HC], F[:, n * P:n * P + P], ident[0:HC, 0:HC],
                                start=n == 0, stop=n == TT - 1, skip_group_check=True)
        t = pe.after(ins)
        b.wait(vector, t)
        t = dve.after(vector.tensor_copy(fcol[:].rearrange("p n h -> p (n h)"), bank[7][:, 0:TT * HC]))
        bank_use[7].last = [t]
        attend(HC, 6, "C")
        att.close()

        ys = ExitStack()
        yh = sb(ys, "y_hi", [P, KT, T], F32R)
        yl = sb(ys, "y_lo", [P, KT, T], F32R)
        all_done(tensor, vector, scalar, sync)
        with ExitStack() as s:
            gate = sb(s, "gates", [P, 6, T])
            gate_use = [Buffer(scalar) for _ in range(6)]
            acc = gate
            branch_rows = [P, P, P, P, P, HD, P, P, HD]
            branch_start = [0, P, 2 * P, WA, WA + P, WA + 2 * P, WA + WB, WA + WB + P, WA + WB + 2 * P]
            y_use = Buffer(scalar)
            with b.loop(KT // 2, [*ALLBUF, *gate_use]) as jj:
                for br in range(3):
                    slot = matrix(wi, l, OG + br * D + jj * 256, 256)
                    for q in range(2):
                        bk = (2 * br + q) % 2
                        g = 2 * br + q
                        t = transposed(slot, q * P, h1, [(0, T)], [bk])
                        b.wait(scalar, t)
                        b.acquire(gate_use[g])
                        t = act.after(scalar.activation(gate[:, g, :], bank[bk][:, :], ACT.Sigmoid,
                                                        bias=bg[:, bass.ds(br * KT + jj * 2 + q, 1)]))
                        bank_use[bk].last = [t]
                wb = a["w_branch"][bass.ds(l, 1)].rearrange("l r c -> (l r) c")
                cs = bass.ds(jj * 256, 256)
                pieces = [(slice(n, n + 1), slice(0, 256), rows,
                           wb[r0:r0 + rows, cs].rearrange("(k p) c -> p k c", k=1))
                          for n, (r0, rows) in enumerate(zip(branch_start, branch_rows))]
                slot = weights(9, 256, pieces)
                r, hi, lo, ready = slot
                b.wait(tensor, ready)
                for q in range(2):
                    tb = []
                    for br in range(3):
                        bk = 2 + 3 * q + br
                        b.acquire(bank_use[bk])
                        for n in range(3):
                            k = 3 * br + n
                            rows = branch_rows[k]
                            ins = product(bank[bk][:, :], (hi[0:rows, k, q * P:q * P + P], lo[0:rows, k, q * P:q * P + P]),
                                          (oh[0:rows, k, :], ol[0:rows, k, :]), n == 0, n == 2)
                        tb.append(pe.after(ins))
                    split_use[r].last = [tb[-1]]
                    ts = []
                    for br in range(3):
                        b.wait(vector, tb[br], (act, act.count, act.steps))
                        g = gate[:, 2 * br + q, :]
                        t = dve.after(vector.tensor_tensor(g, bank[2 + 3 * q + br][:, :], g, ALU.mult))
                        bank_use[2 + 3 * q + br].last = [t]
                        ts.append(t)
                    b.wait(vector, *ts)
                    t = dve.after(vector.tensor_tensor(gate[:, q, :], gate[:, q, :], gate[:, 2 + q, :], ALU.add))
                    b.wait(vector, t)
                    t = dve.after(vector.tensor_tensor(gate[:, q, :], gate[:, q, :], gate[:, 4 + q, :], ALU.add))
                    t = split_out(dyn(yh, jj * 2 + q), dyn(yl, jj * 2 + q), gate[:, q, :], t)
                    for n in (q, 2 + q, 4 + q):
                        gate_use[n].last = [t]
            all_done(tensor, vector, scalar, sync)
        residual(a["w_out"], l, lambda k: (yh[:, k, :], yl[:, k, :]), KT, 0, [(TC, TA, 0, 2, 0)])
        ys.close()
        mix.close()

        norm_scales(pcol[:, KT:2 * KT], 4, 3, 0)
        norm([(TC, TA, 0, 0)], hh, hl)
        with ExitStack() as s:
            uh = sb(s, "hidden_hi", [P, 8, T], F32R)
            ul = sb(s, "hidden_lo", [P, 8, T], F32R)
            sg = sb(s, "silu", [P, 2, T])
            sg_use = [Buffer(scalar), Buffer(scalar)]
            hid_use = Buffer(scalar)
            wf = a["w_ffn_in"]
            all_done(tensor, vector, scalar, sync)
            for t0, nt in ((0, 8), (8, 8), (16, 6)):
                b.wait(scalar, (pe, pe.count, pe.steps))
                b.wait(vector, (pe, pe.count, pe.steps))
                with b.loop(nt // 2, [*ALLBUF, *sg_use]) as i:
                    for q in range(2):
                        c0 = (i * 2 + (t0 + q)) * P
                        slot = weights(KT, 256, [(slice(0, KT), slice(0, P), P, rows_of(wf, l, 0, KT, c0, P)),
                                                 (slice(0, KT), slice(P, 2 * P), P, rows_of(wf, l, 0, KT, c0 + FFN, P))])
                        bg_, bu_ = 2 * q, 2 * q + 1
                        tg = transposed(slot, 0, h1, [(0, T)], [bg_])
                        tu = transposed(slot, P, h1, [(0, T)], [bu_])
                        b.wait(scalar, tg)
                        b.acquire(sg_use[q])
                        t = act.after(scalar.activation(sg[:, q, :], bank[bg_][:, :], ACT.Sigmoid))
                        b.wait(vector, t, tg)
                        t = dve.after(vector.tensor_tensor(sg[:, q, :], bank[bg_][:, :], sg[:, q, :], ALU.mult))
                        bank_use[bg_].last = [t]
                        b.wait(vector, t, tu)
                        t = dve.after(vector.tensor_tensor(sg[:, q, :], bank[bu_][:, :], sg[:, q, :], ALU.mult))
                        bank_use[bu_].last = [t]
                        t = split_out(dyn(uh, i * 2 + q), dyn(ul, i * 2 + q), sg[:, q, :], t)
                        sg_use[q].last = [t]
                residual(a["w_ffn_out"], l, lambda k: (uh[:, k, :], ul[:, k, :]), nt, t0 * P, [(TC, TA, 0, 5, 0)])
            all_done(tensor, vector, scalar, sync)

    def residual(w, l, h, kt, r0, segments):
        b.wait(tensor, (dve, dve.count, dve.steps), (act, act.count, act.steps))
        n_seg = len(segments)
        with b.loop(2, ALLBUF) as i:
            for q in range(2):
                slot = matrix(w, l, i * 512 + q * 256, 256, kt=kt, r0=r0)
                for c in range(2):
                    tile = i * 4 + 2 * q + c
                    banks = [(2 * q + c) * n_seg + n for n in range(n_seg)]
                    t = transposed(slot, c * P, h, [(h0, h0 + x1 - x0) for x0, x1, _, _, h0 in segments], banks)
                    b.wait(vector, t)
                    for bk, (x0, x1, m, part, _) in zip(banks, segments):
                        xs = dynx(tile, x0, x1)
                        g = mod[:, bass.ds(part * 8 + tile, 1), m]
                        t = dve.after(vector.scalar_tensor_tensor(out=xs, in0=bank[bk][:, 0:x1 - x0], scalar=g, in1=xs,
                                                                  op0=ALU.mult, op1=ALU.add))
                        bank_use[bk].last = [t]

    def dynx(tile, x0, x1):
        return X[:, bass.ds(tile, 1), x0:x1].rearrange("p a n -> p (a n)")

    def scale_norm(g):
        with ExitStack() as s:
            tmp = {"rstd": sb(s, "rstd_f", [P, 512]), "sq": sb(s, "squares_f", [P, 2, 512])}
            gf = sb(s, "norm_g", [P, KT])
            all_done(sync, vector, scalar, tensor)
            t_g = load(gf[:], g)
            rstd = mean_square(s, TC, TA, tmp, [Buffer(scalar), Buffer(scalar)])
            b.wait(vector, t_g)
            for k in range(KT):
                dve.after(vector.scalar_tensor_tensor(out=X[:, k, TC:TA], in0=X[:, k, TC:TA], scalar=gf[:, k:k + 1],
                                                      in1=rstd, op0=ALU.mult, op1=ALU.mult))
            all_done(sync, vector, scalar, tensor)

    negsel = sb(first, "minus_row_select", [P, HC, P])
    t_ns = load(negsel[0:HC], a["negsel"])
    b.wait(tensor, t_ns)
    condition([a["c_cols"]])
    rope_tables()
    if n_first:
        with b.loop(n_first, ALLBUF) as l:
            first_layer(l)
    first.close()
    scale_norm(a["final1_cols"])

    second = ExitStack()
    gh = sb(second, "h2_hi", [P, KT, TA], F32R)
    gl = sb(second, "h2_lo", [P, KT, TA], F32R)
    cos2 = sb(second, "axial_cos", [P, T])
    sin2 = sb(second, "axial_sin", [P, T])
    perm2 = sb(second, "swap_halves", [P, P])
    edge = sb(second, "edge_factors", [P, 4, 16])
    pcol2 = sb(second, "layer_columns_2", [P, 2 * KT + 4 + 1])
    lamr = sb(second, "lambda_rows", [P, 4, HD])
    lams = sb(second, "lambda_columns", [P, 8])
    stat2 = sb(second, "softmax_stats_2", [P, 4, 8])

    def h2(k):
        return gh[:, k, :], gl[:, k, :]

    CTX, TOK = (0, TC), (TC, TA)

    def second_layer(L, last):
        lam0 = 0.8 - 0.6 * float(np.exp(-0.3 * L))
        all_done(sync, vector, scalar, tensor)
        t_c = load(pcol2[:], a["cols2"][L])
        t_l = load(lamr[:], a["lam"][L:L + 1].to_broadcast((P, 4, HD)))
        b.wait(vector, t_c, t_l)
        b.wait(scalar, t_c, t_l)
        ada(a["w_ada_2"], a["b_ada_2_cols"][L], L, 2)
        for n in range(2):
            t = dve.after(vector.tensor_tensor(lamr[:, 2 * n, :], lamr[:, 2 * n, :], lamr[:, 2 * n + 1, :], ALU.mult))
            b.wait(vector, t)
            t = dve.after(vector.tensor_reduce(lams[:, n:n + 1], lamr[:, 2 * n, :], AX.X, ALU.add))
        b.wait(scalar, t)
        t = act.after(scalar.activation(lams[:, 2:4], lams[:, 0:2], ACT.Exp))
        b.wait(vector, t)
        t = dve.after(vector.tensor_tensor(lams[:, 4:5], lams[:, 2:3], lams[:, 3:4], ALU.subtract))
        b.wait(vector, t)
        dve.after(vector.tensor_scalar(lams[:, 5:6], lams[:, 4:5], lam0, -1.0, ALU.add, ALU.mult))
        dve.after(vector.tensor_scalar(lams[:, 6:7], pcol2[:, 2 * KT + 4:2 * KT + 5], 1.0 - lam0, None, ALU.mult))
        for m in range(2):
            norm_scales(pcol2[:, 0:KT], 1, 0, m)
        norm([(0, TC, 0, 1), (TC, TA, TC, 0)], gh, gl)

        att = ExitStack()
        q_t = sb(att, "q2", [P, NH2, TA])
        k_t = sb(att, "k2", [P, NH2, TA])
        v_n = sb(att, "v2", [P, TA // P, NH2 * P])
        u_t = sb(att, "pool_in", [P, NH2, UPAD])
        prob = sb(att, "maps", [P, 2, 2 * TA])
        probt = sb(att, "map_t", [P, 2, TA])
        tmp = prob[:, 0, 0:T]
        tmp_use = Buffer(vector)
        w = a["w_in_2"]
        all_done(vector, scalar, tensor)
        t_z = dve.after(vector.memset(u_t[:], 0.0))
        b.wait(scalar, t_z)
        segs = [TOK] if last else [CTX, TOK]
        for part, dst in ((0, u_t), (1, q_t), (2, k_t)):
            chunks = [CTX, TOK] if part == 2 else segs
            for half in range(2):
                slot = matrix(w, L, 512 * part + 256 * half, 256)
                for c in range(2):
                    n = 2 * half + c
                    banks = [2 * (n % 2) + i for i in range(len(chunks))]
                    t = transposed(slot, c * P, h2, chunks, banks)
                    b.wait(scalar, t)
                    for bk, (c0, c1) in zip(banks, chunks):
                        if part == 0:
                            o = PAD if c0 == 0 else 3 * PAD
                            t = act.after(scalar.copy(dst[:, n, o + c0:o + c1], bank[bk][:, 0:c1 - c0]))
                        else:
                            t = act.after(scalar.activation(dst[:, n, c0:c1], bank[bk][:, 0:c1 - c0], ACT.Copy,
                                                            scale=HD ** -0.5 if part == 1 else 1.0))
                        bank_use[bk].last = [t]
                    if part:
                        b.wait(vector, t)
                        rope(t, dst[:, n, TC:TA], cos2[:], sin2[:], tmp, tmp_use, 4 + n % 2, perm2[:])
        for half in range(2):
            slot = matrix(w, L, 1536 + 256 * half, 256)
            for n in range(TA // P):
                t = natural(slot, 0, 256, h2, n * P, n % 4)
                b.wait(scalar, t)
                t = act.after(scalar.copy(v_n[:, n, 256 * half:256 * half + 256], bank[n % 4][:, 0:256]))
                bank_use[n % 4].last = [t]
        all_done(vector, scalar, tensor, sync)

        with ExitStack() as s:
            wp = sb(s, "w_pool", [P, 4, P])
            s_a, s_b = prob[:, 0, 0:UPAD], prob[:, 1, 0:UPAD]
            t_w = load(wp[:], a["w_pool_2"][L].rearrange("g c d -> c g d"))
            b.wait(tensor, t_w)
            for g, win in enumerate(WINDOWS):
                u = u_t[:, g, :]
                src, dst, other, lo, hi_ = u, s_a, s_b, 1, UPAD
                t = dve.after(vector.tensor_tensor(s_a[:, 1:UPAD], u[:, 0:UPAD - 1], u[:, 1:UPAD], ALU.add))
                cur, nxt = s_a, s_b
                step, lo, hi_ = 1, 1, UPAD
                while 2 * step < win:
                    b.wait(vector, t)
                    lo, hi_ = lo + step, hi_ - step
                    t = dve.after(vector.tensor_tensor(nxt[:, lo:hi_], cur[:, lo - step:hi_ - step],
                                                       cur[:, lo + step:hi_ + step], ALU.add))
                    cur, nxt = nxt, cur
                    step *= 2
                b.wait(vector, t)
                for c0, c1 in segs:
                    o = PAD if c0 == 0 else 3 * PAD
                    x0, x1 = o + c0, o + c1
                    dve.after(vector.tensor_tensor(cur[:, x0:x0 + 8], cur[:, x0:x0 + 8], edge[:, g, 0:8], ALU.mult))
                    t = dve.after(vector.tensor_tensor(cur[:, x1 - 8:x1], cur[:, x1 - 8:x1], edge[:, g, 8:16], ALU.mult))
                    b.wait(vector, t)
                    t = dve.after(vector.scalar_tensor_tensor(out=cur[:, x0:x1], in0=cur[:, x0:x1], scalar=1.0 / win,
                                                              in1=u[:, x0:x1], op0=ALU.mult, op1=ALU.subtract))
                    b.wait(tensor, t)
                    bk = 4 + (c0 > 0)
                    b.acquire(bank_use[bk])
                    t = pe.after(tensor.matmul(bank[bk][:, 0:c1 - c0], wp[:, g, :], cur[:, x0:x1], start=True, stop=True))
                    b.wait(scalar, t)
                    b.wait(vector, t)
                    y = probt[:, c0 > 0, 0:c1 - c0]
                    b.wait(scalar, (dve, dve.count, dve.steps))
                    t = act.after(scalar.activation(y, bank[bk][:, 0:c1 - c0], ACT.Copy,
                                                    scale=pcol2[:, 2 * KT + g:2 * KT + g + 1]))
                    bank_use[bk].last = [t]
                    split_out(gh[:, g, c0:c1], gl[:, g, c0:c1], y, t)
            all_done(vector, scalar, tensor, sync)

        head = sb(att, "head_out", [P, 2, T])
        prob_use = [Buffer(scalar), Buffer(scalar)]
        probt_use = [Buffer(scalar), Buffer(scalar)]
        pair_use = [Buffer(tensor), Buffer(tensor)]
        units = []
        for n in range(NH2):
            if not last:
                units += [(n, t, TC, 0) for t in range(2)]
            units += [(n, t, TA, 1) for t in range(2, TA // P)]
        st = {}

        def scores(u):
            n, t, nk, _ = units[u]
            q = u % 2
            o = q * 3 * 512
            b.acquire(pair_use[q])
            if nk > 512:
                cuts = [(0, 512, nk), (0, 0, 512), (1, 256, nk), (1, 0, 256)]
            else:
                cuts = [(0, 0, nk), (1, 0, nk)]
            for m, c0, c1 in cuts:
                if (m, c0, nk) == (1, 0, TA):
                    b.wait(tensor, shared)
                at = o + m * max(nk, 512) + c0
                ins = tensor.matmul(psum[:, at:at + c1 - c0], q_t[HD * m:HD * m + HD, n, t * P:t * P + P],
                                    k_t[HD * m:HD * m + HD, n, c0:c1], start=True, stop=True)
                if (m, c0) == (0, 512):
                    shared = pe.after(ins)
            st["s", u] = pe.after(ins)

        def soften(u):
            n, t, nk, _ = units[u]
            q = u % 2
            o = q * 3 * 512
            nm, rs = stat2[:, u % 4, 0:2], stat2[:, u % 4, 2:4]
            b.wait(vector, st["s", u])
            tk = dve.after(vector.tensor_reduce(nm, psum[:, o:o + 2 * max(nk, 512)].rearrange("p (m k) -> p m k", m=2)[:, :, 0:nk],
                                                AX.X, ALU.max, negate=True))
            b.wait(scalar, tk)
            b.acquire(prob_use[q])
            for m in range(2):
                tk = act.after(scalar.activation(prob[:, q, m * nk:m * nk + nk], psum[:, o + m * max(nk, 512):o + m * max(nk, 512) + nk],
                                                 ACT.Exp, bias=nm[:, m:m + 1], accum_out=rs[:, m:m + 1]))
            pair_use[q].last = [tk]
            st["e", u] = tk

        def combine(u):
            n, t, nk, _ = units[u]
            q = u % 2
            rs, rr = stat2[:, u % 4, 2:4], stat2[:, u % 4, 4:6]
            e0, e1 = prob[:, q, 0:nk], prob[:, q, nk:2 * nk]
            b.wait(vector, st["e", u])
            tk = dve.after(vector.reciprocal(rr, rs))
            b.wait(vector, tk)
            tk = dve.after(vector.tensor_scalar(e1, e1, rr[:, 1:2], lams[:, 5:6], ALU.mult, ALU.mult))
            b.wait(vector, tk)
            tk = dve.after(vector.scalar_tensor_tensor(out=e0, in0=e0, scalar=rr[:, 0:1], in1=e1,
                                                       op0=ALU.mult, op1=ALU.add))
            b.wait(tensor, tk)
            for j0 in range(0, nk // P, 4):
                j1 = min(j0 + 4, nk // P)
                b.acquire(bank_use[6])
                for j in range(j0, j1):
                    ins = tensor.transpose(bank[6][:, (j - j0) * P:(j - j0) * P + P], prob[:, q, j * P:j * P + P], ident)
                tk = pe.after(ins)
                b.wait(scalar, tk)
                if j0 == 0:
                    b.acquire(probt_use[q])
                tc_ = act.after(scalar.copy(probt[:, q, j0 * P:j1 * P], bank[6][:, 0:(j1 - j0) * P]))
                bank_use[6].last = [tc_]
            prob_use[q].last = [tk]
            st["t", u] = tc_

        def values(u):
            n, t, nk, is_tok = units[u]
            q = u % 2
            o = (t - 2) * P if is_tok else t * P
            b.wait(tensor, st["t", u])
            if o == 0:
                b.acquire(bank_use[7])
            for j in range(nk // P):
                ins = tensor.matmul(bank[7][:, o:o + P], v_n[:, j, n * P:n * P + P], probt[:, q, j * P:j * P + P],
                                    start=j == 0, stop=j == nk // P - 1)
            tk = pe.after(ins)
            probt_use[q].last = [tk]
            if t == TA // P - 1 or (not is_tok and t == 1):
                w_ = T if is_tok else TC
                c0 = TC if is_tok else 0
                ho, sq = head[:, 0, 0:w_], head[:, 1, 0:w_]
                b.wait(scalar, tk, (dve, dve.count, dve.steps))
                t_o = act.after(scalar.copy(ho, bank[7][:, 0:w_]))
                b.wait(scalar, t_o)
                t_q = act.after(scalar.activation(sq, ho, ACT.Square))
                b.wait(tensor, t_q)
                tk = pe.after(tensor.matmul(bank[7][:, 0:w_], meanm, sq, start=True, stop=True))
                b.wait(scalar, tk)
                tk = act.after(scalar.activation(sq, bank[7][:, 0:w_], ACT.Sqrt, bias=eps[:, 0:1], scale=float(D // P)))
                bank_use[7].last = [tk]
                b.wait(vector, tk)
                tk = dve.after(vector.reciprocal(sq, sq))
                b.wait(vector, tk)
                tk = dve.after(vector.scalar_tensor_tensor(out=ho, in0=ho, scalar=lams[:, 6:7], in1=sq,
                                                           op0=ALU.mult, op1=ALU.mult))
                split_out(gh[:, 4 + n, c0:c0 + w_], gl[:, 4 + n, c0:c0 + w_], ho, tk)

        for u in range(len(units) + 2):
            if u < len(units):
                scores(u)
                soften(u)
            if 1 <= u <= len(units):
                combine(u - 1)
            if u >= 2:
                values(u - 2)
        all_done(vector, scalar, tensor, sync)
        att.close()
        out_segs = [(TC, TA, 0, 2, TC)] if last else [(0, TC, 1, 2, 0), (TC, TA, 0, 2, TC)]
        residual(a["w_out_2"], L, h2, KT, 0, out_segs)

        for m in range(2):
            norm_scales(pcol2[:, KT:2 * KT], 4, 3, m)
        norm([(TC, TA, TC, 0)] if last else [(0, TC, 0, 1), (TC, TA, TC, 0)], gh, gl)
        with ExitStack() as s:
            uh = sb(s, "hidden2_hi", [P, 8, TA], F32R)
            ul = sb(s, "hidden2_lo", [P, 8, TA], F32R)
            sq = sb(s, "relu_squared", [P, 2, T])
            sq_use = [Buffer(scalar), Buffer(scalar)]
            hid_use = Buffer(scalar)
            all_done(vector, scalar, tensor, sync)
            with b.loop(DFF // D, [*ALLBUF, *sq_use, hid_use]) as chunk:
                b.acquire(hid_use)
                with b.loop(2, [*ALLBUF, *sq_use]) as i:
                    for q in range(2):
                        slot = matrix(a["w_mlp1_2"], L, chunk * D + i * 512 + q * 256, 256)
                        for c in range(2):
                            banks = [(2 * q + c) * len(segs) + n for n in range(len(segs))]
                            t = transposed(slot, c * P, h2, segs, banks)
                            for bk, (c0, c1) in zip(banks, segs):
                                sb_ = bk % 2
                                y = sq[:, sb_, 0:c1 - c0]
                                b.wait(scalar, t)
                                b.acquire(sq_use[sb_])
                                tk = act.after(scalar.activation(y, bank[bk][:, 0:c1 - c0], ACT.Relu))
                                bank_use[bk].last = [tk]
                                b.wait(vector, tk)
                                tk = dve.after(vector.tensor_tensor(y, y, y, ALU.mult))
                                dst = i * 4 + (2 * q + c)
                                tk = split_out(uh[:, bass.ds(dst, 1), c0:c1].rearrange("p a n -> p (a n)"),
                                               ul[:, bass.ds(dst, 1), c0:c1].rearrange("p a n -> p (a n)"), y, tk)
                                sq_use[sb_].last = [tk]
                out_segs = [(x0, x1, m, 5, h0) for x0, x1, m, _, h0 in out_segs]
                residual(a["w_mlp2_2"], L, lambda k: (uh[:, k, :], ul[:, k, :]), KT, chunk * D, out_segs)
                hid_use.last = [(pe, pe.count, pe.steps)]
            all_done(vector, scalar, tensor, sync)

    load_t = [load(cos2[:], a["cos2"]), load(sin2[:], a["sin2"]), load(perm2[:], a["perm2"]), load(edge[:], a["edge"])]
    b.wait(vector, *load_t)
    b.wait(tensor, *load_t)
    condition([a["c2_cols"], a["cctx_cols"]])
    for L in range(n_second):
        second_layer(L, L == DEPTH - 1)
    second.close()

    scale_norm(a["g_final_cols"])
    out = a["out"].rearrange("(k p) t -> k p t", p=P)
    stores = b.counter("stores", step=16)
    all_done(sync)
    for k in range(KT):
        t_out = stores.after(sync.dma_start(out[k], X[:, k, TC:TA]))
    b.wait(sync, t_out)
    return b


def columns(v):
    v = np.asarray(v)
    v = v.reshape(v.shape[:-1] + (v.shape[-1] // P, P))
    return np.ascontiguousarray(np.swapaxes(v, -1, -2))


def swap_matrix(half, span):
    m = np.zeros((P, P), np.float32)
    for r in range(P):
        d = r % HD
        if d < span:
            m[r, r + half if d % (2 * half) < half else r - half] = 1.0
    return m


def constants():
    ident = np.eye(P, dtype=np.float32)
    swap = swap_matrix(8, 16)
    dup = np.zeros((P, P), np.float32)
    dup[np.arange(P) % HD, np.arange(P)] = 1.0
    sel = np.zeros((P, P), np.float32)
    for g in range(4):
        sel[32 * g, 0] = sel[32 * g + 1, 1] = 1.0
    consts = np.stack([ident, swap, np.full((P, P), 1.0 / D, np.float32), dup, dup @ swap, sel], 1)
    d = np.arange(P) % HD
    inv = np.where(d < 16, 500000.0 ** (-(d % 8) / 8.0), 0.0)
    sign = np.where(d < 8, -1.0, np.where(d < 16, 1.0, 0.0))
    negsel = np.zeros((HC, HC, P), np.float32)
    for h in range(HC):
        negsel[h, h] = -1.0
    causal = np.where(np.arange(P)[None, :] <= np.arange(P)[:, None], 0.0, NEG)
    t = np.arange(T)
    j = np.arange(HD // 4)
    freq = 10000.0 ** (-j / (HD // 4.0))
    angle = np.concatenate([(t // 64)[:, None] * freq, (t % 64)[:, None] * freq], -1).T
    angle = angle[np.arange(P) % (HD // 2)]
    half = np.where(np.arange(P) % HD < HD // 2, -1.0, 1.0)[:, None]
    edge = np.ones((P, 4, 16), np.float32)
    for g, w in enumerate(WINDOWS):
        for e in range(8):
            edge[:, g, e] = w / min(w, e + w // 2)
            edge[:, g, 8 + e] = w / min(w, (8 - e) + w // 2)
    second = {"cos2": np.cos(angle).astype(np.float32), "sin2": (np.sin(angle) * half).astype(np.float32),
              "perm2": swap_matrix(HD // 2, HD), "edge": edge}
    return {**second, "consts": np.ascontiguousarray(consts), "rope_cols": np.stack([inv, sign], 1).astype(np.float32),
            "negsel": negsel, "causal": causal.astype(np.float32)}


def lay_out(i):
    i = {k: np.asarray(v) for k, v in i.items()}
    b_in = i["b_in"]
    tiles = np.stack([b_in[:, o:o + P] for o in TILES], -1)
    gates = columns(b_in[:, OG:])
    rel = i["rel_bias"]
    rel = np.concatenate([rel, np.repeat(rel[:, :, -1:], REL_ROW - rel.shape[2], 2)], 2)
    a = {
        "x_t": np.ascontiguousarray(i["x"][0].T), "ctx_t": np.ascontiguousarray(i["ctx_2"][0].T),
        "positions": i["positions"], "c_cols": columns(i["c"][0]),
        "ada_w": i["ada_w"], "ada_b_cols": columns(i["ada_b"]),
        "cols1": np.concatenate([columns(i["norm1_g"]), columns(i["norm2_g"]), tiles, gates], -1),
        "w_in": i["w_in"], "b_in": b_in, "rel": rel, "w_branch": i["w_branch"], "w_out": i["w_out"],
        "final1_cols": columns(i["final_g"]), "w_ffn_in": i["w_ffn_in"], "w_ffn_out": i["w_ffn_out"], "g_final_cols": columns(i["g_final_2"]),
    }
    a.update({
        "c2_cols": columns(i["c_2"][0]), "cctx_cols": columns(i["c_ctx_2"]),
        "w_ada_2": i["w_ada_2"], "b_ada_2_cols": columns(i["b_ada_2"]),
        "cols2": np.concatenate([columns(i["g_mix_2"]), columns(i["g_mlp_2"]), columns(i["s_pool_2"]),
                                 columns(i["g_subln_2"])], -1),
        "lam": np.stack([i["lam_q1_2"], i["lam_k1_2"], i["lam_q2_2"], i["lam_k2_2"]], 1),
        "w_in_2": i["w_in_2"], "w_pool_2": i["w_pool_2"], "w_out_2": i["w_out_2"],
        "w_mlp1_2": i["w_mlp1_2"], "w_mlp2_2": i["w_mlp2_2"],
    })
    a.update(constants())
    return {k: np.ascontiguousarray(v) for k, v in a.items()}


def kernel(**inputs):
    import concourse.bacc as bacc
    from concourse.bass_utils import run_bass_kernel_spmd

    arrays = lay_out(inputs)

    def build(plan):
        nc = bacc.Bacc("TRN2", target_bir_lowering=False, num_devices=1)
        a = {n: nc.dram_tensor(f"in_{n}", v.shape, mybir.dt.from_np(v.dtype), kind="ExternalInput").ap()
             for n, v in arrays.items()}
        a["out"] = nc.dram_tensor("out_t", (D, T), F32, kind="ExternalOutput").ap()
        with program(nc, plan, a).ctx:
            pass
        return nc

    plan = {}
    build(plan)
    nc = build(plan)
    r = run_bass_kernel_spmd(nc, [{f"in_{n}": v for n, v in arrays.items()}], core_ids=[0])
    return np.ascontiguousarray(r.results[0]["out_t"].T)[None]
```

```python
from contextlib import ExitStack, contextmanager

import numpy as np

import concourse.bass as bass
from concourse import mybir
from concourse.alu_op_type import AluOpType as ALU

F32 = mybir.dt.float32
F32R = mybir.dt.float32r
BF16 = mybir.dt.bfloat16
I32 = mybir.dt.int32
ACT = mybir.ActivationFunctionType
AX = mybir.AxisListType

P = 128
D = 1024
KT = D // P
T = 512
TT = T // P
TC = 256
TA = TC + T
HD = 64
CHUNK = 64
EPS = 1e-6
NEG = -1.0e30
TAKEN = -3.0e38
TOPK = min(256, T // 4)

HA, HB, HC, HI = 6, 5, 5, 8
WA, WB, WC = HA * HD, HB * HD, HC * HD
OQA, OKA, OVA = 0, WA, 2 * WA
OQI = 3 * WA
OKI = OQI + HI * HD
OWI = OKI + HD
OB = OWI + HI
OC = OB + 3 * WB
OF = OC + 3 * WC
OG = OF + HC
INW = OG + 3 * D
FFN = -(-8 * D // 768) * 256
TILES = ([OQA + P * i for i in range(6)] + [OQI + P * i for i in range(4)] + [OKI]
         + [o + P * i for o in (OB, OB + WB, OC, OC + WC) for i in range(3)] + [OF]
         + [o + P * i for o in (OVA, OB + 2 * WB, OC + 2 * WC) for i in range(3)])
TA0, TQI, TKI, TB0, TC0, TF, TV0 = 0, 6, 10, 11, 17, 23, 24
REL = 128

NH2 = 4
POOLW = 512
WINDOWS = (2, 4, 8, 16)
INW2 = 2048
DFF = 4 * D

DEPTH = 2
PAD = 8
UPAD = TA + 4 * PAD
REL_ROW = 512

SLOT = 9 * 2 * P
CREDIT = 4096


class Progress:

    def __init__(self, nc, sem, engine=None, step=1):
        self.sem, self.step, self.steps = sem, step, 0
        self.count = CREDIT
        (engine or nc.sync).sem_inc(sem, self.count)

    def after(self, instruction):
        instruction.then_inc(self.sem, self.step)
        self.builder.waiting.pop(id(self.engine), None)
        self.count = self.count + self.step
        self.steps += self.step
        return (self, self.count, self.steps)


class Buffer:

    def __init__(self, writer):
        self.writer, self.last = writer, []


class Builder:

    def __init__(self, nc, plan):
        self.nc, self.plan, self.n_loops = nc, plan, 0
        self.ctx = ExitStack()
        self.counters, self.seen, self.waiting = [], {}, {}
        self.pe = self.counter("pe_done", nc.tensor)
        self.act = self.counter("act_done", nc.scalar)
        self.dve = self.counter("dve_done", nc.vector)
        self.pool = self.counter("pool_done", nc.gpsimd)
        self.held = self.ctx.enter_context(nc.semaphore("held"))

    def counter(self, name, engine=None, step=1):
        c = Progress(self.nc, self.ctx.enter_context(self.nc.semaphore(name)), engine, step)
        c.engine, c.builder = engine, self
        self.counters.append(c)
        return c

    def wait(self, engine, *tokens):
        for token in tokens:
            if token is None:
                continue
            if isinstance(token, list):
                self.wait(engine, *token)
                continue
            counter, count, steps = token
            key = (id(engine), id(counter))
            if steps is not None and key in self.seen and self.seen[key] >= steps:
                continue
            waiting = self.waiting.setdefault(id(engine), set())
            if not isinstance(count, int) and id(counter) in waiting:
                self.hold(engine)
                waiting.clear()
            engine.wait_ge(counter.sem, count)
            waiting.add(id(counter))
            if not isinstance(count, int) and engine not in (self.nc.tensor, self.nc.scalar):
                self.hold(engine)
                waiting.clear()
            if steps is not None:
                self.seen[key] = steps

    def hold(self, engine):
        engine.sem_inc(self.held, 1)

    def acquire(self, buffer):
        self.wait(buffer.writer, *buffer.last)

    @contextmanager
    def loop(self, trips, buffers, engines=None):
        key = self.n_loops
        self.n_loops += 1
        plan = self.plan.get(key, {})
        start = [(c, c.count, c.steps) for c in self.counters]
        at = {id(c): n for n, (c, _, _) in enumerate(start)}
        delta = plan.get("delta", [0] * len(start))
        ends = plan.get("ends", [None] * len(buffers))
        for b, end in zip(buffers, ends):
            met = {at_end: c.steps + off - delta[at_end] for at_end, off in end or [] for c in [self.counters[at_end]]}
            if not plan or not all(at[id(c)] in met and steps <= met[at[id(c)]] for c, _, steps in b.last):
                self.acquire(b)
        if engines is None:
            self.hold(self.nc.tensor)
        before = [b.last for b in buffers]
        seen = dict(self.seen)
        kw = {} if engines is None else {"engines": engines}
        with self.nc.Fori(0, trips, **kw) as i:
            self.seen = {}
            for (c, count, _), d in zip(start, delta):
                if d:
                    c.count = count + i * d
            carried = []
            for b, end in zip(buffers, ends):
                if end is not None:
                    b.last = [(start[n][0], start[n][1] + i * delta[n] + (off - delta[n]), start[n][2] + off - delta[n])
                              for n, off in end]
                else:
                    b.last = list(b.last)
                carried.append(b.last)
            yield i
            found = [c.steps - s for c, _, s in start]
            now = []
            for b, was in zip(buffers, carried):
                now.append(None if b.last is was else
                           [(at[id(c)], steps - start[at[id(c)]][2]) for c, _, steps in b.last])
            self.plan[key] = {"delta": found, "ends": now}
        for (c, count, steps), d in zip(start, found):
            c.count = count + trips * d
            c.steps = steps + trips * d
        for b, end, was in zip(buffers, now, before):
            b.last = was if end is None else [
                (start[n][0], start[n][1] + (trips - 1) * found[n] + off,
                 start[n][2] + (trips - 1) * found[n] + off) for n, off in end]
        self.seen = seen


def dyn(ap, index):
    if isinstance(index, int):
        return ap[:, index]
    got = ap[:, bass.ds(index, 1)]
    if len(got.shape) == 3:
        return got.rearrange("p a n -> p (a n)")
    return got


def program(nc, plan, a, n_first=2, n_second=2):
    b = Builder(nc, plan)
    tensor, vector, scalar, gpsimd, sync = nc.tensor, nc.vector, nc.scalar, nc.gpsimd, nc.sync
    pe, act, dve, pool = b.pe, b.act, b.dve, b.pool

    names = {}

    def sb(scope, name, shape, dt=F32):
        names[name] = names.get(name, 0) + 1
        if names[name] > 1:
            name = f"{name}_{names[name]}"
        return scope.enter_context(nc.sbuf_tensor(name, shape, dt))

    top = b.ctx
    X = sb(top, "x", [P, KT, TA])
    raw = sb(top, "raw_weights", [P, 2, SLOT])
    whi = sb(top, "weights_hi", [P, 2, SLOT], F32R)
    wlo = sb(top, "weights_lo", [P, 2, SLOT], F32R)
    cst = sb(top, "constants", [P, 6, P])
    ident, perm, meanm, dup, dupperm, sel = (cst[:, n, :] for n in range(6))
    identb = sb(top, "identity_bf16", [P, P], BF16)
    causal = sb(top, "causal_bf16", [P, P], BF16)
    eps = sb(top, "eps", [P, 1])
    cond = sb(top, "cond", [P, KT, 32])
    mod = sb(top, "mod", [P, 48, 2])
    mod_next = sb(top, "mod_next", [P, 48, 3])
    bias_next = sb(top, "ada_bias", [P, 48])
    ada_rows = sb(top, "ada_rows", [P, 2, 256])
    col = sb(top, "norm_columns", [P, 2, KT, 2])
    small = sb(top, "small", [P, 16, 4])
    psum = top.enter_context(nc.psum_tensor("psum", [P, 8 * 512], F32))
    bank = [psum[:, 512 * n:512 * n + 512] for n in range(8)]
    bank_use = [Buffer(tensor) for _ in range(8)]

    arrived = [b.counter(f"weights_arrived{r}", step=16) for r in range(2)]
    loaded = [b.counter(f"small_load{n}", step=16) for n in range(8)]
    loads = [0]
    raw_use = [Buffer(sync), Buffer(sync)]
    split_use = [Buffer(gpsimd), Buffer(gpsimd)]
    ring, split_ring = [0], [0]

    def load(dst, src):
        loads[0] += 1
        return loaded[loads[0] % 8].after(scalar.dma_start(dst, src))

    def fetch(kt, cols, pieces):
        r = ring[0] % 2
        ring[0] += 1
        view = raw[:, r, 0:kt * cols].rearrange("p (k n) -> p k n", k=kt)
        b.acquire(raw_use[r])
        for ks, cs, rows, src in pieces:
            token = arrived[r].after(sync.dma_start(view[0:rows, ks, cs], src))
        return r, view, token

    def weights(kt, cols, pieces):
        from_, _, token = fetch(kt, cols, pieces)
        n = kt * cols
        r = split_ring[0] % 2
        split_ring[0] += 1
        b.acquire(split_use[r])
        b.wait(gpsimd, token)
        hi_done = pool.after(gpsimd.tensor_scalar(whi[:, r, 0:n], raw[:, from_, 0:n], 1.0, 1.0, ALU.mult, ALU.mult))
        b.wait(gpsimd, hi_done)
        done = pool.after(gpsimd.tensor_tensor(wlo[:, r, 0:n], raw[:, from_, 0:n], whi[:, r, 0:n].bitcast(F32),
                                               ALU.subtract))
        raw_use[from_].last = [done]
        hi = whi[:, r, 0:n].rearrange("p (k n) -> p k n", k=kt)
        lo = wlo[:, r, 0:n].rearrange("p (k n) -> p k n", k=kt)
        return r, hi, lo, done

    def rows_of(w, l, r0, kt, c0, cols):
        if l is None:
            v = w[r0:r0 + kt * P] if isinstance(r0, int) else w[bass.ds(r0, kt * P)]
        else:
            v = w[bass.ds(l, 1)].rearrange("l r c -> (l r) c") if not isinstance(l, int) else w[l]
            v = v[r0:r0 + kt * P] if isinstance(r0, int) else v[bass.ds(r0, kt * P)]
        v = v.rearrange("(k p) c -> p k c", p=P)
        return v[:, :, c0:c0 + cols] if isinstance(c0, int) else v[:, :, bass.ds(c0, cols)]

    def matrix(w, l, c0, cols, kt=KT, r0=0):
        return weights(kt, cols, [(slice(0, kt), slice(0, cols), P, rows_of(w, l, r0, kt, c0, cols))])

    def product(out, stationary, moving, first, last):
        (sh, sl), (mh, ml) = stationary, moving
        tensor.matmul(out, sh, mh, start=first, stop=False)
        tensor.matmul(out, sh, ml, start=False, stop=False)
        return tensor.matmul(out, sl, mh, start=False, stop=last)

    for r in range(2):
        raw_use[r].last = [dve.after(vector.memset(raw[:, r, :], 0.0))]
    t_const = load(cst[:], a["consts"])
    t_x = load(X[:, :, TC:TA], a["x_t"].rearrange("(k p) t -> p k t", p=P))
    t_ctx = load(X[:, :, 0:TC], a["ctx_t"].rearrange("(k p) t -> p k t", p=P))
    with ExitStack() as s:
        cm = sb(s, "causal_f32", [P, P])
        t_cm = load(cm[:], a["causal"])
        b.wait(vector, t_cm, t_const)
        dve.after(vector.tensor_copy(identb[:], ident))
        dve.after(vector.tensor_copy(causal[:], cm[:]))
        dve.after(vector.memset(eps[:], EPS))
        t_init = dve.after(vector.memset(small[:], 0.0))
        for e in (tensor, scalar):
            b.wait(e, t_init, t_const)

    def all_done(*engines):
        for e in engines:
            for c in (pe, act, dve):
                if c.steps:
                    b.wait(e, (c, c.count, c.steps))

    def condition(sources):
        with ExitStack() as s:
            cin = sb(s, "cond_in", [P, 3, KT])
            sg = sb(s, "cond_sigmoid", [P, 3, KT])
            all_done(scalar, vector)
            t = [load(cin[:, m, :], src) for m, src in enumerate(sources)]
            z = dve.after(vector.memset(cond[:], 0.0))
            m = len(sources)
            b.wait(scalar, t)
            t = act.after(scalar.activation(sg[:, 0:m, :], cin[:, 0:m, :], ACT.Sigmoid))
            b.wait(vector, t, z)
            for n in range(m):
                dve.after(vector.tensor_tensor(cond[:, :, n], cin[:, n, :], sg[:, n, :], ALU.mult))
            all_done(scalar, tensor)

    def ada_first():
        with ExitStack() as s:
            rows = sb(s, "ada_rows", [P, 2, 512])
            m = 3
            row_use = Buffer(scalar)
            row_use.last = [(dve, dve.count, dve.steps)]
            t_b = load(bias_next[:], a["ada_b_cols"][0])
            b.wait(vector, t_b)
            with b.loop(6, [*raw_use, *bank_use[0:4], row_use]) as i:
                for half in range(2):
                    b.acquire(bank_use[half])
                    for q in range(2):
                        c0 = i * 1024 + (half * 2 + q) * 256
                        r, view, t = fetch(KT, 256, [(slice(0, KT), slice(0, 256), P,
                                                      rows_of(a["ada_w"], 0, 0, KT, c0, 256))])
                        b.wait(tensor, t)
                        for kk in range(2):
                            for g in range(4):
                                ins = tensor.matmul(bank[half][32 * g:32 * g + 32, 256 * q:256 * q + 256],
                                                    cond[:, 4 * kk + g, :], view[:, 4 * kk + g, :],
                                                    start=kk == 0, stop=kk == 1, tile_position=(0, 32 * g))
                        t_rows = pe.after(ins)
                        raw_use[r].last = [t_rows]
                    b.wait(scalar, t_rows)
                    if half == 0:
                        b.acquire(row_use)
                    t_copy = act.after(scalar.copy(rows[:, half, :], bank[half][:, :]))
                    bank_use[half].last = [t_copy]
                    b.acquire(bank_use[2 + half])
                    b.wait(tensor, t_copy)
                    for n in range(4):
                        ins = tensor.matmul(bank[2 + half][:, n * m:n * m + m], rows[:, half, n * P:n * P + P],
                                            sel[:, 0:m], start=n == 0, stop=n == 3, skip_group_check=True)
                    t_cols = pe.after(ins)
                    b.wait(vector, t_cols)
                    bc = bias_next[:, bass.ds(i * 8 + half * 4, 4)]
                    for mm in range(m):
                        t_mod = dve.after(vector.tensor_tensor(
                            mod_next[:, bass.ds(i * 8 + half * 4, 4), mm],
                            bank[2 + half][:, 0:4 * m].rearrange("p (n m) -> p n m", m=m)[:, :, mm], bc, ALU.add))
                    bank_use[2 + half].last = [t_mod]
                    if half == 1:
                        row_use.last = [t_cols]
            all_done(vector, scalar, tensor)

    def ada_steps(layer, j0, n, row_banks, col_bank):
        calls = iter(range(n + 2))
        row_use = [Buffer(scalar), Buffer(scalar)]
        t_rows, t_copy = {}, {}

        def step():
            c = next(calls, None)
            if c is None:
                return
            if 1 <= c <= n:
                q = (c - 1) % 2
                bk = row_banks[(c - 1) % len(row_banks)]
                b.wait(scalar, t_rows[c - 1])
                b.acquire(row_use[q])
                t_copy[c - 1] = act.after(scalar.copy(ada_rows[:, q, :], bank[bk][:, 0:256]))
                bank_use[bk].last = [t_copy[c - 1]]
            if c < n:
                bk = row_banks[c % len(row_banks)]
                r, view, t = fetch(KT, 256, [(slice(0, KT), slice(0, 256), P,
                                              rows_of(a["ada_w"], layer, 0, KT, (j0 + c) * 256, 256))])
                b.wait(tensor, t)
                b.acquire(bank_use[bk])
                for kk in range(2):
                    for g in range(4):
                        ins = tensor.matmul(bank[bk][32 * g:32 * g + 32, 0:256], cond[:, 4 * kk + g, :],
                                            view[:, 4 * kk + g, :], start=kk == 0, stop=kk == 1,
                                            tile_position=(0, 32 * g))
                t_rows[c] = pe.after(ins)
                raw_use[r].last = [t_rows[c]]
            if c >= 2:
                q = (c - 2) % 2
                b.wait(tensor, t_copy[c - 2])
                if c == 2:
                    b.acquire(bank_use[col_bank])
                for h in range(2):
                    at = (2 * (c - 2) + h) * 3
                    ins = tensor.matmul(bank[col_bank][:, at:at + 3], ada_rows[:, q, h * P:h * P + P], sel[:, 0:3],
                                        start=c == 2 and h == 0, stop=c == n + 1 and h == 1, skip_group_check=True)
                t = pe.after(ins)
                row_use[q].last = [t]
                step.last = t

        def finish():
            for _ in range(n + 2):
                step()
            b.wait(vector, step.last)
            for m in range(3):
                t = dve.after(vector.tensor_tensor(
                    mod_next[:, 2 * j0:2 * (j0 + n), m],
                    bank[col_bank][:, 0:6 * n].rearrange("p (n m) -> p n m", m=3)[:, :, m],
                    bias_next[:, 2 * j0:2 * (j0 + n)], ALU.add))
            bank_use[col_bank].last = [t]
        step.finish = finish
        return step

    def next_mod(m0, m, layer):
        all_done(vector, scalar)
        t = dve.after(vector.tensor_copy(mod[:, :, 0:m], mod_next[:, :, m0:m0 + m]))
        b.wait(vector, t)
        if layer is not None:
            bias = a["ada_b_cols"][layer] if isinstance(layer, int) else \
                a["ada_b_cols"][bass.ds(layer, 1)].rearrange("l p n -> (l p) n")
            b.wait(scalar, t)
            b.wait(vector, load(bias_next[:], bias))

    def norm_scales(g, sc, sh, m):
        b.wait(vector, (dve, dve.count, dve.steps))
        t = dve.after(vector.scalar_tensor_tensor(out=col[:, 0, :, m], in0=mod[:, sc * 8:sc * 8 + 8, m], scalar=1.0,
                                                  in1=g, op0=ALU.add, op1=ALU.mult))
        t = dve.after(vector.tensor_copy(col[:, 1, :, m], mod[:, sh * 8:sh * 8 + 8, m]))
        return t

    def mean_square(s, x0, x1, tmp, sq_use, src=None):
        n = x1 - x0
        rstd = tmp["rstd"][:, 0:n]
        b.acquire(bank_use[7])
        for k in range(KT):
            q = k % 2
            b.acquire(sq_use[q])
            t = act.after(scalar.activation(tmp["sq"][:, q, 0:n], X[:, k, x0:x1], ACT.Square))
            b.wait(tensor, t)
            t = pe.after(tensor.matmul(bank[7][:, 0:n], meanm, tmp["sq"][:, q, 0:n], start=k == 0, stop=k == KT - 1))
            sq_use[q].last = [t]
        b.wait(scalar, t)
        t = act.after(scalar.activation(rstd, bank[7][:, 0:n], ACT.Sqrt, bias=eps[:, 0:1]))
        bank_use[7].last = [t]
        b.wait(vector, t)
        t = dve.after(vector.reciprocal(rstd, rstd))
        b.wait(vector, t)
        return rstd

    def norm(segments, hh, hl, ada_part=None):
        with ExitStack() as s:
            tmp = {"rstd": sb(s, "rstd", [P, 512]), "sq": sb(s, "squares", [P, 2, 512]), "u": sb(s, "scaled", [P, 4, 512])}
            sq_use = [Buffer(scalar), Buffer(scalar)]
            all_done(scalar, vector, tensor)
            for seg, (x0, x1, h0, m) in enumerate(segments):
                n = x1 - x0
                step = ada_steps(ada_part[0], ada_part[1] + ada_part[2] * seg, ada_part[2], (0, 1), 2) if ada_part else None
                if step:
                    step()
                rstd = mean_square(s, x0, x1, tmp, sq_use)
                all_done(vector)
                use = [Buffer(vector) for _ in range(4)]
                th = {}
                for k in range(KT + 1):
                    if k < KT:
                        u = tmp["u"][:, k % 4, 0:n]
                        b.acquire(use[k % 4])
                        t = dve.after(vector.scalar_tensor_tensor(out=u, in0=X[:, k, x0:x1], scalar=col[:, 0, k, m:m + 1],
                                                                  in1=rstd, op0=ALU.mult, op1=ALU.mult))
                        b.wait(scalar, t)
                        th[k] = act.after(scalar.activation(hh[:, k, h0:h0 + n], u, ACT.Identity, bias=col[:, 1, k, m:m + 1]))
                    if step and (k % 2 == 1 or ada_part[2] > 4):
                        step()
                    if k:
                        k -= 1
                        b.wait(vector, th[k])
                        use[k % 4].last = [dve.after(vector.scalar_tensor_tensor(
                            out=hl[:, k, h0:h0 + n], in0=tmp["u"][:, k % 4, 0:n], scalar=col[:, 1, k, m:m + 1],
                            in1=hh[:, k, h0:h0 + n].bitcast(F32), op0=ALU.add, op1=ALU.subtract))]
                if step:
                    step.finish()
                all_done(scalar, vector, tensor)

    def split_out(hi, lo, value, token):
        b.wait(scalar, token)
        t = act.after(scalar.copy(hi, value))
        b.wait(vector, t, token)
        return dve.after(vector.tensor_tensor(lo, value, hi.bitcast(F32), ALU.subtract))

    def transposed(slot, c, h, chunks, banks, k_rows=None):
        r, hi, lo, ready = slot
        b.wait(tensor, ready)
        for (c0, c1), bk in zip(chunks, banks):
            b.acquire(bank_use[bk])
            kt = hi.shape[1]
            for k in range(kt):
                n = P if k_rows is None else k_rows[k]
                xh, xl = h(k)
                ins = product(bank[bk][:, 0:c1 - c0], (hi[0:n, k, c:c + P], lo[0:n, k, c:c + P]),
                              (xh[0:n, c0:c1], xl[0:n, c0:c1]), k == 0, k == kt - 1)
        t = pe.after(ins)
        split_use[r].last = [t]
        return t

    def natural(slot, c, n, h, tok0, bk):
        r, hi, lo, ready = slot
        b.wait(tensor, ready)
        b.acquire(bank_use[bk])
        for k in range(KT):
            xh, xl = h(k)
            ins = product(bank[bk][:, 0:n], (xh[:, tok0:tok0 + P], xl[:, tok0:tok0 + P]),
                          (hi[:, k, c:c + n], lo[:, k, c:c + n]), k == 0, k == KT - 1)
        t = pe.after(ins)
        split_use[r].last = [t]
        return t

    ALLBUF = [*raw_use, *split_use, *bank_use]

    first = ExitStack()
    hh = sb(first, "h_hi", [P, KT, T], F32R)
    hl = sb(first, "h_lo", [P, KT, T], F32R)
    ropec = sb(first, "rope_cos", [P, T])
    ropes = sb(first, "rope_sin", [P, T])
    pcol = sb(first, "layer_columns", [P, 2 * KT + len(TILES) + 3 * KT])
    wicol = sb(first, "index_weights", [P, TT, HI])
    stat = sb(first, "softmax_stats", [P, 4, 4])

    def h1(k):
        return hh[:, k, :], hl[:, k, :]

    def rope_tables():
        with ExitStack() as s:
            pi_ = sb(s, "pos_int", [P, T], I32)
            ang = sb(s, "angle", [P, T])
            turns = sb(s, "turns", [P, T])
            ti = load(pi_[:], a["positions"].to_broadcast((P, T)))
            tc = load(small[:, 0, 0:2], a["rope_cols"])
            b.wait(vector, tc, ti)

            def step(ins):
                t = dve.after(ins)
                b.wait(vector, t)
                return t
            step(vector.tensor_copy(ang[:], pi_[:]))
            step(vector.tensor_scalar(ang[:], ang[:], small[:, 0, 0:1], None, ALU.mult))
            magic = 1.5 * 2.0 ** 23
            tau = 2.0 * np.pi
            parts = [6.28125]
            parts.append(float(np.float32(np.round((tau - parts[0]) * 2 ** 21) / 2 ** 21)))
            parts.append(float(tau - parts[0] - parts[1]))
            for quarter, red in ((0.25, ropec), (0.0, ropes)):
                step(vector.tensor_scalar(turns[:], ang[:], float(1.0 / tau), quarter, ALU.mult, ALU.add))
                step(vector.tensor_scalar(turns[:], turns[:], magic, None, ALU.add))
                step(vector.tensor_scalar(turns[:], turns[:], magic, None, ALU.subtract))
                src = ang
                for part in parts:
                    step(vector.scalar_tensor_tensor(out=red[:], in0=turns[:], scalar=-part, in1=src[:],
                                                     op0=ALU.mult, op1=ALU.add))
                    src = red
                if quarter:
                    step(vector.tensor_scalar(red[:], red[:], float(np.pi / 2), None, ALU.add))
                t = step(vector.tensor_scalar(red[:], red[:], 3.14159, -3.14159, ALU.min, ALU.max))
        return t

    def rope_sines(t):
        b.wait(scalar, t)
        for x in (ropec, ropes):
            t = act.after(scalar.activation(x[:], x[:], ACT.Sin))
        b.wait(vector, t)
        dve.after(vector.tensor_scalar(ropes[:], ropes[:], small[:, 0, 1:2], None, ALU.mult))

    def rope(t_in, x, cos, sin, tmp, tmp_use, bk, perm=perm):
        b.wait(tensor, t_in)
        b.acquire(bank_use[bk])
        t = pe.after(tensor.matmul(bank[bk][:, 0:x.shape[1]], perm, x, start=True, stop=True))
        b.wait(vector, t)
        b.acquire(tmp_use)
        t1 = dve.after(vector.tensor_tensor(tmp, bank[bk][:, 0:x.shape[1]], sin, ALU.mult))
        bank_use[bk].last = [t1]
        t2 = dve.after(vector.tensor_tensor(x, x, cos, ALU.mult))
        b.wait(vector, t1, t2)
        t3 = dve.after(vector.tensor_tensor(x, x, tmp, ALU.add))
        tmp_use.last = [t3]
        return t3

    def first_layer(l):
        b.wait(scalar, t_x, t_ctx)
        b.wait(vector, t_x, t_ctx)
        wi = a["w_in"]
        all_done(scalar)
        t_cols = load(pcol[:], a["cols1"][bass.ds(l, 1)].rearrange("l p n -> (l p) n"))
        next_mod(0, 1, l + 1)
        bt = pcol[:, 2 * KT:2 * KT + len(TILES)]
        bg = pcol[:, 2 * KT + len(TILES):]
        b.wait(vector, t_cols)
        b.wait(scalar, t_cols)
        norm_scales(pcol[:, 0:KT], 1, 0, 0)
        norm([(TC, TA, 0, 0)], hh, hl, (l + 1, 0, 4))

        mix = ExitStack()
        oh = sb(mix, "o_hi", [P, 9, T], F32R)
        ol = sb(mix, "o_lo", [P, 9, T], F32R)
        att = ExitStack()
        maska = sb(att, "select_mask", [P, TT, T], BF16)
        qk = sb(att, "qk", [P, 6, T])
        val = sb(att, "values", [P, TT, WA])
        soft = sb(att, "softmax_buffers", [P, 8, T])
        logit, prob, probt, biast = (soft[:, n:n + 2, :] for n in (0, 2, 4, 6))
        relt = sb(att, "bias_diagonals", [P, 384])
        frow = sb(att, "forget", [P, 2, T])
        fcol = sb(att, "forget_columns", [P, TT, HC])
        bq = sb(att, "scaled_query_bias", [P, 3, 3])
        logit_use = [Buffer(vector), Buffer(vector)]
        prob_use = [Buffer(scalar), Buffer(scalar)]
        probt_use = [Buffer(scalar), Buffer(scalar)]
        bias_use = [Buffer(vector), Buffer(vector)]
        relt_use = Buffer(scalar)

        for n, tile0 in enumerate((TA0, TB0, TC0)):
            t_bq = dve.after(vector.tensor_scalar(bq[:, n, :], bt[:, tile0:tile0 + 3], HD ** -0.5, None, ALU.mult))
        with ExitStack() as s:
            work, relu, tmp, ki = soft[:, 0:3, :], soft[:, 3:5, :], soft[:, 5, :], soft[:, 7, :]
            qi = [val[:].rearrange("p n c -> p (n c)")[:, T * n:T * n + T] for n in range(3)] + [frow[:, 0, :]]
            tmp_use = Buffer(vector)
            all_done(tensor, vector, scalar)
            t_q = []
            for half in range(2):
                slot = matrix(wi, l, OQI + 256 * half, 256)
                for q in range(2):
                    n = 2 * half + q
                    t = transposed(slot, q * P, h1, [(0, T)], [n])
                    b.wait(scalar, t)
                    t = act.after(scalar.activation(qi[n], bank[n][:, :], ACT.Identity, bias=bt[:, TQI + n:TQI + n + 1]))
                    bank_use[n].last = [t]
                    t_q.append(t)
            slot = matrix(wi, l, OKI, P)
            t = transposed(slot, 0, h1, [(0, T)], [4])
            b.wait(scalar, t)
            t_k = act.after(scalar.activation(ki, bank[4][:, :], ACT.Identity, bias=bt[:, TKI:TKI + 1]))
            bank_use[4].last = [t_k]
            for n in range(4):
                t_q[n] = rope(t_q[n], qi[n], ropec[:], ropes[:], tmp, tmp_use, 5 + n % 2)
            b.wait(tensor, t_k)
            b.acquire(bank_use[7])
            for n in range(TT):
                ins = tensor.transpose(bank[7][:, n * P:n * P + P], ki[:, n * P:n * P + P], ident)
            t = pe.after(ins)
            b.wait(vector, t)
            t_w = dve.after(vector.tensor_scalar(
                wicol[:], bank[7][:, :].rearrange("p (n c) -> p n c", n=TT)[:, :, HD:HD + HI],
                float(HI ** -0.5 * HD ** -0.5), None, ALU.mult))
            bank_use[7].last = [t_w]
            b.acquire(bank_use[5])
            b.acquire(bank_use[6])
            tensor.matmul(bank[5][:, :], dup, ki, start=True, stop=True)
            t = pe.after(tensor.matmul(bank[6][:, :], dupperm, ki, start=True, stop=True))
            b.wait(vector, t)
            b.acquire(tmp_use)
            t1 = dve.after(vector.tensor_tensor(ki, bank[5][:, :], ropec[:], ALU.mult))
            t2 = dve.after(vector.tensor_tensor(tmp, bank[6][:, :], ropes[:], ALU.mult))
            bank_use[5].last = [t1]
            bank_use[6].last = [t2]
            b.wait(vector, t1, t2)
            t_k = dve.after(vector.tensor_tensor(ki, ki, tmp, ALU.add))
            b.wait(tensor, t_k)
            b.wait(scalar, t_k)
            relu_use = [Buffer(scalar), Buffer(scalar)]
            n = 0
            done = [None] * 3
            for h in range(HI):
                for i in range(1, TT):
                    w = (i + 1) * P
                    bk, q = n % 4, n % 2
                    n += 1
                    p0 = HD * (h % 2)
                    b.acquire(bank_use[bk])
                    t = pe.after(tensor.matmul(bank[bk][:, 0:w], qi[h // 2][p0:p0 + HD, i * P:i * P + P],
                                               ki[p0:p0 + HD, 0:w], start=True, stop=True))
                    b.wait(scalar, t)
                    b.acquire(relu_use[q])
                    t = act.after(scalar.activation(relu[:, q, 0:w], bank[bk][:, 0:w], ACT.Relu))
                    bank_use[bk].last = [t]
                    b.wait(vector, t, t_w, done[i - 1])
                    wc = wicol[:, i, h:h + 1]
                    if h == 0:
                        t = dve.after(vector.tensor_scalar(work[:, i - 1, 0:w], relu[:, q, 0:w], wc, None, ALU.mult))
                    else:
                        t = dve.after(vector.scalar_tensor_tensor(out=work[:, i - 1, 0:w], in0=relu[:, q, 0:w], scalar=wc,
                                                                  in1=work[:, i - 1, 0:w], op0=ALU.mult, op1=ALU.add))
                    done[i - 1] = t
                    relu_use[q].last = [t]
            for i in range(1, TT):
                b.wait(vector, done[i - 1])
                done[i - 1] = dve.after(vector.memset(work[0:CHUNK, i - 1, (i + 1) * P - CHUNK:(i + 1) * P], NEG))
            top8 = small[:, 1:7, :].rearrange("p a c -> p (a c)")
            b.wait(vector, *done)
            scored = list(done)
            chain = [Buffer(vector) for _ in range(3)]
            for i in range(3):
                chain[i].last = [done[i]]
            with b.loop(TOPK // 8, chain, engines=[mybir.EngineType.DVE]) as _:
                tops = []
                for i in range(3):
                    b.acquire(chain[i])
                    tops.append(dve.after(vector.max(top8[:, 8 * i:8 * i + 8], work[:, i, 0:(i + 2) * P])))
                for i in range(3):
                    w = work[:, i, 0:(i + 2) * P]
                    b.wait(vector, tops[i])
                    chain[i].last = [dve.after(vector.match_replace(
                        out=w, in_to_replace=top8[:, 8 * i:8 * i + 8], in_values=w, imm_value=TAKEN))]

        def select():
            for i in range(3):
                b.acquire(chain[i])
                dve.after(vector.tensor_scalar(maska[:, i + 1, 0:(i + 2) * P], work[:, i, 0:(i + 2) * P],
                                               -2.9e38, NEG, ALU.is_gt, ALU.mult))
            t = dve.after(vector.memset(maska[:, 0, 0:P], 0.0))
            b.wait(vector, t)
            t = dve.after(vector.memset(maska[0:CHUNK, 0, CHUNK:P], NEG))
            b.wait(vector, t)

        def project(kind, o_q, o_k, o_v, n_heads, tile0, with_rope, extra=0):
            n = 0
            ts, t_v = [], []
            for which, o in ((0, o_q), (1, o_k)):
                for c0, cols in ((0, 256), (256, 128)):
                    slot = matrix(wi, l, o + c0, cols)
                    for q in range(cols // P):
                        tile = which * 3 + (c0 // P) + q
                        bk = n % 4
                        n += 1
                        t = transposed(slot, q * P, h1, [(0, T)], [bk])
                        b.wait(scalar, t)
                        if which == 0:
                            t = act.after(scalar.activation(qk[:, tile, :], bank[bk][:, :], ACT.Identity,
                                                            bias=bq[:, kind, tile:tile + 1], scale=HD ** -0.5))
                        else:
                            t = act.after(scalar.activation(qk[:, tile, :], bank[bk][:, :], ACT.Identity,
                                                            bias=bt[:, tile0 + tile:tile0 + tile + 1]))
                        bank_use[bk].last = [t]
                        ts.append((t, tile))
            vt_use = [prob_use[1], probt_use[0]]
            for c0, cols in ((0, 256), (256, P)):
                slot = matrix(wi, l, o_v + c0, cols + (extra if c0 else 0))
                for q in range(cols // P):
                    tile = c0 // P + q
                    bk, vt = n % 4, soft[:, 3 + tile % 2, :]
                    n += 1
                    t = transposed(slot, q * P, h1, [(0, T)], [bk])
                    b.wait(scalar, t)
                    b.acquire(vt_use[tile % 2])
                    at = TV0 + 3 * kind + tile
                    t = act.after(scalar.activation(vt, bank[bk][:, :], ACT.Identity, bias=bt[:, at:at + 1]))
                    bank_use[bk].last = [t]
                    b.wait(tensor, t)
                    bk = 5 + tile % 2
                    b.acquire(bank_use[bk])
                    for j in range(TT):
                        ins = tensor.transpose(bank[bk][:, j * P:j * P + P], vt[:, j * P:j * P + P], ident)
                    t = pe.after(ins)
                    vt_use[tile % 2].last = [t]
                    b.wait(scalar, t)
                    t = act.after(scalar.copy(val[:, :, tile * P:tile * P + P],
                                              bank[bk][:, :].rearrange("p (n c) -> p n c", n=TT)))
                    bank_use[bk].last = [t]
                    t_v.append(t)
            if kind == 0:
                ada_a()
                select()
            if with_rope:
                for n, (t, tile) in enumerate(ts):
                    b.wait(vector, t)
                    ts[n] = (rope(t, qk[:, tile, :], ropec[:], ropes[:], biast[:, tile % 2, :], bias_use[tile % 2],
                                  5 + tile % 2), tile)
                    ada_a()
                ada_a.finish()
            return slot, [t for t, _ in ts], t_v

        def attend(n_heads, tile0, kind, t_qk, t_v):
            units = [(h, i) for h in range(n_heads) for i in range(TT)]
            st = {}

            def load_diagonals(h):
                b.acquire(relt_use)
                src = a["rel"]
                st["d", h] = load(relt[:], bass.AP(src.tensor, l * (HB * REL_ROW) + h * REL_ROW, [[1, P], [1, 384]]))

            def prepare(h):
                if kind == "B":
                    b.wait(vector, st["d", h])
                    b.acquire(bias_use[h % 2])
                    bt_ = biast[:, h % 2, :]
                    t1 = dve.after(vector.tensor_copy(bt_[:, 256:512], relt[:, 256:0:-1]))
                    t2 = dve.after(vector.tensor_copy(bt_[:, 0:256], relt[:, 383:384].to_broadcast((P, 256))))
                    b.wait(vector, t1, t2)
                    t = dve.after(vector.memset(bt_[0:CHUNK, 448:512], NEG))
                    b.wait(vector, t)
                    relt_use.last = [t]
                if kind == "C":
                    b.acquire(bank_use[6 + h % 2])
                    st["nf", h] = pe.after(tensor.matmul(bank[6 + h % 2][:, :], negsel[0:HC, h, :], frow[0:HC, 1, :],
                                                         start=True, stop=True))

            def scores(u):
                h, i = units[u]
                if i == 0:
                    prepare(h)
                if kind == "B" and i == 1 and h + 1 < n_heads:
                    load_diagonals(h + 1)
                w = (i + 1) * P
                p0 = HD * (h % 2)
                bk = u % 2
                if kind == "C":
                    q = u % 2
                    b.wait(scalar, st["nf", h])
                    b.wait(scalar, *bias_use[q].last)
                    t = act.after(scalar.activation(biast[:, q, 0:w], bank[6 + h % 2][:, 0:w], ACT.Identity,
                                                    bias=fcol[:, i, h:h + 1]))
                    if i == TT - 1:
                        bank_use[6 + h % 2].last = [t]
                    st["b", u] = t
                b.acquire(bank_use[bk])
                if kind == "A":
                    tensor.matmul(bank[bk][:, 0:w], identb[:], maska[:, i, 0:w], start=True, stop=False)
                if kind == "C":
                    tensor.matmul(bank[bk][:, w - P:w], identb[:], causal[:], start=True, stop=False)
                q_ = qk[p0:p0 + HD, h // 2, i * P:i * P + P]
                k_ = qk[p0:p0 + HD, 3 + h // 2, 0:w]
                if kind == "C":
                    ins = tensor.matmul(bank[bk][:, w - P:w], q_, k_[:, w - P:w], start=False, stop=True)
                    if i:
                        ins = tensor.matmul(bank[bk][:, 0:w - P], q_, k_[:, 0:w - P], start=True, stop=True)
                else:
                    ins = tensor.matmul(bank[bk][:, 0:w], q_, k_, start=kind == "B", stop=True)
                st["s", u] = pe.after(ins)

            def maximum(u):
                h, i = units[u]
                w = (i + 1) * P
                bk, q = u % 2, u % 2
                nm, rs = stat[:, u % 4, 0:1], stat[:, u % 4, 1:2]
                if kind == "A":
                    b.wait(vector, st["s", u])
                    t = dve.after(vector.tensor_reduce(nm, bank[bk][:, 0:w], AX.X, ALU.max, negate=True))
                else:
                    if kind == "B":
                        extra_logit = biast[:, h % 2, T - w:T]
                    else:
                        extra_logit = biast[:, q, 0:w]
                        b.wait(vector, st["b", u])
                    b.wait(vector, st["s", u])
                    b.acquire(logit_use[q])
                    t = dve.after(vector.tensor_tensor_reduce(
                        out=logit[:, q, 0:w], in0=bank[bk][:, 0:w], in1=extra_logit, scale=-1.0, scalar=3e38,
                        op0=ALU.add, op1=ALU.min, accum_out=nm))
                    bank_use[bk].last = [t]
                    if kind == "C":
                        bias_use[q].last = [t]
                    elif i == TT - 1:
                        bias_use[h % 2].last = [t]
                st["m", u] = t

            def exponential(u):
                h, i = units[u]
                w = (i + 1) * P
                bk, q = u % 2, u % 2
                nm, rs = stat[:, u % 4, 0:1], stat[:, u % 4, 1:2]
                src, scale = (bank[bk][:, 0:w], 1.0) if kind == "A" else (logit[:, q, 0:w], -1.0)
                b.wait(scalar, st["m", u])
                b.acquire(prob_use[q])
                t = act.after(scalar.activation(prob[:, q, 0:w], src, ACT.Exp, bias=nm, scale=scale, accum_out=rs))
                if kind == "A":
                    bank_use[bk].last = [t]
                else:
                    logit_use[q].last = [t]
                st["e", u] = t

            def normalise(u):
                h, i = units[u]
                w = (i + 1) * P
                q = u % 2
                rs, rr = stat[:, u % 4, 1:2], stat[:, u % 4, 2:3]
                b.wait(vector, st["e", u])
                t = dve.after(vector.reciprocal(rr, rs))
                b.wait(vector, t)
                t = dve.after(vector.tensor_scalar(prob[:, q, 0:w], prob[:, q, 0:w], rr, None, ALU.mult))
                b.wait(tensor, t)
                bk = 2 + q
                b.acquire(bank_use[bk])
                for j in range(i + 1):
                    ins = tensor.transpose(bank[bk][:, j * P:j * P + P], prob[:, q, j * P:j * P + P], ident)
                t = pe.after(ins)
                prob_use[q].last = [t]
                st["p", u] = t

            def take_out(u):
                h, i = units[u]
                w = (i + 1) * P
                q = u % 2
                bk = 2 + q
                b.wait(scalar, st["p", u])
                b.acquire(probt_use[q])
                t = act.after(scalar.copy(probt[:, q, 0:w], bank[bk][:, 0:w]))
                bank_use[bk].last = [t]
                st["t", u] = t

            def values(u):
                h, i = units[u]
                q = u % 2
                p0 = HD * (h % 2)
                ob = 4 + (h // 2) % 2
                b.wait(tensor, st["t", u])
                if h % 2 == 0 and i == 0:
                    b.acquire(bank_use[ob])
                for j in range(i + 1):
                    ins = tensor.matmul(bank[ob][p0:p0 + HD, i * P:i * P + P], val[:, j, h * HD:h * HD + HD],
                                        probt[:, q, j * P:j * P + P], start=j == 0, stop=j == i)
                t = pe.after(ins)
                probt_use[q].last = [t]
                if i == TT - 1 and (h % 2 == 1 or h == n_heads - 1):
                    n = p0 + HD
                    tile = tile0 + h // 2
                    t = split_out(oh[0:n, tile, :], ol[0:n, tile, :], bank[ob][0:n, :], t)
                    bank_use[ob].last = [t]

            if kind == "B":
                load_diagonals(0)
            step = ada_steps(l + 1, {"A": 8, "B": 14}[kind], 6, (6,), 7) if kind != "C" else None
            b.wait(tensor, *t_qk)
            scores(0)
            for u in range(len(units) + 2):
                if u == 2:
                    b.wait(tensor, *t_v)
                if u + 1 < len(units):
                    scores(u + 1)
                if u < len(units):
                    maximum(u)
                    exponential(u)
                if 1 <= u <= len(units):
                    normalise(u - 1)
                    take_out(u - 1)
                if u >= 2:
                    values(u - 2)
                if step and u % 5 in (1, 3):
                    step()
            if step:
                step.finish()

        ada_a = ada_steps(l + 1, 4, 4, (4,), 7)
        b.wait(scalar, *scored)
        _, *tokens = project(0, OQA, OKA, OVA, HA, TA0, True)
        attend(HA, 0, "A", *tokens)
        _, *tokens = project(1, OB, OB + WB, OB + 2 * WB, HB, TB0, False)
        attend(HB, 3, "B", *tokens)
        slot, *tokens = project(2, OC, OC + WC, OC + 2 * WC, HC, TC0, False, extra=P)
        t = transposed(slot, HD, h1, [(0, T)], [4])
        z, m = (frow[0:HC, n, :] for n in range(2))
        F = m
        b.wait(scalar, t)
        t = act.after(scalar.activation(z, bank[4][0:HC, :], ACT.Identity, bias=bt[0:HC, TF:TF + 1]))
        bank_use[4].last = [t]
        b.wait(vector, t)
        t = dve.after(vector.scalar_tensor_tensor(out=m, in0=z, scalar=-1.0, in1=z, op0=ALU.mult, op1=ALU.max))
        b.wait(scalar, t)
        t = act.after(scalar.activation(m, m, ACT.Exp, scale=-1.0))
        b.wait(scalar, t)
        t = act.after(scalar.activation(m, m, ACT.Ln, bias=1.0))
        b.wait(vector, t)
        t = dve.after(vector.scalar_tensor_tensor(out=z, in0=z, scalar=0.0, in1=m, op0=ALU.min, op1=ALU.subtract))
        b.acquire(logit_use[0])
        t1 = dve.after(vector.memset(logit[0:HC, 0, :], 1.0))
        b.wait(vector, t, t1)
        t = dve.after(vector.tensor_tensor_scan(F, logit[0:HC, 0, :], z, 0.0, ALU.mult, ALU.add))
        b.wait(tensor, t)
        b.acquire(bank_use[7])
        for n in range(TT):
            ins = tensor.matmul(bank[7][:, n * HC:n * HC + HC], F[:, n * P:n * P + P], ident[0:HC, 0:HC],
                                start=n == 0, stop=n == TT - 1, skip_group_check=True)
        t = pe.after(ins)
        b.wait(vector, t)
        t = dve.after(vector.tensor_copy(fcol[:].rearrange("p n h -> p (n h)"), bank[7][:, 0:TT * HC]))
        bank_use[7].last = [t]
        b.wait(scalar, t)
        attend(HC, 6, "C", *tokens)
        all_done(tensor, vector, scalar)
        att.close()

        ys = ExitStack()
        yh = sb(ys, "y_hi", [P, KT, T], F32R)
        yl = sb(ys, "y_lo", [P, KT, T], F32R)
        all_done(tensor, vector, scalar)
        with ExitStack() as s:
            gate = sb(s, "gates", [P, 6, T])
            gate_use = [Buffer(scalar) for _ in range(6)]
            branch_rows = [P, P, P, P, P, HD, P, P, HD]
            branch_start = [0, P, 2 * P, WA, WA + P, WA + 2 * P, WA + WB, WA + WB + P, WA + WB + 2 * P]
            with b.loop(KT // 2, [*ALLBUF, *gate_use]) as jj:
                for br in range(3):
                    slot = matrix(wi, l, OG + br * D + jj * 256, 256)
                    for q in range(2):
                        bk = (2 * br + q) % 2
                        g = 2 * br + q
                        t = transposed(slot, q * P, h1, [(0, T)], [bk])
                        b.wait(scalar, t)
                        b.acquire(gate_use[g])
                        t = act.after(scalar.activation(gate[:, g, :], bank[bk][:, :], ACT.Sigmoid,
                                                        bias=bg[:, bass.ds(br * KT + jj * 2 + q, 1)]))
                        bank_use[bk].last = [t]
                wb = a["w_branch"][bass.ds(l, 1)].rearrange("l r c -> (l r) c")
                cs = bass.ds(jj * 256, 256)
                pieces = [(slice(n, n + 1), slice(0, 256), rows,
                           wb[r0:r0 + rows, cs].rearrange("(k p) c -> p k c", k=1))
                          for n, (r0, rows) in enumerate(zip(branch_start, branch_rows))]
                slot = weights(9, 256, pieces)
                r, hi, lo, ready = slot
                b.wait(tensor, ready)
                for q in range(2):
                    tb = []
                    for br in range(3):
                        bk = 2 + 3 * q + br
                        b.acquire(bank_use[bk])
                        for n in range(3):
                            k = 3 * br + n
                            rows = branch_rows[k]
                            ins = product(bank[bk][:, :], (hi[0:rows, k, q * P:q * P + P], lo[0:rows, k, q * P:q * P + P]),
                                          (oh[0:rows, k, :], ol[0:rows, k, :]), n == 0, n == 2)
                        tb.append(pe.after(ins))
                    split_use[r].last = [tb[-1]]
                    ts = []
                    for br in range(3):
                        b.wait(vector, tb[br], (act, act.count, act.steps))
                        g = gate[:, 2 * br + q, :]
                        t = dve.after(vector.tensor_tensor(g, bank[2 + 3 * q + br][:, :], g, ALU.mult))
                        bank_use[2 + 3 * q + br].last = [t]
                        ts.append(t)
                    b.wait(vector, *ts)
                    t = dve.after(vector.tensor_tensor(gate[:, q, :], gate[:, q, :], gate[:, 2 + q, :], ALU.add))
                    b.wait(vector, t)
                    t = dve.after(vector.tensor_tensor(gate[:, q, :], gate[:, q, :], gate[:, 4 + q, :], ALU.add))
                    t = split_out(dyn(yh, jj * 2 + q), dyn(yl, jj * 2 + q), gate[:, q, :], t)
                    for n in (q, 2 + q, 4 + q):
                        gate_use[n].last = [t]
            all_done(tensor, vector, scalar)
        residual(a["w_out"], l, lambda k: (yh[:, k, :], yl[:, k, :]), KT, 0, [(TC, TA, 0, 2, 0)])
        ys.close()
        mix.close()

        norm_scales(pcol[:, KT:2 * KT], 4, 3, 0)
        norm([(TC, TA, 0, 0)], hh, hl, (l + 1, 20, 4))
        with ExitStack() as s:
            uh = sb(s, "hidden_hi", [P, 8, T], F32R)
            ul = sb(s, "hidden_lo", [P, 8, T], F32R)
            sg = sb(s, "silu", [P, 2, T])
            sg_use = [Buffer(scalar), Buffer(scalar)]
            hid_use = Buffer(scalar)
            wf = a["w_ffn_in"]
            all_done(tensor, vector, scalar)
            for t0, nt in ((0, 8), (8, 8), (16, 6)):
                b.wait(scalar, (pe, pe.count, pe.steps))
                b.wait(vector, (pe, pe.count, pe.steps))
                with b.loop(nt // 2, [*ALLBUF, *sg_use]) as i:
                    for q in range(2):
                        c0 = (i * 2 + (t0 + q)) * P
                        slot = weights(KT, 256, [(slice(0, KT), slice(0, P), P, rows_of(wf, l, 0, KT, c0, P)),
                                                 (slice(0, KT), slice(P, 2 * P), P, rows_of(wf, l, 0, KT, c0 + FFN, P))])
                        bg_, bu_ = 2 * q, 2 * q + 1
                        tg = transposed(slot, 0, h1, [(0, T)], [bg_])
                        tu = transposed(slot, P, h1, [(0, T)], [bu_])
                        b.wait(scalar, tg)
                        b.acquire(sg_use[q])
                        t = act.after(scalar.activation(sg[:, q, :], bank[bg_][:, :], ACT.Sigmoid))
                        b.wait(vector, t, tg)
                        t = dve.after(vector.tensor_tensor(sg[:, q, :], bank[bg_][:, :], sg[:, q, :], ALU.mult))
                        bank_use[bg_].last = [t]
                        b.wait(vector, t, tu)
                        t = dve.after(vector.tensor_tensor(sg[:, q, :], bank[bu_][:, :], sg[:, q, :], ALU.mult))
                        bank_use[bu_].last = [t]
                        t = split_out(dyn(uh, i * 2 + q), dyn(ul, i * 2 + q), sg[:, q, :], t)
                        sg_use[q].last = [t]
                residual(a["w_ffn_out"], l, lambda k: (uh[:, k, :], ul[:, k, :]), nt, t0 * P, [(TC, TA, 0, 5, 0)])
            all_done(tensor, vector, scalar)

    def residual(w, l, h, kt, r0, segments):
        b.wait(tensor, (dve, dve.count, dve.steps), (act, act.count, act.steps))
        n_seg = len(segments)
        with b.loop(2, ALLBUF) as i:
            for q in range(2):
                slot = matrix(w, l, i * 512 + q * 256, 256, kt=kt, r0=r0)
                for c in range(2):
                    tile = i * 4 + 2 * q + c
                    banks = [(2 * q + c) * n_seg + n for n in range(n_seg)]
                    t = transposed(slot, c * P, h, [(h0, h0 + x1 - x0) for x0, x1, _, _, h0 in segments], banks)
                    b.wait(vector, t)
                    for bk, (x0, x1, m, part, _) in zip(banks, segments):
                        xs = dynx(tile, x0, x1)
                        g = mod[:, bass.ds(part * 8 + tile, 1), m]
                        t = dve.after(vector.scalar_tensor_tensor(out=xs, in0=bank[bk][:, 0:x1 - x0], scalar=g, in1=xs,
                                                                  op0=ALU.mult, op1=ALU.add))
                        bank_use[bk].last = [t]

    def dynx(tile, x0, x1):
        return X[:, bass.ds(tile, 1), x0:x1].rearrange("p a n -> p (a n)")

    def scale_norm(g):
        with ExitStack() as s:
            tmp = {"rstd": sb(s, "rstd_f", [P, 512]), "sq": sb(s, "squares_f", [P, 2, 512])}
            gf = sb(s, "norm_g", [P, KT])
            all_done(vector, scalar, tensor)
            t_g = load(gf[:], g)
            rstd = mean_square(s, TC, TA, tmp, [Buffer(scalar), Buffer(scalar)])
            b.wait(vector, t_g)
            for k in range(KT):
                dve.after(vector.scalar_tensor_tensor(out=X[:, k, TC:TA], in0=X[:, k, TC:TA], scalar=gf[:, k:k + 1],
                                                      in1=rstd, op0=ALU.mult, op1=ALU.mult))
            all_done(vector, scalar, tensor)

    negsel = sb(first, "minus_row_select", [P, HC, P])
    t_ns = load(negsel[0:HC], a["negsel"])
    b.wait(tensor, t_ns)
    condition([a["c_cols"], a["c2_cols"], a["cctx_cols"]])
    t_angles = rope_tables()
    ada_first()
    rope_sines(t_angles)
    if n_first:
        with b.loop(n_first, ALLBUF) as l:
            first_layer(l)
    first.close()
    scale_norm(a["final1_cols"])

    second = ExitStack()
    gh = sb(second, "h2_hi", [P, KT, TA], F32R)
    gl = sb(second, "h2_lo", [P, KT, TA], F32R)
    cos2 = sb(second, "axial_cos", [P, T])
    sin2 = sb(second, "axial_sin", [P, T])
    perm2 = sb(second, "swap_halves", [P, P])
    edge = sb(second, "edge_factors", [P, 4, 16])
    pcol2 = sb(second, "layer_columns_2", [P, 2 * KT + 4 + 1])
    lamr = sb(second, "lambda_rows", [P, 4, HD])
    lams = sb(second, "lambda_columns", [P, 8])
    stat2 = sb(second, "softmax_stats_2", [P, 4, 8])

    def h2(k):
        return gh[:, k, :], gl[:, k, :]

    CTX, TOK = (0, TC), (TC, TA)

    def second_layer(L, last):
        lam0 = 0.8 - 0.6 * float(np.exp(-0.3 * L))
        all_done(vector, scalar, tensor)
        t_c = load(pcol2[:], a["cols2"][L])
        t_l = load(lamr[:], a["lam"][L:L + 1].to_broadcast((P, 4, HD)))
        b.wait(vector, t_c, t_l)
        b.wait(scalar, t_c, t_l)
        next_mod(1, 2, None if last else DEPTH + L + 1)
        for n in range(2):
            t = dve.after(vector.tensor_tensor(lamr[:, 2 * n, :], lamr[:, 2 * n, :], lamr[:, 2 * n + 1, :], ALU.mult))
            b.wait(vector, t)
            t = dve.after(vector.tensor_reduce(lams[:, n:n + 1], lamr[:, 2 * n, :], AX.X, ALU.add))
        b.wait(scalar, t)
        t = act.after(scalar.activation(lams[:, 2:4], lams[:, 0:2], ACT.Exp))
        b.wait(vector, t)
        t = dve.after(vector.tensor_tensor(lams[:, 4:5], lams[:, 2:3], lams[:, 3:4], ALU.subtract))
        b.wait(vector, t)
        dve.after(vector.tensor_scalar(lams[:, 5:6], lams[:, 4:5], lam0, -1.0, ALU.add, ALU.mult))
        dve.after(vector.tensor_scalar(lams[:, 6:7], pcol2[:, 2 * KT + 4:2 * KT + 5], 1.0 - lam0, None, ALU.mult))
        for m in range(2):
            norm_scales(pcol2[:, 0:KT], 1, 0, m)
        norm([(0, TC, 0, 1), (TC, TA, TC, 0)], gh, gl, None if last else (DEPTH + L + 1, 0, 6))

        att = ExitStack()
        q_t = sb(att, "q2", [P, NH2, TA])
        k_t = sb(att, "k2", [P, NH2, TA])
        v_n = sb(att, "v2", [P, TA // P, NH2 * P])
        u_t = sb(att, "pool_in", [P, NH2, UPAD])
        prob = sb(att, "maps", [P, 2, 2 * TA])
        probt = sb(att, "map_t", [P, 2, TA])
        tmp = prob[:, 0, 0:T]
        tmp_use = Buffer(vector)
        w = a["w_in_2"]
        all_done(vector, scalar, tensor)
        t_z = dve.after(vector.memset(u_t[:], 0.0))
        b.wait(scalar, t_z)
        segs = [TOK] if last else [CTX, TOK]
        for part, dst in ((0, u_t), (1, q_t), (2, k_t)):
            chunks = [CTX, TOK] if part == 2 else segs
            for half in range(2):
                slot = matrix(w, L, 512 * part + 256 * half, 256)
                for c in range(2):
                    n = 2 * half + c
                    banks = [2 * (n % 2) + i for i in range(len(chunks))]
                    t = transposed(slot, c * P, h2, chunks, banks)
                    b.wait(scalar, t)
                    for bk, (c0, c1) in zip(banks, chunks):
                        if part == 0:
                            o = PAD if c0 == 0 else 3 * PAD
                            t = act.after(scalar.copy(dst[:, n, o + c0:o + c1], bank[bk][:, 0:c1 - c0]))
                        else:
                            t = act.after(scalar.activation(dst[:, n, c0:c1], bank[bk][:, 0:c1 - c0], ACT.Copy,
                                                            scale=HD ** -0.5 if part == 1 else 1.0))
                        bank_use[bk].last = [t]
                    if part:
                        b.wait(vector, t)
                        rope(t, dst[:, n, TC:TA], cos2[:], sin2[:], tmp, tmp_use, 4 + n % 2, perm2[:])
        s_a, s_b = prob[:, 0, 0:UPAD], prob[:, 1, 0:UPAD]
        wp = ada_rows[:].rearrange("p a n -> p (a n)").rearrange("p (g d) -> p g d", g=4)
        b.acquire(tmp_use)

        def centred_mean(g):
            win, u = WINDOWS[g], u_t[:, g, :]
            t = dve.after(vector.tensor_tensor(s_a[:, 1:UPAD], u[:, 0:UPAD - 1], u[:, 1:UPAD], ALU.add))
            cur, nxt = s_a, s_b
            step, lo, hi_ = 1, 1, UPAD
            while 2 * step < win:
                b.wait(vector, t)
                lo, hi_ = lo + step, hi_ - step
                t = dve.after(vector.tensor_tensor(nxt[:, lo:hi_], cur[:, lo - step:hi_ - step],
                                                   cur[:, lo + step:hi_ + step], ALU.add))
                cur, nxt = nxt, cur
                step *= 2
            b.wait(vector, t)
            for c0, c1 in segs:
                o = PAD if c0 == 0 else 3 * PAD
                x0, x1 = o + c0, o + c1
                dve.after(vector.tensor_tensor(cur[:, x0:x0 + 8], cur[:, x0:x0 + 8], edge[:, g, 0:8], ALU.mult))
                t = dve.after(vector.tensor_tensor(cur[:, x1 - 8:x1], cur[:, x1 - 8:x1], edge[:, g, 8:16], ALU.mult))
                b.wait(vector, t)
                t = dve.after(vector.scalar_tensor_tensor(out=u[:, x0:x1], in0=cur[:, x0:x1], scalar=1.0 / win,
                                                          in1=u[:, x0:x1], op0=ALU.mult, op1=ALU.subtract))
            b.wait(vector, t)

        def pool_out(g, c0, c1):
            o = PAD if c0 == 0 else 3 * PAD
            b.acquire(bank_use[6])
            y = bank[6][:, 0:c1 - c0]
            t = pe.after(tensor.matmul(y, wp[:, g, :], u_t[:, g, o + c0:o + c1], start=True, stop=True))
            b.wait(scalar, t)
            scale = pcol2[:, 2 * KT + g:2 * KT + g + 1]
            t = act.after(scalar.activation(gh[:, g, c0:c1], y, ACT.Copy, scale=scale))
            b.wait(vector, t)
            t = dve.after(vector.scalar_tensor_tensor(out=gl[:, g, c0:c1], in0=y, scalar=scale,
                                                      in1=gh[:, g, c0:c1].bitcast(F32), op0=ALU.mult, op1=ALU.subtract))
            bank_use[6].last = [t]

        for half in range(2):
            slot = matrix(w, L, 1536 + 256 * half, 256)
            for n in range(TA // P):
                t = natural(slot, 0, 256, h2, n * P, n % 4)
                b.wait(scalar, t)
                t = act.after(scalar.copy(v_n[:, n, 256 * half:256 * half + 256], bank[n % 4][:, 0:256]))
                bank_use[n % 4].last = [t]
            for g in (2 * half, 2 * half + 1):
                centred_mean(g)
        all_done(vector, scalar, tensor)
        t_w = load(wp, a["w_pool_2"][L].rearrange("g c d -> c g d"))

        head = u_t[:, 2:4, 0:T]
        prob_use = [Buffer(scalar), Buffer(scalar)]
        probt_use = [Buffer(scalar), Buffer(scalar)]
        pair_use = [Buffer(tensor), Buffer(tensor)]
        units = []
        for n in range(NH2):
            if not last:
                units += [(n, t, TC, 0) for t in range(2)]
            units += [(n, t, TA, 1) for t in range(2, TA // P)]
        st, ended, head_use = {}, [], Buffer(scalar)

        def scores(u):
            n, t, nk, _ = units[u]
            q = u % 2
            o = q * 3 * 512
            b.acquire(pair_use[q])
            if nk > 512:
                cuts = [(0, 512, nk), (0, 0, 512), (1, 256, nk), (1, 0, 256)]
            else:
                cuts = [(0, 0, nk), (1, 0, nk)]
            for m, c0, c1 in cuts:
                if (m, c0, nk) == (1, 0, TA):
                    b.wait(tensor, shared)
                at = o + m * max(nk, 512) + c0
                ins = tensor.matmul(psum[:, at:at + c1 - c0], q_t[HD * m:HD * m + HD, n, t * P:t * P + P],
                                    k_t[HD * m:HD * m + HD, n, c0:c1], start=True, stop=True)
                if (m, c0) == (0, 512):
                    shared = pe.after(ins)
            st["s", u] = pe.after(ins)

        def maximum(u):
            n, t, nk, _ = units[u]
            o = (u % 2) * 3 * 512
            b.wait(vector, st["s", u])
            st["m", u] = dve.after(vector.tensor_reduce(
                stat2[:, u % 4, 0:2], psum[:, o:o + 2 * max(nk, 512)].rearrange("p (m k) -> p m k", m=2)[:, :, 0:nk],
                AX.X, ALU.max, negate=True))

        def exponential(u):
            n, t, nk, _ = units[u]
            q = u % 2
            o = q * 3 * 512
            nm, rs = stat2[:, u % 4, 0:2], stat2[:, u % 4, 2:4]
            b.wait(scalar, st["m", u])
            b.acquire(prob_use[q])
            for m in range(2):
                tk = act.after(scalar.activation(prob[:, q, m * nk:m * nk + nk], psum[:, o + m * max(nk, 512):o + m * max(nk, 512) + nk],
                                                 ACT.Exp, bias=nm[:, m:m + 1], accum_out=rs[:, m:m + 1]))
            pair_use[q].last = [tk]
            st["e", u] = tk

        def combine(u):
            n, t, nk, _ = units[u]
            q = u % 2
            rs, rr = stat2[:, u % 4, 2:4], stat2[:, u % 4, 4:6]
            e0, e1 = prob[:, q, 0:nk], prob[:, q, nk:2 * nk]
            b.wait(vector, st["e", u])
            tk = dve.after(vector.reciprocal(rr, rs))
            b.wait(vector, tk)
            tk = dve.after(vector.tensor_scalar(e1, e1, rr[:, 1:2], lams[:, 5:6], ALU.mult, ALU.mult))
            b.wait(vector, tk)
            st["c", u] = dve.after(vector.scalar_tensor_tensor(out=e0, in0=e0, scalar=rr[:, 0:1], in1=e1,
                                                               op0=ALU.mult, op1=ALU.add))

        def turn(u, j0):
            n, t, nk, _ = units[u]
            q = u % 2
            j1 = min(j0 + 4, nk // P)
            if j0 >= j1:
                return
            b.wait(tensor, st["c", u])
            b.acquire(bank_use[6])
            for j in range(j0, j1):
                ins = tensor.transpose(bank[6][:, (j - j0) * P:(j - j0) * P + P], prob[:, q, j * P:j * P + P], ident)
            tk = pe.after(ins)
            prob_use[q].last = [tk]
            st["p", u] = tk

        def take_out(u, j0):
            n, t, nk, _ = units[u]
            q = u % 2
            j1 = min(j0 + 4, nk // P)
            if j0 >= j1:
                return
            b.wait(scalar, st["p", u])
            if j0 == 0:
                b.acquire(probt_use[q])
            tk = act.after(scalar.copy(probt[:, q, j0 * P:j1 * P], bank[6][:, 0:(j1 - j0) * P]))
            bank_use[6].last = [tk]
            st["t", u] = tk

        def values(u):
            n, t, nk, is_tok = units[u]
            q = u % 2
            o = (t - 2) * P if is_tok else t * P
            b.wait(tensor, st["t", u])
            if o == 0:
                b.acquire(bank_use[7])
            for j in range(nk // P):
                ins = tensor.matmul(bank[7][:, o:o + P], v_n[:, j, n * P:n * P + P], probt[:, q, j * P:j * P + P],
                                    start=j == 0, stop=j == nk // P - 1)
            tk = pe.after(ins)
            probt_use[q].last = [tk]
            if t == TA // P - 1 or (not is_tok and t == 1):
                w_ = T if is_tok else TC
                b.wait(scalar, tk)
                b.acquire(head_use)
                t_o = act.after(scalar.copy(head[:, 0, 0:w_], bank[7][:, 0:w_]))
                bank_use[7].last = [t_o]
                b.wait(scalar, t_o)
                t_q = act.after(scalar.activation(head[:, 1, 0:w_], head[:, 0, 0:w_], ACT.Square))
                ended.append((n, w_, TC if is_tok else 0, t_q))

        def head_norm():
            n, w_, c0, t_q = ended.pop(0)
            ho, sq = head[:, 0, 0:w_], head[:, 1, 0:w_]
            b.wait(tensor, t_q)
            b.acquire(bank_use[6])
            tk = pe.after(tensor.matmul(bank[6][:, 0:w_], meanm, sq, start=True, stop=True))
            b.wait(scalar, tk)
            tk = act.after(scalar.activation(sq, bank[6][:, 0:w_], ACT.Sqrt, bias=eps[:, 0:1], scale=float(D // P)))
            bank_use[6].last = [tk]
            b.wait(vector, tk)
            tk = dve.after(vector.reciprocal(sq, sq))
            b.wait(vector, tk)
            tk = dve.after(vector.scalar_tensor_tensor(out=ho, in0=ho, scalar=lams[:, 6:7], in1=sq,
                                                       op0=ALU.mult, op1=ALU.mult))
            head_use.last = [split_out(gh[:, 4 + n, c0:c0 + w_], gl[:, 4 + n, c0:c0 + w_], ho, tk)]

        scores(0)
        for u in range(len(units) + 3):
            if u + 1 < len(units):
                scores(u + 1)
            if u < len(units):
                maximum(u)
                exponential(u)
            if 1 <= u <= len(units):
                combine(u - 1)
                turn(u - 1, 0)
                take_out(u - 1, 0)
            ending = list(ended)
            if 2 <= u <= len(units) + 1:
                values(u - 2)
            if 1 <= u <= len(units):
                turn(u - 1, 4)
                take_out(u - 1, 4)
            if ending:
                head_norm()
            for g in {0: (2,), 1: (3,), 3: (0,), 5: (1,)}.get(u, ()):
                b.wait(tensor, t_w)
                for c0, c1 in segs:
                    pool_out(g, c0, c1)
        all_done(vector, scalar, tensor)
        att.close()
        out_segs = [(TC, TA, 0, 2, TC)] if last else [(0, TC, 1, 2, 0), (TC, TA, 0, 2, TC)]
        residual(a["w_out_2"], L, h2, KT, 0, out_segs)

        for m in range(2):
            norm_scales(pcol2[:, KT:2 * KT], 4, 3, m)
        norm([(TC, TA, TC, 0)] if last else [(0, TC, 0, 1), (TC, TA, TC, 0)], gh, gl,
             None if last else (DEPTH + L + 1, 12, 6))
        with ExitStack() as s:
            uh = sb(s, "hidden2_hi", [P, 8, TA], F32R)
            ul = sb(s, "hidden2_lo", [P, 8, TA], F32R)
            sq = sb(s, "relu_squared", [P, 2, T])
            sq_use = [Buffer(scalar), Buffer(scalar)]
            hid_use = Buffer(scalar)
            all_done(vector, scalar, tensor)
            with b.loop(DFF // D, [*ALLBUF, *sq_use, hid_use]) as chunk:
                b.acquire(hid_use)
                with b.loop(2, [*ALLBUF, *sq_use]) as i:
                    for q in range(2):
                        slot = matrix(a["w_mlp1_2"], L, chunk * D + i * 512 + q * 256, 256)
                        for c in range(2):
                            banks = [(2 * q + c) * len(segs) + n for n in range(len(segs))]
                            t = transposed(slot, c * P, h2, segs, banks)
                            for bk, (c0, c1) in zip(banks, segs):
                                sb_ = bk % 2
                                y = sq[:, sb_, 0:c1 - c0]
                                b.wait(scalar, t)
                                b.acquire(sq_use[sb_])
                                tk = act.after(scalar.activation(y, bank[bk][:, 0:c1 - c0], ACT.Relu))
                                bank_use[bk].last = [tk]
                                b.wait(vector, tk)
                                tk = dve.after(vector.tensor_tensor(y, y, y, ALU.mult))
                                dst = i * 4 + (2 * q + c)
                                tk = split_out(uh[:, bass.ds(dst, 1), c0:c1].rearrange("p a n -> p (a n)"),
                                               ul[:, bass.ds(dst, 1), c0:c1].rearrange("p a n -> p (a n)"), y, tk)
                                sq_use[sb_].last = [tk]
                out_segs = [(x0, x1, m, 5, h0) for x0, x1, m, _, h0 in out_segs]
                residual(a["w_mlp2_2"], L, lambda k: (uh[:, k, :], ul[:, k, :]), KT, chunk * D, out_segs)
                hid_use.last = [(pe, pe.count, pe.steps)]
            all_done(vector, scalar, tensor)

    load_t = [load(cos2[:], a["cos2"]), load(sin2[:], a["sin2"]), load(perm2[:], a["perm2"]), load(edge[:], a["edge"])]
    b.wait(vector, *load_t)
    b.wait(tensor, *load_t)
    for L in range(n_second):
        second_layer(L, L == DEPTH - 1)
    second.close()

    scale_norm(a["g_final_cols"])
    out = a["out"].rearrange("(k p) t -> k p t", p=P)
    stores = b.counter("stores", step=16)
    all_done(sync)
    for k in range(KT):
        t_out = stores.after(sync.dma_start(out[k], X[:, k, TC:TA]))
    b.wait(sync, t_out)
    return b


def columns(v):
    v = np.asarray(v)
    v = v.reshape(v.shape[:-1] + (v.shape[-1] // P, P))
    return np.ascontiguousarray(np.swapaxes(v, -1, -2))


def swap_matrix(half, span):
    m = np.zeros((P, P), np.float32)
    for r in range(P):
        d = r % HD
        if d < span:
            m[r, r + half if d % (2 * half) < half else r - half] = 1.0
    return m


def constants():
    ident = np.eye(P, dtype=np.float32)
    swap = swap_matrix(8, 16)
    dup = np.zeros((P, P), np.float32)
    dup[np.arange(P) % HD, np.arange(P)] = 1.0
    sel = np.zeros((P, P), np.float32)
    for g in range(4):
        sel[32 * g, 0] = sel[32 * g + 1, 1] = sel[32 * g + 2, 2] = 1.0
    consts = np.stack([ident, swap, np.full((P, P), 1.0 / D, np.float32), dup, dup @ swap, sel], 1)
    d = np.arange(P) % HD
    inv = np.where(d < 16, 500000.0 ** (-(d % 8) / 8.0), 0.0)
    sign = np.where(d < 8, -1.0, np.where(d < 16, 1.0, 0.0))
    negsel = np.zeros((HC, HC, P), np.float32)
    for h in range(HC):
        negsel[h, h] = -1.0
    causal = np.where(np.arange(P)[None, :] <= np.arange(P)[:, None], 0.0, NEG)
    t = np.arange(T)
    j = np.arange(HD // 4)
    freq = 10000.0 ** (-j / (HD // 4.0))
    angle = np.concatenate([(t // 64)[:, None] * freq, (t % 64)[:, None] * freq], -1).T
    angle = angle[np.arange(P) % (HD // 2)]
    half = np.where(np.arange(P) % HD < HD // 2, -1.0, 1.0)[:, None]
    edge = np.ones((P, 4, 16), np.float32)
    for g, w in enumerate(WINDOWS):
        for e in range(8):
            edge[:, g, e] = w / min(w, e + w // 2)
            edge[:, g, 8 + e] = w / min(w, (8 - e) + w // 2)
    second = {"cos2": np.cos(angle).astype(np.float32), "sin2": (np.sin(angle) * half).astype(np.float32),
              "perm2": swap_matrix(HD // 2, HD), "edge": edge}
    return {**second, "consts": np.ascontiguousarray(consts), "rope_cols": np.stack([inv, sign], 1).astype(np.float32),
            "negsel": negsel, "causal": causal.astype(np.float32)}


def lay_out(i):
    i = {k: np.asarray(v) for k, v in i.items()}
    b_in = i["b_in"]
    tiles = np.stack([b_in[:, o:o + P] for o in TILES], -1)
    gates = columns(b_in[:, OG:])
    rel = i["rel_bias"]
    rel = np.concatenate([rel, np.repeat(rel[:, :, -1:], REL_ROW - rel.shape[2], 2)], 2)
    a = {
        "x_t": np.ascontiguousarray(i["x"][0].T), "ctx_t": np.ascontiguousarray(i["ctx_2"][0].T),
        "positions": i["positions"], "c_cols": columns(i["c"][0]),
        "ada_w": np.concatenate([i["ada_w"], i["w_ada_2"]]), "ada_b_cols": columns(np.concatenate([i["ada_b"], i["b_ada_2"]])),
        "cols1": np.concatenate([columns(i["norm1_g"]), columns(i["norm2_g"]), tiles, gates], -1),
        "w_in": i["w_in"], "b_in": b_in, "rel": rel, "w_branch": i["w_branch"], "w_out": i["w_out"],
        "final1_cols": columns(i["final_g"]), "w_ffn_in": i["w_ffn_in"], "w_ffn_out": i["w_ffn_out"], "g_final_cols": columns(i["g_final_2"]),
    }
    a.update({
        "c2_cols": columns(i["c_2"][0]), "cctx_cols": columns(i["c_ctx_2"]),
        "cols2": np.concatenate([columns(i["g_mix_2"]), columns(i["g_mlp_2"]), columns(i["s_pool_2"]),
                                 columns(i["g_subln_2"])], -1),
        "lam": np.stack([i["lam_q1_2"], i["lam_k1_2"], i["lam_q2_2"], i["lam_k2_2"]], 1),
        "w_in_2": i["w_in_2"], "w_pool_2": i["w_pool_2"], "w_out_2": i["w_out_2"],
        "w_mlp1_2": i["w_mlp1_2"], "w_mlp2_2": i["w_mlp2_2"],
    })
    a.update(constants())
    return {k: np.ascontiguousarray(v) for k, v in a.items()}


def kernel(**inputs):
    import concourse.bacc as bacc
    from concourse.bass_utils import run_bass_kernel_spmd

    arrays = lay_out(inputs)

    def build(plan):
        nc = bacc.Bacc("TRN2", target_bir_lowering=False, num_devices=1)
        a = {n: nc.dram_tensor(f"in_{n}", v.shape, mybir.dt.from_np(v.dtype), kind="ExternalInput").ap()
             for n, v in arrays.items()}
        a["out"] = nc.dram_tensor("out_t", (D, T), F32, kind="ExternalOutput").ap()
        with program(nc, plan, a).ctx:
            pass
        return nc

    plan = {}
    build(plan)
    nc = build(plan)
    r = run_bass_kernel_spmd(nc, [{f"in_{n}": v for n, v in arrays.items()}], core_ids=[0])
    return np.ascontiguousarray(r.results[0]["out_t"].T)[None]
```

```python
from contextlib import ExitStack, contextmanager

import numpy as np

import concourse.bass as bass
from concourse import mybir
from concourse.alu_op_type import AluOpType as ALU

F32 = mybir.dt.float32
F32R = mybir.dt.float32r
BF16 = mybir.dt.bfloat16
I32 = mybir.dt.int32
ACT = mybir.ActivationFunctionType
AX = mybir.AxisListType

P = 128
D = 1024
KT = D // P
T = 512
TT = T // P
TC = 256
TA = TC + T
HD = 64
CHUNK = 64
EPS = 1e-6
NEG = -1.0e30
TAKEN = -3.0e38
TOPK = min(256, T // 4)

HA, HB, HC, HI = 6, 5, 5, 8
WA, WB, WC = HA * HD, HB * HD, HC * HD
OQA, OKA, OVA = 0, WA, 2 * WA
OQI = 3 * WA
OKI = OQI + HI * HD
OWI = OKI + HD
OB = OWI + HI
OC = OB + 3 * WB
OF = OC + 3 * WC
OG = OF + HC
INW = OG + 3 * D
FFN = -(-8 * D // 768) * 256
TILES = ([OQA + P * i for i in range(6)] + [OQI + P * i for i in range(4)] + [OKI]
         + [o + P * i for o in (OB, OB + WB, OC, OC + WC) for i in range(3)] + [OF]
         + [o + P * i for o in (OVA, OB + 2 * WB, OC + 2 * WC) for i in range(3)])
TA0, TQI, TKI, TB0, TC0, TF, TV0 = 0, 6, 10, 11, 17, 23, 24
REL = 128

NH2 = 4
POOLW = 512
WINDOWS = (2, 4, 8, 16)
INW2 = 2048
DFF = 4 * D

DEPTH = 2
PAD = 8
UPAD = TA + 4 * PAD
REL_ROW = 512

SLOT = 9 * 2 * P
CREDIT = 4096


class Progress:

    def __init__(self, nc, sem, engine=None, step=1):
        self.sem, self.step, self.steps = sem, step, 0
        self.count = CREDIT
        (engine or nc.sync).sem_inc(sem, self.count)

    def after(self, instruction):
        instruction.then_inc(self.sem, self.step)
        self.builder.waiting.pop(id(self.engine), None)
        self.count = self.count + self.step
        self.steps += self.step
        return (self, self.count, self.steps)


class Buffer:

    def __init__(self, writer):
        self.writer, self.last = writer, []


class Builder:

    def __init__(self, nc, plan):
        self.nc, self.plan, self.n_loops = nc, plan, 0
        self.ctx = ExitStack()
        self.counters, self.seen, self.waiting = [], {}, {}
        self.pe = self.counter("pe_done", nc.tensor)
        self.act = self.counter("act_done", nc.scalar)
        self.dve = self.counter("dve_done", nc.vector)
        self.pool = self.counter("pool_done", nc.gpsimd)
        self.held = self.ctx.enter_context(nc.semaphore("held"))

    def counter(self, name, engine=None, step=1):
        c = Progress(self.nc, self.ctx.enter_context(self.nc.semaphore(name)), engine, step)
        c.engine, c.builder = engine, self
        self.counters.append(c)
        return c

    def wait(self, engine, *tokens):
        for token in tokens:
            if token is None:
                continue
            if isinstance(token, list):
                self.wait(engine, *token)
                continue
            counter, count, steps = token
            key = (id(engine), id(counter))
            if steps is not None and key in self.seen and self.seen[key] >= steps:
                continue
            waiting = self.waiting.setdefault(id(engine), set())
            if not isinstance(count, int) and id(counter) in waiting:
                self.hold(engine)
                waiting.clear()
            engine.wait_ge(counter.sem, count)
            waiting.add(id(counter))
            if not isinstance(count, int) and engine not in (self.nc.tensor, self.nc.scalar):
                self.hold(engine)
                waiting.clear()
            if steps is not None:
                self.seen[key] = steps

    def hold(self, engine):
        engine.sem_inc(self.held, 1)

    def acquire(self, buffer):
        self.wait(buffer.writer, *buffer.last)

    @contextmanager
    def loop(self, trips, buffers, engines=None):
        key = self.n_loops
        self.n_loops += 1
        plan = self.plan.get(key, {})
        start = [(c, c.count, c.steps) for c in self.counters]
        at = {id(c): n for n, (c, _, _) in enumerate(start)}
        delta = plan.get("delta", [0] * len(start))
        ends = plan.get("ends", [None] * len(buffers))
        earlier = {}
        for b, end in zip(buffers, ends):
            met = {n: start[n][2] + off - delta[n] for n, off in end or []}
            open_ = [t for t in b.last if at[id(t[0])] not in met or t[2] is None or t[2] > met[at[id(t[0])]]]
            if b.writer is self.nc.tensor and plan and end and not any(at[id(t[0])] in met for t in open_):
                earlier[id(b)] = before_loop(open_)
            elif not plan or open_:
                self.acquire(b)
        if engines is None:
            self.hold(self.nc.tensor)
        before = [b.last for b in buffers]
        seen = dict(self.seen)
        kw = {} if engines is None else {"engines": engines}
        with self.nc.Fori(0, trips, **kw) as i:
            self.seen = {}
            for (c, count, _), d in zip(start, delta):
                if d:
                    c.count = count + i * d
            carried = []
            for b, end in zip(buffers, ends):
                if end is not None:
                    b.last = [(start[n][0], start[n][1] + i * delta[n] + (off - delta[n]), start[n][2] + off - delta[n])
                              for n, off in end] + earlier.get(id(b), [])
                else:
                    b.last = list(b.last)
                carried.append(b.last)
            yield i
            found = [c.steps - s for c, _, s in start]
            now = []
            for b, was in zip(buffers, carried):
                now.append(None if b.last is was else
                           [(at[id(c)], steps - start[at[id(c)]][2]) for c, _, steps in b.last])
            self.plan[key] = {"delta": found, "ends": now}
        for (c, count, steps), d in zip(start, found):
            c.count = count + trips * d
            c.steps = steps + trips * d
        for b, end, was in zip(buffers, now, before):
            b.last = was if end is None else [
                (start[n][0], start[n][1] + (trips - 1) * found[n] + off,
                 start[n][2] + (trips - 1) * found[n] + off) for n, off in end]
        self.seen = seen


def before_loop(tokens):
    return [(c, count, None) for c, count, _ in tokens]


def dyn(ap, index):
    if isinstance(index, int):
        return ap[:, index]
    got = ap[:, bass.ds(index, 1)]
    if len(got.shape) == 3:
        return got.rearrange("p a n -> p (a n)")
    return got


def program(nc, plan, a, n_first=2, n_second=2):
    b = Builder(nc, plan)
    tensor, vector, scalar, gpsimd, sync = nc.tensor, nc.vector, nc.scalar, nc.gpsimd, nc.sync
    pe, act, dve, pool = b.pe, b.act, b.dve, b.pool

    names = {}

    def sb(scope, name, shape, dt=F32):
        names[name] = names.get(name, 0) + 1
        if names[name] > 1:
            name = f"{name}_{names[name]}"
        return scope.enter_context(nc.sbuf_tensor(name, shape, dt))

    top = b.ctx
    X = sb(top, "x", [P, KT, TA])
    raw = sb(top, "raw_weights", [P, 2, SLOT])
    whi = sb(top, "weights_hi", [P, 2, SLOT], F32R)
    wlo = sb(top, "weights_lo", [P, 2, SLOT], F32R)
    cst = sb(top, "constants", [P, 6, P])
    ident, perm, meanm, dup, dupperm, sel = (cst[:, n, :] for n in range(6))
    identb = sb(top, "identity_bf16", [P, P], BF16)
    causal = sb(top, "causal_bf16", [P, P], BF16)
    eps = sb(top, "eps", [P, 1])
    cond = sb(top, "cond", [P, KT, 32])
    mod = sb(top, "mod", [P, 48, 3])
    ada_bias = sb(top, "ada_bias", [P, 48])
    ada_rows = sb(top, "ada_rows", [P, 2, 256])
    col = sb(top, "norm_columns", [P, 2, KT, 3])
    small = sb(top, "small", [P, 16, 4])
    psum = top.enter_context(nc.psum_tensor("psum", [P, 8 * 512], F32))
    bank = [psum[:, 512 * n:512 * n + 512] for n in range(8)]
    bank_use = [Buffer(tensor) for _ in range(8)]

    arrived = [b.counter(f"weights_arrived{r}", step=16) for r in range(2)]
    loaded = [b.counter(f"small_load{n}", step=16) for n in range(12)]
    loads = [0]
    raw_use = [Buffer(sync), Buffer(sync)]
    split_use = [Buffer(gpsimd), Buffer(gpsimd)]
    ring, split_ring = [0], [0]

    def load(dst, src):
        loads[0] += 1
        return loaded[loads[0] % 12].after(scalar.dma_start(dst, src))

    def fetch(kt, cols, pieces):
        r = ring[0] % 2
        ring[0] += 1
        view = raw[:, r, 0:kt * cols].rearrange("p (k n) -> p k n", k=kt)
        b.acquire(raw_use[r])
        for ks, cs, rows, src in pieces:
            token = arrived[r].after(sync.dma_start(view[0:rows, ks, cs], src))
        return r, view, token

    def weights(kt, cols, pieces):
        from_, _, token = fetch(kt, cols, pieces)
        n = kt * cols
        r = split_ring[0] % 2
        split_ring[0] += 1
        b.acquire(split_use[r])
        b.wait(gpsimd, token)
        hi_done = pool.after(gpsimd.tensor_scalar(whi[:, r, 0:n], raw[:, from_, 0:n], 1.0, 1.0, ALU.mult, ALU.mult))
        b.wait(gpsimd, hi_done)
        done = pool.after(gpsimd.tensor_tensor(wlo[:, r, 0:n], raw[:, from_, 0:n], whi[:, r, 0:n].bitcast(F32),
                                               ALU.subtract))
        raw_use[from_].last = [done]
        hi = whi[:, r, 0:n].rearrange("p (k n) -> p k n", k=kt)
        lo = wlo[:, r, 0:n].rearrange("p (k n) -> p k n", k=kt)
        return r, hi, lo, done

    def rows_of(w, l, r0, kt, c0, cols):
        if l is None:
            v = w[r0:r0 + kt * P] if isinstance(r0, int) else w[bass.ds(r0, kt * P)]
        else:
            v = w[bass.ds(l, 1)].rearrange("l r c -> (l r) c") if not isinstance(l, int) else w[l]
            v = v[r0:r0 + kt * P] if isinstance(r0, int) else v[bass.ds(r0, kt * P)]
        v = v.rearrange("(k p) c -> p k c", p=P)
        return v[:, :, c0:c0 + cols] if isinstance(c0, int) else v[:, :, bass.ds(c0, cols)]

    def matrix(w, l, c0, cols, kt=KT, r0=0):
        return weights(kt, cols, [(slice(0, kt), slice(0, cols), P, rows_of(w, l, r0, kt, c0, cols))])

    def product(out, stationary, moving, first, last):
        (sh, sl), (mh, ml) = stationary, moving
        tensor.matmul(out, sh, mh, start=first, stop=False)
        tensor.matmul(out, sh, ml, start=False, stop=False)
        return tensor.matmul(out, sl, mh, start=False, stop=last)

    cond_in = sb(top, "cond_in", [P, 3, KT])
    cond_sigmoid = sb(top, "cond_sigmoid", [P, 3, KT])
    t_cond = [load(cond_in[:, m, :], a[name]) for m, name in enumerate(("c_cols", "c2_cols", "cctx_cols"))]
    for r in range(2):
        raw_use[r].last = [dve.after(vector.memset(raw[:, r, :], 0.0))]
    t_const = load(cst[:], a["consts"])
    with ExitStack() as s:
        cm = sb(s, "causal_f32", [P, P])
        t_cm = load(cm[:], a["causal"])
        b.wait(vector, t_cm, t_const)
        dve.after(vector.tensor_copy(identb[:], ident))
        dve.after(vector.tensor_copy(causal[:], cm[:]))
        dve.after(vector.memset(eps[:], EPS))
        t_init = dve.after(vector.memset(small[:], 0.0))
        b.wait(tensor, t_init, t_const)

    def all_done(*engines):
        for e in engines:
            for c in (pe, act, dve):
                if c.steps:
                    b.wait(e, (c, c.count, c.steps))

    def condition():
        z = dve.after(vector.memset(cond[:], 0.0))
        b.wait(scalar, t_cond)
        t = act.after(scalar.activation(cond_sigmoid[:], cond_in[:], ACT.Sigmoid))
        b.wait(vector, t, z)
        for n in range(3):
            dve.after(vector.tensor_tensor(cond[:, :, n], cond_in[:, n, :], cond_sigmoid[:, n, :], ALU.mult))
        all_done(scalar, tensor)

    def ada_first(rows):
        m = 3
        row_use = Buffer(scalar)
        t_b = load(ada_bias[:], a["ada_b_cols"][0])
        b.wait(vector, t_b)
        with b.loop(2, [*raw_use, *bank_use[0:4], row_use]) as i:
            for half in range(2):
                b.acquire(bank_use[half])
                for q in range(2):
                    c0 = i * 1024 + (half * 2 + q) * 256
                    r, view, t = fetch(KT, 256, [(slice(0, KT), slice(0, 256), P,
                                                  rows_of(a["ada_w"], 0, 0, KT, c0, 256))])
                    b.wait(tensor, t)
                    for kk in range(2):
                        for g in range(4):
                            ins = tensor.matmul(bank[half][32 * g:32 * g + 32, 256 * q:256 * q + 256],
                                                cond[:, 4 * kk + g, :], view[:, 4 * kk + g, :],
                                                start=kk == 0, stop=kk == 1, tile_position=(0, 32 * g))
                    t_rows = pe.after(ins)
                    raw_use[r].last = [t_rows]
                b.wait(scalar, t_rows)
                if half == 0:
                    b.acquire(row_use)
                t_copy = act.after(scalar.copy(rows[:, half, :], bank[half][:, :]))
                bank_use[half].last = [t_copy]
                b.acquire(bank_use[2 + half])
                b.wait(tensor, t_copy)
                for n in range(4):
                    ins = tensor.matmul(bank[2 + half][:, n * m:n * m + m], rows[:, half, n * P:n * P + P],
                                        sel[:, 0:m], start=n == 0, stop=n == 3, skip_group_check=True)
                t_cols = pe.after(ins)
                b.wait(vector, t_cols)
                bc = ada_bias[:, bass.ds(i * 8 + half * 4, 4)]
                for mm in range(m):
                    t_mod = dve.after(vector.tensor_tensor(
                        mod[:, bass.ds(i * 8 + half * 4, 4), mm],
                        bank[2 + half][:, 0:4 * m].rearrange("p (n m) -> p n m", m=m)[:, :, mm], bc, ALU.add))
                bank_use[2 + half].last = [t_mod]
                if half == 1:
                    row_use.last = [t_cols]
        all_done(vector, scalar, tensor)

    def ada_steps(slots, row_banks, col_bank):
        n = len(slots)
        calls = iter(range(n + 2))
        row_use = [Buffer(scalar), Buffer(scalar)]
        t_rows, t_copy = {}, {}

        def step():
            c = next(calls, None)
            if c is None:
                return
            if 1 <= c <= n:
                q = (c - 1) % 2
                bk = row_banks[(c - 1) % len(row_banks)]
                b.wait(scalar, t_rows[c - 1])
                b.acquire(row_use[q])
                t_copy[c - 1] = act.after(scalar.copy(ada_rows[:, q, :], bank[bk][:, 0:256]))
                bank_use[bk].last = [t_copy[c - 1]]
            if c < n:
                bk = row_banks[c % len(row_banks)]
                r, view, t = fetch(KT, 256, [(slice(0, KT), slice(0, 256), P,
                                              rows_of(a["ada_w"], slots[c][0], 0, KT, slots[c][1] * 256, 256))])
                b.wait(tensor, t)
                b.acquire(bank_use[bk])
                for kk in range(2):
                    for g in range(4):
                        ins = tensor.matmul(bank[bk][32 * g:32 * g + 32, 0:256], cond[:, 4 * kk + g, :],
                                            view[:, 4 * kk + g, :], start=kk == 0, stop=kk == 1,
                                            tile_position=(0, 32 * g))
                t_rows[c] = pe.after(ins)
                raw_use[r].last = [t_rows[c]]
            if c >= 2:
                q = (c - 2) % 2
                b.wait(tensor, t_copy[c - 2])
                if c == 2:
                    b.acquire(bank_use[col_bank])
                for h in range(2):
                    at = (2 * (c - 2) + h) * 3
                    ins = tensor.matmul(bank[col_bank][:, at:at + 3], ada_rows[:, q, h * P:h * P + P], sel[:, 0:3],
                                        start=c == 2 and h == 0, stop=c == n + 1 and h == 1, skip_group_check=True)
                t = pe.after(ins)
                row_use[q].last = [t]
                step.last = t

        def finish():
            for _ in range(n + 2):
                step()
            b.wait(vector, step.last)
            at = 0
            while at < n:
                j0, end = slots[at][1], at + 1
                while end < n and slots[end][1] == j0 + end - at:
                    end += 1
                j1 = j0 + end - at
                for m in range(3):
                    t = dve.after(vector.tensor_tensor(
                        mod[:, 2 * j0:2 * j1, m],
                        bank[col_bank][:, 6 * at:6 * end].rearrange("p (n m) -> p n m", m=3)[:, :, m],
                        ada_bias[:, 2 * j0:2 * j1], ALU.add))
                at = end
            bank_use[col_bank].last = [t]
        step.finish = finish
        return step

    def ada_slots(layer, j0, j1):
        return [(layer + j // 24, j % 24) for j in range(j0, j1)]

    def load_bias(layer, with_next):
        all_done(scalar)
        for l_, c0, c1 in ((layer, 16, 48), (layer + 1, 0, 16))[0:1 + with_next]:
            src = a["ada_b_cols"][l_] if isinstance(l_, int) else \
                a["ada_b_cols"][bass.ds(l_, 1)].rearrange("l p n -> (l p) n")
            b.wait(vector, load(ada_bias[:, c0:c1], src[:, c0:c1]))

    def norm_scales(g, sc, sh, m):
        b.wait(vector, (dve, dve.count, dve.steps))
        t = dve.after(vector.scalar_tensor_tensor(out=col[:, 0, :, m], in0=mod[:, sc * 8:sc * 8 + 8, m], scalar=1.0,
                                                  in1=g, op0=ALU.add, op1=ALU.mult))
        t = dve.after(vector.tensor_copy(col[:, 1, :, m], mod[:, sh * 8:sh * 8 + 8, m]))
        return t

    def squares(x0, x1, tmp, bk):
        n = x1 - x0
        b.acquire(bank_use[bk])
        for pair in range(KT // 2):
            first, second = (tmp["work"][:, 2 * (pair % 2) + i, 0:n] for i in range(2))
            b.acquire(tmp["sq_use"][pair % 2])
            act.after(scalar.activation(first, X[:, 2 * pair, x0:x1], ACT.Square))
            t = act.after(scalar.activation(second, X[:, 2 * pair + 1, x0:x1], ACT.Square))
            b.wait(vector, t)
            t = dve.after(vector.tensor_tensor(first, first, second, ALU.add))
            b.wait(tensor, t)
            t = pe.after(tensor.matmul(bank[bk][:, 0:n], meanm, first, start=pair == 0, stop=pair == KT // 2 - 1))
            tmp["sq_use"][pair % 2].last = [t]
        return t

    def inverse_root(t, x0, x1, tmp, bk):
        rstd = tmp["rstd"][:, 0:x1 - x0]
        b.wait(scalar, t)
        b.acquire(tmp["rstd_use"])
        t = act.after(scalar.activation(rstd, bank[bk][:, 0:x1 - x0], ACT.Sqrt, bias=eps[:, 0:1]))
        bank_use[bk].last = [t]
        b.wait(vector, t)
        t = dve.after(vector.reciprocal(rstd, rstd))
        b.wait(vector, t)
        return rstd

    def norm_buffers(s):
        return {"rstd": sb(s, "rstd", [P, 512]), "work": sb(s, "norm_work", [P, 4, 512]),
                "sq_use": [Buffer(scalar), Buffer(scalar)], "rstd_use": Buffer(scalar)}

    h_ready = {}

    def norm(segments, hh, hl, ada_parts):
        with ExitStack() as s:
            tmp = norm_buffers(s)
            scaled = tmp["work"]
            use = [Buffer(vector) for _ in range(4)]
            all_done(scalar, vector, tensor)
            for seg, (x0, x1, h0, m) in enumerate(segments):
                n = x1 - x0
                step = ada_steps(ada_parts[seg], (0, 1), 2)
                step()
                step()
                t = squares(x0, x1, tmp, 7 - seg)
                step()
                rstd = inverse_root(t, x0, x1, tmp, 7 - seg)
                for u_ in use:
                    u_.last = [t]
                th = {}
                for k in range(KT + 1):
                    if k < KT:
                        u = scaled[:, k % 4, 0:n]
                        b.acquire(use[k % 4])
                        t = dve.after(vector.scalar_tensor_tensor(out=u, in0=X[:, k, x0:x1], scalar=col[:, 0, k, m:m + 1],
                                                                  in1=rstd, op0=ALU.mult, op1=ALU.mult))
                        tmp["rstd_use"].last = [t]
                        b.wait(scalar, t)
                        th[k] = act.after(scalar.activation(hh[:, k, h0:h0 + n], u, ACT.Identity, bias=col[:, 1, k, m:m + 1]))
                    step()
                    if k:
                        k -= 1
                        b.wait(vector, th[k])
                        t = dve.after(vector.scalar_tensor_tensor(
                            out=hl[:, k, h0:h0 + n], in0=scaled[:, k % 4, 0:n], scalar=col[:, 1, k, m:m + 1],
                            in1=hh[:, k, h0:h0 + n].bitcast(F32), op0=ALU.add, op1=ALU.subtract))
                        use[k % 4].last = [t]
                        h_ready[k] = t
                for q in range(2):
                    tmp["sq_use"][q].last = [t]
                step.finish()
            all_done(scalar, vector)

    def split_out(hi, lo, value, token):
        b.wait(scalar, token)
        t = act.after(scalar.copy(hi, value))
        b.wait(vector, t, token)
        return dve.after(vector.tensor_tensor(lo, value, hi.bitcast(F32), ALU.subtract))

    def transposed(slot, c, h, chunks, banks, k_rows=None):
        r, hi, lo, ready = slot
        b.wait(tensor, ready)
        for (c0, c1), bk in zip(chunks, banks):
            b.acquire(bank_use[bk])
            kt = hi.shape[1]
            for k in range(kt):
                n = P if k_rows is None else k_rows[k]
                xh, xl = h(k)
                if k in h_ready:
                    b.wait(tensor, h_ready.pop(k))
                ins = product(bank[bk][:, 0:c1 - c0], (hi[0:n, k, c:c + P], lo[0:n, k, c:c + P]),
                              (xh[0:n, c0:c1], xl[0:n, c0:c1]), k == 0, k == kt - 1)
        t = pe.after(ins)
        split_use[r].last = [t]
        return t

    def natural(slot, c, n, h, tok0, bk):
        r, hi, lo, ready = slot
        b.wait(tensor, ready)
        b.acquire(bank_use[bk])
        for k in range(KT):
            xh, xl = h(k)
            ins = product(bank[bk][:, 0:n], (xh[:, tok0:tok0 + P], xl[:, tok0:tok0 + P]),
                          (hi[:, k, c:c + n], lo[:, k, c:c + n]), k == 0, k == KT - 1)
        t = pe.after(ins)
        split_use[r].last = [t]
        return t

    ALLBUF = [*raw_use, *split_use, *bank_use]

    first = ExitStack()
    hh = sb(first, "h_hi", [P, KT, T], F32R)
    hl = sb(first, "h_lo", [P, KT, T], F32R)
    ropec = sb(first, "rope_cos", [P, T])
    ropes = sb(first, "rope_sin", [P, T])
    pcol = sb(first, "layer_columns", [P, 2 * KT + len(TILES) + 3 * KT])
    wicol = sb(first, "index_weights", [P, TT, HI])
    stat = sb(first, "softmax_stats", [P, 4, 4])

    def h1(k):
        return hh[:, k, :], hl[:, k, :]

    def rope_tables():
        with ExitStack() as s:
            pi_ = sb(s, "pos_int", [P, T], I32)
            ang = sb(s, "angle", [P, T])
            turns = sb(s, "turns", [P, T])
            ti = load(pi_[:], a["positions"].to_broadcast((P, T)))
            tc = load(small[:, 0, 0:2], a["rope_cols"])
            b.wait(vector, tc, ti)

            def step(ins):
                t = dve.after(ins)
                b.wait(vector, t)
                return t
            step(vector.tensor_copy(ang[:], pi_[:]))
            step(vector.tensor_scalar(ang[:], ang[:], small[:, 0, 0:1], None, ALU.mult))
            magic = 1.5 * 2.0 ** 23
            tau = 2.0 * np.pi
            parts = [6.28125]
            parts.append(float(np.float32(np.round((tau - parts[0]) * 2 ** 21) / 2 ** 21)))
            parts.append(float(tau - parts[0] - parts[1]))
            for quarter, red in ((0.25, ropec), (0.0, ropes)):
                step(vector.tensor_scalar(turns[:], ang[:], float(1.0 / tau), quarter, ALU.mult, ALU.add))
                step(vector.tensor_scalar(turns[:], turns[:], magic, None, ALU.add))
                step(vector.tensor_scalar(turns[:], turns[:], magic, None, ALU.subtract))
                src = ang
                for part in parts:
                    step(vector.scalar_tensor_tensor(out=red[:], in0=turns[:], scalar=-part, in1=src[:],
                                                     op0=ALU.mult, op1=ALU.add))
                    src = red
                if quarter:
                    step(vector.tensor_scalar(red[:], red[:], float(np.pi / 2), None, ALU.add))
                t = step(vector.tensor_scalar(red[:], red[:], 3.14159, -3.14159, ALU.min, ALU.max))
        return t

    def rope_sines(t):
        b.wait(scalar, t)
        for x in (ropec, ropes):
            t = act.after(scalar.activation(x[:], x[:], ACT.Sin))
        b.wait(vector, t)
        dve.after(vector.tensor_scalar(ropes[:], ropes[:], small[:, 0, 1:2], None, ALU.mult))

    def rope(t_in, x, cos, sin, tmp, tmp_use, bk, perm=perm):
        b.wait(tensor, t_in)
        b.acquire(bank_use[bk])
        t = pe.after(tensor.matmul(bank[bk][:, 0:x.shape[1]], perm, x, start=True, stop=True))
        b.wait(vector, t)
        b.acquire(tmp_use)
        t1 = dve.after(vector.tensor_tensor(tmp, bank[bk][:, 0:x.shape[1]], sin, ALU.mult))
        bank_use[bk].last = [t1]
        t2 = dve.after(vector.tensor_tensor(x, x, cos, ALU.mult))
        b.wait(vector, t1, t2)
        t3 = dve.after(vector.tensor_tensor(x, x, tmp, ALU.add))
        tmp_use.last = [t3]
        return t3

    def first_layer(l):
        b.wait(scalar, t_x, t_ctx)
        b.wait(vector, t_x, t_ctx)
        wi = a["w_in"]
        all_done(scalar)
        t_cols = load(pcol[:], a["cols1"][bass.ds(l, 1)].rearrange("l p n -> (l p) n"))
        load_bias(l, True)
        bt = pcol[:, 2 * KT:2 * KT + len(TILES)]
        bg = pcol[:, 2 * KT + len(TILES):]
        b.wait(vector, t_cols)
        b.wait(scalar, t_cols)
        norm_scales(pcol[:, 0:KT], 1, 0, 0)
        norm([(TC, TA, 0, 0)], hh, hl, [ada_slots(l, 8, 12)])

        mix = ExitStack()
        oh = sb(mix, "o_hi", [P, 9, T], F32R)
        ol = sb(mix, "o_lo", [P, 9, T], F32R)
        att = ExitStack()
        maska = sb(att, "select_mask", [P, TT, T], BF16)
        qk = sb(att, "qk", [P, 6, T])
        val = sb(att, "values", [P, TT, WA])
        soft = sb(att, "softmax_buffers", [P, 8, T])
        logit, prob, probt, biast = (soft[:, n:n + 2, :] for n in (0, 2, 4, 6))
        relt = sb(att, "bias_diagonals", [P, 384])
        frow = sb(att, "forget", [P, 2, T])
        fcol = sb(att, "forget_columns", [P, TT, HC])
        bq = sb(att, "scaled_query_bias", [P, 3, 3])
        logit_use = [Buffer(vector), Buffer(vector)]
        prob_use = [Buffer(scalar), Buffer(scalar)]
        probt_use = [Buffer(scalar), Buffer(scalar)]
        bias_use = [Buffer(vector), Buffer(vector)]
        relt_use = Buffer(scalar)

        for n, tile0 in enumerate((TA0, TB0, TC0)):
            t_bq = dve.after(vector.tensor_scalar(bq[:, n, :], bt[:, tile0:tile0 + 3], HD ** -0.5, None, ALU.mult))
        with ExitStack() as s:
            work, relu, tmp, ki = soft[:, 0:3, :], soft[:, 3:5, :], soft[:, 5, :], soft[:, 7, :]
            qi = [val[:].rearrange("p n c -> p (n c)")[:, T * n:T * n + T] for n in range(3)] + [frow[:, 0, :]]
            tmp_use = Buffer(vector)
            all_done(tensor, vector, scalar)
            t_q = []
            for half in range(2):
                slot = matrix(wi, l, OQI + 256 * half, 256)
                for q in range(2):
                    n = 2 * half + q
                    t = transposed(slot, q * P, h1, [(0, T)], [n])
                    b.wait(scalar, t)
                    t = act.after(scalar.activation(qi[n], bank[n][:, :], ACT.Identity, bias=bt[:, TQI + n:TQI + n + 1]))
                    bank_use[n].last = [t]
                    t_q.append(t)
            slot = matrix(wi, l, OKI, P)
            t = transposed(slot, 0, h1, [(0, T)], [4])
            b.wait(scalar, t)
            t_k = act.after(scalar.activation(ki, bank[4][:, :], ACT.Identity, bias=bt[:, TKI:TKI + 1]))
            bank_use[4].last = [t_k]
            for n in range(4):
                t_q[n] = rope(t_q[n], qi[n], ropec[:], ropes[:], tmp, tmp_use, 5 + n % 2)
            b.wait(tensor, t_k)
            b.acquire(bank_use[7])
            for n in range(TT):
                ins = tensor.transpose(bank[7][:, n * P:n * P + P], ki[:, n * P:n * P + P], ident)
            t = pe.after(ins)
            b.wait(vector, t)
            t_w = dve.after(vector.tensor_scalar(
                wicol[:], bank[7][:, :].rearrange("p (n c) -> p n c", n=TT)[:, :, HD:HD + HI],
                float(HI ** -0.5 * HD ** -0.5), None, ALU.mult))
            bank_use[7].last = [t_w]
            b.acquire(bank_use[5])
            b.acquire(bank_use[6])
            tensor.matmul(bank[5][:, :], dup, ki, start=True, stop=True)
            t = pe.after(tensor.matmul(bank[6][:, :], dupperm, ki, start=True, stop=True))
            b.wait(vector, t)
            b.acquire(tmp_use)
            t1 = dve.after(vector.tensor_tensor(ki, bank[5][:, :], ropec[:], ALU.mult))
            t2 = dve.after(vector.tensor_tensor(tmp, bank[6][:, :], ropes[:], ALU.mult))
            bank_use[5].last = [t1]
            bank_use[6].last = [t2]
            b.wait(vector, t1, t2)
            t_k = dve.after(vector.tensor_tensor(ki, ki, tmp, ALU.add))
            b.wait(tensor, t_k)
            b.wait(scalar, t_k)
            relu_use = [Buffer(scalar), Buffer(scalar)]
            n = 0
            done = [None] * 3
            for h in range(HI):
                for i in range(1, TT):
                    w = (i + 1) * P
                    bk, q = n % 4, n % 2
                    n += 1
                    p0 = HD * (h % 2)
                    b.acquire(bank_use[bk])
                    t = pe.after(tensor.matmul(bank[bk][:, 0:w], qi[h // 2][p0:p0 + HD, i * P:i * P + P],
                                               ki[p0:p0 + HD, 0:w], start=True, stop=True))
                    b.wait(scalar, t)
                    b.acquire(relu_use[q])
                    t = act.after(scalar.activation(relu[:, q, 0:w], bank[bk][:, 0:w], ACT.Relu))
                    bank_use[bk].last = [t]
                    b.wait(vector, t, t_w, done[i - 1])
                    wc = wicol[:, i, h:h + 1]
                    if h == 0:
                        t = dve.after(vector.tensor_scalar(work[:, i - 1, 0:w], relu[:, q, 0:w], wc, None, ALU.mult))
                    else:
                        t = dve.after(vector.scalar_tensor_tensor(out=work[:, i - 1, 0:w], in0=relu[:, q, 0:w], scalar=wc,
                                                                  in1=work[:, i - 1, 0:w], op0=ALU.mult, op1=ALU.add))
                    done[i - 1] = t
                    relu_use[q].last = [t]
            for i in range(1, TT):
                b.wait(vector, done[i - 1])
                done[i - 1] = dve.after(vector.memset(work[0:CHUNK, i - 1, (i + 1) * P - CHUNK:(i + 1) * P], NEG))
            top8 = small[:, 1:7, :].rearrange("p a c -> p (a c)")
            b.wait(vector, *done)
            scored = list(done)
            chain = [Buffer(vector) for _ in range(3)]
            for i in range(3):
                chain[i].last = [done[i]]
            with b.loop(TOPK // 8, chain, engines=[mybir.EngineType.DVE]) as _:
                tops = []
                for i in range(3):
                    b.acquire(chain[i])
                    tops.append(dve.after(vector.max(top8[:, 8 * i:8 * i + 8], work[:, i, 0:(i + 2) * P])))
                for i in range(3):
                    w = work[:, i, 0:(i + 2) * P]
                    b.wait(vector, tops[i])
                    chain[i].last = [dve.after(vector.match_replace(
                        out=w, in_to_replace=top8[:, 8 * i:8 * i + 8], in_values=w, imm_value=TAKEN))]

        def select():
            for i in range(3):
                b.acquire(chain[i])
                dve.after(vector.tensor_scalar(maska[:, i + 1, 0:(i + 2) * P], work[:, i, 0:(i + 2) * P],
                                               -2.9e38, NEG, ALU.is_gt, ALU.mult))
            t = dve.after(vector.memset(maska[:, 0, 0:P], 0.0))
            b.wait(vector, t)
            t = dve.after(vector.memset(maska[0:CHUNK, 0, CHUNK:P], NEG))
            b.wait(vector, t)

        def project(kind, o_q, o_k, o_v, n_heads, tile0, with_rope, extra=0):
            n = 0
            ts, t_v, late = [], [], []
            vt_use = [prob_use[1], probt_use[0]]

            def turn(tile, t):
                vt, bk = soft[:, 3 + tile % 2, :], 5 + tile % 2
                b.wait(tensor, t)
                b.acquire(bank_use[bk])
                for j in range(TT):
                    ins = tensor.transpose(bank[bk][:, j * P:j * P + P], vt[:, j * P:j * P + P], ident)
                t = pe.after(ins)
                vt_use[tile % 2].last = [t]
                b.wait(scalar, t)
                t = act.after(scalar.copy(val[:, :, tile * P:tile * P + P],
                                          bank[bk][:, :].rearrange("p (n c) -> p n c", n=TT)))
                bank_use[bk].last = [t]
                t_v.append(t)

            for c0, cols in ((0, 256), (256, P)):
                slot = matrix(wi, l, o_v + c0, cols + (extra if c0 else 0))
                for q in range(cols // P):
                    tile = c0 // P + q
                    bk, vt = n % 4, soft[:, 3 + tile % 2, :]
                    n += 1
                    t = transposed(slot, q * P, h1, [(0, T)], [bk])
                    b.wait(scalar, t)
                    b.acquire(vt_use[tile % 2])
                    at = TV0 + 3 * kind + tile
                    t = act.after(scalar.activation(vt, bank[bk][:, :], ACT.Identity, bias=bt[:, at:at + 1]))
                    bank_use[bk].last = [t]
                    if late:
                        turn(*late.pop())
                    late.append((tile, t))
            if extra:
                forget(slot)
            for which, o in ((0, o_q), (1, o_k)):
                for c0, cols in ((0, 256), (256, 128)):
                    slot = matrix(wi, l, o + c0, cols)
                    for q in range(cols // P):
                        tile = which * 3 + (c0 // P) + q
                        bk = n % 4
                        n += 1
                        t = transposed(slot, q * P, h1, [(0, T)], [bk])
                        b.wait(scalar, t)
                        if which == 0:
                            t = act.after(scalar.activation(qk[:, tile, :], bank[bk][:, :], ACT.Identity,
                                                            bias=bq[:, kind, tile:tile + 1], scale=HD ** -0.5))
                        else:
                            t = act.after(scalar.activation(qk[:, tile, :], bank[bk][:, :], ACT.Identity,
                                                            bias=bt[:, tile0 + tile:tile0 + tile + 1]))
                        bank_use[bk].last = [t]
                        ts.append(t)
                        if late:
                            turn(*late.pop())
                        if extra and tile == 3:
                            forget_columns()
            if kind == 0:
                ada_a()
                select()
            if with_rope:
                for tile in range(6):
                    b.wait(vector, ts[tile])
                    ts[tile] = rope(ts[tile], qk[:, tile, :], ropec[:], ropes[:], biast[:, tile % 2, :],
                                    bias_use[tile % 2], 5 + tile % 2)
                    ada_a()
                ada_a.finish()
            return ts, t_v

        def attend(n_heads, tile0, kind, t_qk, t_v):
            units = [(h, i) for h in range(n_heads) for i in range(TT)]
            st = {}

            def load_diagonals(h):
                b.acquire(relt_use)
                src = a["rel"]
                st["d", h] = load(relt[:], bass.AP(src.tensor, l * (HB * REL_ROW) + h * REL_ROW, [[1, P], [1, 384]]))

            def prepare(h):
                if kind == "B":
                    b.wait(vector, st["d", h])
                    b.acquire(bias_use[h % 2])
                    bt_ = biast[:, h % 2, :]
                    t1 = dve.after(vector.tensor_copy(bt_[:, 256:512], relt[:, 256:0:-1]))
                    t2 = dve.after(vector.tensor_copy(bt_[:, 0:256], relt[:, 383:384].to_broadcast((P, 256))))
                    b.wait(vector, t1, t2)
                    t = dve.after(vector.memset(bt_[0:CHUNK, 448:512], NEG))
                    b.wait(vector, t)
                    relt_use.last = [t]
                if kind == "C":
                    b.acquire(bank_use[6 + h % 2])
                    st["nf", h] = pe.after(tensor.matmul(bank[6 + h % 2][:, :], negsel[0:HC, h, :], frow[0:HC, 1, :],
                                                         start=True, stop=True))

            def scores(u):
                h, i = units[u]
                if i == 0:
                    b.wait(tensor, t_qk[h // 2], t_qk[3 + h // 2])
                    prepare(h)
                if kind == "B" and i == 1 and h + 1 < n_heads:
                    load_diagonals(h + 1)
                w = (i + 1) * P
                p0 = HD * (h % 2)
                bk = u % 2
                if kind == "C":
                    q = u % 2
                    b.wait(scalar, st["nf", h])
                    b.wait(scalar, *bias_use[q].last)
                    t = act.after(scalar.activation(biast[:, q, 0:w], bank[6 + h % 2][:, 0:w], ACT.Identity,
                                                    bias=fcol[:, i, h:h + 1]))
                    if i == TT - 1:
                        bank_use[6 + h % 2].last = [t]
                    st["b", u] = t
                b.acquire(bank_use[bk])
                if kind == "A":
                    tensor.matmul(bank[bk][:, 0:w], identb[:], maska[:, i, 0:w], start=True, stop=False)
                if kind == "C":
                    tensor.matmul(bank[bk][:, w - P:w], identb[:], causal[:], start=True, stop=False)
                q_ = qk[p0:p0 + HD, h // 2, i * P:i * P + P]
                k_ = qk[p0:p0 + HD, 3 + h // 2, 0:w]
                if kind == "C":
                    ins = tensor.matmul(bank[bk][:, w - P:w], q_, k_[:, w - P:w], start=False, stop=True)
                    if i:
                        ins = tensor.matmul(bank[bk][:, 0:w - P], q_, k_[:, 0:w - P], start=True, stop=True)
                else:
                    ins = tensor.matmul(bank[bk][:, 0:w], q_, k_, start=kind == "B", stop=True)
                st["s", u] = pe.after(ins)

            def maximum(u):
                h, i = units[u]
                w = (i + 1) * P
                bk, q = u % 2, u % 2
                nm, rs = stat[:, u % 4, 0:1], stat[:, u % 4, 1:2]
                if kind == "A":
                    b.wait(vector, st["s", u])
                    t = dve.after(vector.tensor_reduce(nm, bank[bk][:, 0:w], AX.X, ALU.max, negate=True))
                else:
                    if kind == "B":
                        extra_logit = biast[:, h % 2, T - w:T]
                    else:
                        extra_logit = biast[:, q, 0:w]
                        b.wait(vector, st["b", u])
                    b.wait(vector, st["s", u])
                    b.acquire(logit_use[q])
                    t = dve.after(vector.tensor_tensor_reduce(
                        out=logit[:, q, 0:w], in0=bank[bk][:, 0:w], in1=extra_logit, scale=-1.0, scalar=3e38,
                        op0=ALU.add, op1=ALU.min, accum_out=nm))
                    bank_use[bk].last = [t]
                    if kind == "C":
                        bias_use[q].last = [t]
                    elif i == TT - 1:
                        bias_use[h % 2].last = [t]
                st["m", u] = t

            def exponential(u):
                h, i = units[u]
                w = (i + 1) * P
                bk, q = u % 2, u % 2
                nm, rs = stat[:, u % 4, 0:1], stat[:, u % 4, 1:2]
                src, scale = (bank[bk][:, 0:w], 1.0) if kind == "A" else (logit[:, q, 0:w], -1.0)
                b.wait(scalar, st["m", u])
                b.acquire(prob_use[q])
                t = act.after(scalar.activation(prob[:, q, 0:w], src, ACT.Exp, bias=nm, scale=scale, accum_out=rs))
                if kind == "A":
                    bank_use[bk].last = [t]
                else:
                    logit_use[q].last = [t]
                st["e", u] = t

            def normalise(u):
                h, i = units[u]
                w = (i + 1) * P
                q = u % 2
                rs, rr = stat[:, u % 4, 1:2], stat[:, u % 4, 2:3]
                b.wait(vector, st["e", u])
                t = dve.after(vector.reciprocal(rr, rs))
                b.wait(vector, t)
                t = dve.after(vector.tensor_scalar(prob[:, q, 0:w], prob[:, q, 0:w], rr, None, ALU.mult))
                b.wait(tensor, t)
                bk = 2 + q
                b.acquire(bank_use[bk])
                for j in range(i + 1):
                    ins = tensor.transpose(bank[bk][:, j * P:j * P + P], prob[:, q, j * P:j * P + P], ident)
                t = pe.after(ins)
                prob_use[q].last = [t]
                st["p", u] = t

            def take_out(u):
                h, i = units[u]
                w = (i + 1) * P
                q = u % 2
                bk = 2 + q
                b.wait(scalar, st["p", u])
                b.acquire(probt_use[q])
                t = act.after(scalar.copy(probt[:, q, 0:w], bank[bk][:, 0:w]))
                bank_use[bk].last = [t]
                st["t", u] = t

            def values(u):
                h, i = units[u]
                q = u % 2
                p0 = HD * (h % 2)
                ob = 4 + (h // 2) % 2
                b.wait(tensor, st["t", u])
                if h % 2 == 0 and i == 0:
                    b.acquire(bank_use[ob])
                for j in range(i + 1):
                    ins = tensor.matmul(bank[ob][p0:p0 + HD, i * P:i * P + P], val[:, j, h * HD:h * HD + HD],
                                        probt[:, q, j * P:j * P + P], start=j == 0, stop=j == i)
                t = pe.after(ins)
                probt_use[q].last = [t]
                if i == TT - 1 and (h % 2 == 1 or h == n_heads - 1):
                    n = p0 + HD
                    tile = tile0 + h // 2
                    t = split_out(oh[0:n, tile, :], ol[0:n, tile, :], bank[ob][0:n, :], t)
                    bank_use[ob].last = [t]

            if kind == "B":
                load_diagonals(0)
            step = ada_steps(ada_slots(l, *{"A": (16, 22), "B": (22, 28)}[kind]), (6,), 7) if kind != "C" else None
            scores(0)
            for u in range(len(units) + 2):
                if u == 2:
                    b.wait(tensor, *t_v)
                if u + 1 < len(units):
                    scores(u + 1)
                if u < len(units):
                    maximum(u)
                    exponential(u)
                if 1 <= u <= len(units):
                    normalise(u - 1)
                    take_out(u - 1)
                if u >= 2:
                    values(u - 2)
                if step and u % 5 in (1, 3):
                    step()
            if step:
                step.finish()

        z, F = (frow[0:HC, n, :] for n in range(2))
        f_sum = []

        def forget(slot):
            t = transposed(slot, HD, h1, [(0, T)], [4])
            b.wait(scalar, t)
            t = act.after(scalar.activation(z, bank[4][0:HC, :], ACT.Identity, bias=bt[0:HC, TF:TF + 1]))
            bank_use[4].last = [t]
            b.wait(vector, t)
            t = dve.after(vector.scalar_tensor_tensor(out=F, in0=z, scalar=-1.0, in1=z, op0=ALU.mult, op1=ALU.max))
            b.wait(scalar, t)
            t = act.after(scalar.activation(F, F, ACT.Exp, scale=-1.0))
            b.wait(scalar, t)
            t = act.after(scalar.activation(F, F, ACT.Ln, bias=1.0))
            b.wait(vector, t)
            t = dve.after(vector.scalar_tensor_tensor(out=z, in0=z, scalar=0.0, in1=F, op0=ALU.min, op1=ALU.subtract))
            b.acquire(logit_use[0])
            t1 = dve.after(vector.memset(logit[0:HC, 0, :], 1.0))
            b.wait(vector, t, t1)
            f_sum.append(dve.after(vector.tensor_tensor_scan(F, logit[0:HC, 0, :], z, 0.0, ALU.mult, ALU.add)))

        def forget_columns():
            b.wait(tensor, *f_sum)
            b.acquire(bank_use[7])
            for n in range(TT):
                ins = tensor.matmul(bank[7][:, n * HC:n * HC + HC], F[:, n * P:n * P + P], ident[0:HC, 0:HC],
                                    start=n == 0, stop=n == TT - 1, skip_group_check=True)
            t = pe.after(ins)
            b.wait(vector, t)
            t = dve.after(vector.tensor_copy(fcol[:].rearrange("p n h -> p (n h)"), bank[7][:, 0:TT * HC]))
            bank_use[7].last = [t]
            b.wait(scalar, t)

        ada_a = ada_steps(ada_slots(l, 12, 16), (4,), 7)
        b.wait(scalar, *scored)
        tokens = project(0, OQA, OKA, OVA, HA, TA0, True)
        attend(HA, 0, "A", *tokens)
        tokens = project(1, OB, OB + WB, OB + 2 * WB, HB, TB0, False)
        attend(HB, 3, "B", *tokens)
        tokens = project(2, OC, OC + WC, OC + 2 * WC, HC, TC0, False, extra=P)
        attend(HC, 6, "C", *tokens)
        all_done(tensor, vector, scalar)
        att.close()

        ys = ExitStack()
        yh = sb(ys, "y_hi", [P, KT, T], F32R)
        yl = sb(ys, "y_lo", [P, KT, T], F32R)
        all_done(tensor, vector, scalar)
        with ExitStack() as s:
            gate = sb(s, "gates", [P, 6, T])
            gate_use = [Buffer(scalar) for _ in range(6)]
            branch_rows = [P, P, P, P, P, HD, P, P, HD]
            branch_start = [0, P, 2 * P, WA, WA + P, WA + 2 * P, WA + WB, WA + WB + P, WA + WB + 2 * P]
            with b.loop(KT // 2, [*ALLBUF, *gate_use]) as jj:
                for br in range(3):
                    slot = matrix(wi, l, OG + br * D + jj * 256, 256)
                    for q in range(2):
                        bk = (2 * br + q) % 2
                        g = 2 * br + q
                        t = transposed(slot, q * P, h1, [(0, T)], [bk])
                        b.wait(scalar, t)
                        b.acquire(gate_use[g])
                        t = act.after(scalar.activation(gate[:, g, :], bank[bk][:, :], ACT.Sigmoid,
                                                        bias=bg[:, bass.ds(br * KT + jj * 2 + q, 1)]))
                        bank_use[bk].last = [t]
                wb = a["w_branch"][bass.ds(l, 1)].rearrange("l r c -> (l r) c")
                cs = bass.ds(jj * 256, 256)
                pieces = [(slice(n, n + 1), slice(0, 256), rows,
                           wb[r0:r0 + rows, cs].rearrange("(k p) c -> p k c", k=1))
                          for n, (r0, rows) in enumerate(zip(branch_start, branch_rows))]
                slot = weights(9, 256, pieces)
                r, hi, lo, ready = slot
                b.wait(tensor, ready)
                for q in range(2):
                    tb = []
                    for br in range(3):
                        bk = 2 + 3 * q + br
                        b.acquire(bank_use[bk])
                        for n in range(3):
                            k = 3 * br + n
                            rows = branch_rows[k]
                            ins = product(bank[bk][:, :], (hi[0:rows, k, q * P:q * P + P], lo[0:rows, k, q * P:q * P + P]),
                                          (oh[0:rows, k, :], ol[0:rows, k, :]), n == 0, n == 2)
                        tb.append(pe.after(ins))
                    split_use[r].last = [tb[-1]]
                    ts = []
                    for br in range(3):
                        b.wait(vector, tb[br], (act, act.count, act.steps))
                        g = gate[:, 2 * br + q, :]
                        t = dve.after(vector.tensor_tensor(g, bank[2 + 3 * q + br][:, :], g, ALU.mult))
                        bank_use[2 + 3 * q + br].last = [t]
                        ts.append(t)
                    b.wait(vector, *ts)
                    t = dve.after(vector.tensor_tensor(gate[:, q, :], gate[:, q, :], gate[:, 2 + q, :], ALU.add))
                    b.wait(vector, t)
                    t = dve.after(vector.tensor_tensor(gate[:, q, :], gate[:, q, :], gate[:, 4 + q, :], ALU.add))
                    t = split_out(dyn(yh, jj * 2 + q), dyn(yl, jj * 2 + q), gate[:, q, :], t)
                    for n in (q, 2 + q, 4 + q):
                        gate_use[n].last = [t]
            all_done(tensor, vector, scalar)
        residual(a["w_out"], l, lambda k: (yh[:, k, :], yl[:, k, :]), KT, 0, [(TC, TA, 0, 2, 0)])
        ys.close()
        mix.close()

        norm_scales(pcol[:, KT:2 * KT], 4, 3, 0)
        norm([(TC, TA, 0, 0)], hh, hl, [ada_slots(l, 28, 32)])
        with ExitStack() as s:
            uh = sb(s, "hidden_hi", [P, 8, T], F32R)
            ul = sb(s, "hidden_lo", [P, 8, T], F32R)
            sg = sb(s, "silu", [P, 2, T])
            sg_use = [Buffer(scalar), Buffer(scalar)]
            hid = [Buffer(tensor), Buffer(tensor)]
            wf = a["w_ffn_in"]
            all_done(vector, scalar)
            h_ready.update({k: before_loop([t]) for k, t in h_ready.items()})
            for t0, nt in ((0, 8), (8, 8), (16, 6)):
                b.wait(scalar, (pe, pe.count, pe.steps))
                b.wait(vector, (pe, pe.count, pe.steps))
                with b.loop(nt // 2, [*ALLBUF, *sg_use, *hid]) as i:
                    for q in range(2):
                        c0 = (i * 2 + (t0 + q)) * P
                        slot = weights(KT, 256, [(slice(0, KT), slice(0, P), P, rows_of(wf, l, 0, KT, c0, P)),
                                                 (slice(0, KT), slice(P, 2 * P), P, rows_of(wf, l, 0, KT, c0 + FFN, P))])
                        bg_, bu_ = 2 * q, 2 * q + 1
                        tg = transposed(slot, 0, h1, [(0, T)], [bg_])
                        tu = transposed(slot, P, h1, [(0, T)], [bu_])
                        b.wait(scalar, tg)
                        b.acquire(sg_use[q])
                        t = act.after(scalar.activation(sg[:, q, :], bank[bg_][:, :], ACT.Sigmoid))
                        b.wait(vector, t, tg)
                        t = dve.after(vector.tensor_tensor(sg[:, q, :], bank[bg_][:, :], sg[:, q, :], ALU.mult))
                        bank_use[bg_].last = [t]
                        b.wait(vector, t, tu)
                        t = dve.after(vector.tensor_tensor(sg[:, q, :], bank[bu_][:, :], sg[:, q, :], ALU.mult))
                        bank_use[bu_].last = [t]
                        t = split_out(dyn(uh, i * 2 + q), dyn(ul, i * 2 + q), sg[:, q, :], t)
                        sg_use[q].last = hid[q].last = [t]
                residual(a["w_ffn_out"], l, lambda k: (uh[:, k, :], ul[:, k, :]), nt, t0 * P, [(TC, TA, 0, 5, 0)],
                         [h_.last for h_ in hid])
            all_done(tensor, vector, scalar)

    def residual(w, l, h, kt, r0, segments, ready=None):
        if ready is None:
            b.wait(tensor, (dve, dve.count, dve.steps), (act, act.count, act.steps))
        n_seg = len(segments)
        with b.loop(2, ALLBUF) as i:
            if ready is not None:
                h_ready.update({kt - len(ready) + n: before_loop(t) for n, t in enumerate(ready)})
            for q in range(2):
                slot = matrix(w, l, i * 512 + q * 256, 256, kt=kt, r0=r0)
                for c in range(2):
                    tile = i * 4 + 2 * q + c
                    banks = [(2 * q + c) * n_seg + n for n in range(n_seg)]
                    t = transposed(slot, c * P, h, [(h0, h0 + x1 - x0) for x0, x1, _, _, h0 in segments], banks)
                    b.wait(vector, t)
                    for bk, (x0, x1, m, part, _) in zip(banks, segments):
                        xs = dynx(tile, x0, x1)
                        g = mod[:, bass.ds(part * 8 + tile, 1), m]
                        t = dve.after(vector.scalar_tensor_tensor(out=xs, in0=bank[bk][:, 0:x1 - x0], scalar=g, in1=xs,
                                                                  op0=ALU.mult, op1=ALU.add))
                        bank_use[bk].last = [t]

    def dynx(tile, x0, x1):
        return X[:, bass.ds(tile, 1), x0:x1].rearrange("p a n -> p (a n)")

    def scale_norm(g):
        with ExitStack() as s:
            tmp = norm_buffers(s)
            gf = sb(s, "norm_g", [P, KT])
            all_done(vector, scalar, tensor)
            t_g = load(gf[:], g)
            rstd = inverse_root(squares(TC, TA, tmp, 7), TC, TA, tmp, 7)
            b.wait(vector, t_g)
            t_k = [dve.after(vector.scalar_tensor_tensor(out=X[:, k, TC:TA], in0=X[:, k, TC:TA], scalar=gf[:, k:k + 1],
                                                         in1=rstd, op0=ALU.mult, op1=ALU.mult)) for k in range(KT)]
            all_done(vector, scalar, tensor)
        return t_k

    negsel = sb(first, "minus_row_select", [P, HC, P])
    t_ns = load(negsel[0:HC], a["negsel"])
    b.wait(tensor, t_ns)
    condition()
    start = ExitStack()
    first_rows = sb(start, "first_ada_rows", [P, 2, 512])
    t_angles = rope_tables()
    t_x = load(X[:, :, TC:TA], a["x_t"].rearrange("(k p) t -> p k t", p=P))
    t_ctx = load(X[:, :, 0:TC], a["ctx_t"].rearrange("(k p) t -> p k t", p=P))
    ada_first(first_rows)
    start.close()
    rope_sines(t_angles)
    if n_first:
        with b.loop(n_first, ALLBUF) as l:
            first_layer(l)
    first.close()
    scale_norm(a["final1_cols"])

    second = ExitStack()
    gh = sb(second, "h2_hi", [P, KT, TA], F32R)
    gl = sb(second, "h2_lo", [P, KT, TA], F32R)
    cos2 = sb(second, "axial_cos", [P, T])
    sin2 = sb(second, "axial_sin", [P, T])
    perm2 = sb(second, "swap_halves", [P, P])
    edge = sb(second, "edge_factors", [P, 4, 16])
    pcol2 = sb(second, "layer_columns_2", [P, 2 * KT + 4 + 1])
    lamr = sb(second, "lambda_rows", [P, 4, HD])
    lams = sb(second, "lambda_columns", [P, 8])
    stat2 = sb(second, "softmax_stats_2", [P, 4, 8])

    def h2(k):
        return gh[:, k, :], gl[:, k, :]

    CTX, TOK = (0, TC), (TC, TA)

    def second_layer(L, last):
        lam0 = 0.8 - 0.6 * float(np.exp(-0.3 * L))
        all_done(vector, scalar, tensor)
        t_c = load(pcol2[:], a["cols2"][L])
        t_l = load(lamr[:], a["lam"][L:L + 1].to_broadcast((P, 4, HD)))
        b.wait(vector, t_c, t_l)
        b.wait(scalar, t_c, t_l)
        load_bias(DEPTH + L, not last)
        for n in range(2):
            t = dve.after(vector.tensor_tensor(lamr[:, 2 * n, :], lamr[:, 2 * n, :], lamr[:, 2 * n + 1, :], ALU.mult))
            b.wait(vector, t)
            t = dve.after(vector.tensor_reduce(lams[:, n:n + 1], lamr[:, 2 * n, :], AX.X, ALU.add))
        b.wait(scalar, t)
        t = act.after(scalar.activation(lams[:, 2:4], lams[:, 0:2], ACT.Exp))
        b.wait(vector, t)
        t = dve.after(vector.tensor_tensor(lams[:, 4:5], lams[:, 2:3], lams[:, 3:4], ALU.subtract))
        b.wait(vector, t)
        dve.after(vector.tensor_scalar(lams[:, 5:6], lams[:, 4:5], lam0, -1.0, ALU.add, ALU.mult))
        dve.after(vector.tensor_scalar(lams[:, 6:7], pcol2[:, 2 * KT + 4:2 * KT + 5], 1.0 - lam0, None, ALU.mult))
        for m in (1, 2):
            norm_scales(pcol2[:, 0:KT], 1, 0, m)
        norm([(0, TC, 0, 2), (TC, TA, TC, 1)], gh, gl, [ada_slots(DEPTH + L, 8, 14), ada_slots(DEPTH + L, 14, 20)])

        att = ExitStack()
        q_t = sb(att, "q2", [P, NH2, TA])
        k_t = sb(att, "k2", [P, NH2, TA])
        v_n = sb(att, "v2", [P, TA // P, NH2 * P])
        u_t = sb(att, "pool_in", [P, NH2, UPAD])
        prob = sb(att, "maps", [P, 2, 2 * TA])
        probt = sb(att, "map_t", [P, 2, TA])
        tmp = prob[:, 0, 0:T]
        tmp_use = Buffer(vector)
        w = a["w_in_2"]
        all_done(vector, scalar, tensor)
        t_z = dve.after(vector.memset(u_t[:], 0.0))
        b.wait(scalar, t_z)
        segs = [TOK] if last else [CTX, TOK]
        for part, dst in ((0, u_t), (1, q_t), (2, k_t)):
            chunks = [CTX, TOK] if part == 2 else segs
            for half in range(2):
                slot = matrix(w, L, 512 * part + 256 * half, 256)
                for c in range(2):
                    n = 2 * half + c
                    banks = [2 * (n % 2) + i for i in range(len(chunks))]
                    t = transposed(slot, c * P, h2, chunks, banks)
                    b.wait(scalar, t)
                    for bk, (c0, c1) in zip(banks, chunks):
                        if part == 0:
                            o = PAD if c0 == 0 else 3 * PAD
                            t = act.after(scalar.copy(dst[:, n, o + c0:o + c1], bank[bk][:, 0:c1 - c0]))
                        else:
                            t = act.after(scalar.activation(dst[:, n, c0:c1], bank[bk][:, 0:c1 - c0], ACT.Copy,
                                                            scale=HD ** -0.5 if part == 1 else 1.0))
                        bank_use[bk].last = [t]
                    if part:
                        b.wait(vector, t)
                        rope(t, dst[:, n, TC:TA], cos2[:], sin2[:], tmp, tmp_use, 4 + n % 2, perm2[:])
        s_a, s_b = prob[:, 0, 0:UPAD], prob[:, 1, 0:UPAD]
        wp = ada_rows[:].rearrange("p a n -> p (a n)").rearrange("p (g d) -> p g d", g=4)
        b.acquire(tmp_use)
        mix_t = {}

        def centred_mean(g):
            win, u = WINDOWS[g], u_t[:, g, :]
            t = dve.after(vector.tensor_tensor(s_a[:, 1:UPAD], u[:, 0:UPAD - 1], u[:, 1:UPAD], ALU.add))
            cur, nxt = s_a, s_b
            step, lo, hi_ = 1, 1, UPAD
            while 2 * step < win:
                b.wait(vector, t)
                lo, hi_ = lo + step, hi_ - step
                t = dve.after(vector.tensor_tensor(nxt[:, lo:hi_], cur[:, lo - step:hi_ - step],
                                                   cur[:, lo + step:hi_ + step], ALU.add))
                cur, nxt = nxt, cur
                step *= 2
            b.wait(vector, t)
            for c0, c1 in segs:
                o = PAD if c0 == 0 else 3 * PAD
                x0, x1 = o + c0, o + c1
                dve.after(vector.tensor_tensor(cur[:, x0:x0 + 8], cur[:, x0:x0 + 8], edge[:, g, 0:8], ALU.mult))
                t = dve.after(vector.tensor_tensor(cur[:, x1 - 8:x1], cur[:, x1 - 8:x1], edge[:, g, 8:16], ALU.mult))
                b.wait(vector, t)
                t = dve.after(vector.scalar_tensor_tensor(out=u[:, x0:x1], in0=cur[:, x0:x1], scalar=1.0 / win,
                                                          in1=u[:, x0:x1], op0=ALU.mult, op1=ALU.subtract))
            b.wait(vector, t)

        def pool_out(g, c0, c1):
            o = PAD if c0 == 0 else 3 * PAD
            b.acquire(bank_use[6])
            y = bank[6][:, 0:c1 - c0]
            t = pe.after(tensor.matmul(y, wp[:, g, :], u_t[:, g, o + c0:o + c1], start=True, stop=True))
            b.wait(scalar, t)
            scale = pcol2[:, 2 * KT + g:2 * KT + g + 1]
            t = act.after(scalar.activation(gh[:, g, c0:c1], y, ACT.Copy, scale=scale))
            b.wait(vector, t)
            t = dve.after(vector.scalar_tensor_tensor(out=gl[:, g, c0:c1], in0=y, scalar=scale,
                                                      in1=gh[:, g, c0:c1].bitcast(F32), op0=ALU.mult, op1=ALU.subtract))
            bank_use[6].last = mix_t[g] = [t]

        for half in range(2):
            slot = matrix(w, L, 1536 + 256 * half, 256)
            for n in range(TA // P):
                t = natural(slot, 0, 256, h2, n * P, n % 4)
                b.wait(scalar, t)
                t = act.after(scalar.copy(v_n[:, n, 256 * half:256 * half + 256], bank[n % 4][:, 0:256]))
                bank_use[n % 4].last = [t]
            for g in (2 * half, 2 * half + 1):
                centred_mean(g)
        all_done(vector, scalar, tensor)
        t_w = load(wp, a["w_pool_2"][L].rearrange("g c d -> c g d"))

        head_rms = u_t[:, 2:4, :].rearrange("p a n -> p (a n)")[:, 0:TA]
        prob_use = [Buffer(scalar), Buffer(scalar)]
        probt_use = [Buffer(scalar), Buffer(scalar)]
        pair_use = [Buffer(tensor), Buffer(tensor)]
        units = []
        for n in range(NH2):
            if not last:
                units += [(n, t, TC, 0) for t in range(2)]
            units += [(n, t, TA, 1) for t in range(2, TA // P)]
        st, ended, head_use = {}, [], Buffer(scalar)

        def scores(u):
            n, t, nk, _ = units[u]
            q = u % 2
            o = q * 3 * 512
            b.acquire(pair_use[q])
            if nk > 512:
                cuts = [(0, 512, nk), (0, 0, 512), (1, 256, nk), (1, 0, 256)]
            else:
                cuts = [(0, 0, nk), (1, 0, nk)]
            for m, c0, c1 in cuts:
                if (m, c0, nk) == (1, 0, TA):
                    b.wait(tensor, shared)
                at = o + m * max(nk, 512) + c0
                ins = tensor.matmul(psum[:, at:at + c1 - c0], q_t[HD * m:HD * m + HD, n, t * P:t * P + P],
                                    k_t[HD * m:HD * m + HD, n, c0:c1], start=True, stop=True)
                if (m, c0) == (0, 512):
                    shared = pe.after(ins)
            st["s", u] = pe.after(ins)

        def maximum(u):
            n, t, nk, _ = units[u]
            o = (u % 2) * 3 * 512
            b.wait(vector, st["s", u])
            st["m", u] = dve.after(vector.tensor_reduce(
                stat2[:, u % 4, 0:2], psum[:, o:o + 2 * max(nk, 512)].rearrange("p (m k) -> p m k", m=2)[:, :, 0:nk],
                AX.X, ALU.max, negate=True))

        def exponential(u):
            n, t, nk, _ = units[u]
            q = u % 2
            o = q * 3 * 512
            nm, rs = stat2[:, u % 4, 0:2], stat2[:, u % 4, 2:4]
            b.wait(scalar, st["m", u])
            b.acquire(prob_use[q])
            for m in range(2):
                tk = act.after(scalar.activation(prob[:, q, m * nk:m * nk + nk], psum[:, o + m * max(nk, 512):o + m * max(nk, 512) + nk],
                                                 ACT.Exp, bias=nm[:, m:m + 1], accum_out=rs[:, m:m + 1]))
            pair_use[q].last = [tk]
            st["e", u] = tk

        def combine(u):
            n, t, nk, _ = units[u]
            q = u % 2
            rs, rr = stat2[:, u % 4, 2:4], stat2[:, u % 4, 4:6]
            e0, e1 = prob[:, q, 0:nk], prob[:, q, nk:2 * nk]
            b.wait(vector, st["e", u])
            tk = dve.after(vector.reciprocal(rr, rs))
            b.wait(vector, tk)
            tk = dve.after(vector.tensor_scalar(e1, e1, rr[:, 1:2], lams[:, 5:6], ALU.mult, ALU.mult))
            b.wait(vector, tk)
            st["c", u] = dve.after(vector.scalar_tensor_tensor(out=e0, in0=e0, scalar=rr[:, 0:1], in1=e1,
                                                               op0=ALU.mult, op1=ALU.add))

        def turn(u, j0):
            n, t, nk, _ = units[u]
            q = u % 2
            j1 = min(j0 + 4, nk // P)
            if j0 >= j1:
                return
            b.wait(tensor, st["c", u])
            b.acquire(bank_use[6])
            for j in range(j0, j1):
                ins = tensor.transpose(bank[6][:, (j - j0) * P:(j - j0) * P + P], prob[:, q, j * P:j * P + P], ident)
            tk = pe.after(ins)
            prob_use[q].last = [tk]
            st["p", u] = tk

        def take_out(u, j0):
            n, t, nk, _ = units[u]
            q = u % 2
            j1 = min(j0 + 4, nk // P)
            if j0 >= j1:
                return
            b.wait(scalar, st["p", u])
            if j0 == 0:
                b.acquire(probt_use[q])
            tk = act.after(scalar.copy(probt[:, q, j0 * P:j1 * P], bank[6][:, 0:(j1 - j0) * P]))
            bank_use[6].last = [tk]
            st["t", u] = tk

        def values(u):
            n, t, nk, is_tok = units[u]
            q = u % 2
            o = (t - 2) * P if is_tok else t * P
            b.wait(tensor, st["t", u])
            if o == 0:
                b.acquire(bank_use[7])
            for j in range(nk // P):
                ins = tensor.matmul(bank[7][:, o:o + P], v_n[:, j, n * P:n * P + P], probt[:, q, j * P:j * P + P],
                                    start=j == 0, stop=j == nk // P - 1)
            tk = pe.after(ins)
            probt_use[q].last = [tk]
            if t == TA // P - 1 or (not is_tok and t == 1):
                c0, c1 = (TC, TA) if is_tok else (0, TC)
                b.wait(scalar, tk)
                t_o = act.after(scalar.copy(q_t[:, n, c0:c1], bank[7][:, 0:c1 - c0]))
                bank_use[7].last = [t_o]
                if is_tok:
                    ended.append(head_norm(n, t_o))

        def head_norm(n, t_o):
            x0 = TC if last else 0
            ho, rms = q_t[:, n, x0:TA], head_rms[:, x0:TA]
            b.wait(scalar, t_o)
            b.acquire(head_use)
            t_q = act.after(scalar.activation(rms, ho, ACT.Square))
            yield
            for c0, c1 in reversed(segs):
                b.wait(tensor, t_q)
                b.acquire(bank_use[6])
                tk = pe.after(tensor.matmul(bank[6][:, 0:c1 - c0], meanm, head_rms[:, c0:c1], start=True, stop=True))
                b.wait(scalar, tk)
                tk = act.after(scalar.activation(head_rms[:, c0:c1], bank[6][:, 0:c1 - c0], ACT.Sqrt,
                                                 bias=eps[:, 0:1], scale=float(D // P)))
                bank_use[6].last = [tk]
            yield
            b.wait(vector, tk)
            tk = dve.after(vector.reciprocal(rms, rms))
            b.wait(vector, tk)
            t_n = dve.after(vector.scalar_tensor_tensor(out=ho, in0=ho, scalar=lams[:, 6:7], in1=rms,
                                                        op0=ALU.mult, op1=ALU.mult))
            head_use.last = [t_n]
            yield
            b.wait(scalar, t_n)
            t_h = act.after(scalar.copy(gh[:, 4 + n, x0:TA], ho))
            yield
            b.wait(vector, t_h, t_n)
            mix_t[4 + n] = [dve.after(vector.tensor_tensor(gl[:, 4 + n, x0:TA], ho, gh[:, 4 + n, x0:TA].bitcast(F32),
                                                           ALU.subtract))]

        def head_step():
            if ended and next(ended[0], "done") == "done":
                ended.pop(0)

        scores(0)
        for u in range(len(units) + 2):
            if u + 1 < len(units):
                scores(u + 1)
            if u < len(units):
                maximum(u)
                exponential(u)
            if 1 <= u <= len(units):
                combine(u - 1)
                turn(u - 1, 0)
                take_out(u - 1, 0)
            head_step()
            if u >= 2:
                values(u - 2)
            if 1 <= u <= len(units):
                turn(u - 1, 4)
                take_out(u - 1, 4)
            for g in {0: (2,), 1: (3,), 3: (0,), 5: (1,)}.get(u, ()):
                b.wait(tensor, t_w)
                for c0, c1 in segs:
                    pool_out(g, c0, c1)
        while ended:
            head_step()
        all_done(vector, scalar)
        att.close()
        out_segs = [(TC, TA, 1, 2, TC)] if last else [(TC, TA, 1, 2, TC), (0, TC, 2, 2, 0)]
        residual(a["w_out_2"], L, h2, KT, 0, out_segs, [mix_t[k] for k in range(KT)])

        for m in (1, 2):
            norm_scales(pcol2[:, KT:2 * KT], 4, 3, m)
        if last:
            norm([(TC, TA, TC, 1)], gh, gl, [ada_slots(DEPTH + L, 20, 24)])
        else:
            norm([(0, TC, 0, 2), (TC, TA, TC, 1)], gh, gl,
                 [ada_slots(DEPTH + L, 20, 26), ada_slots(DEPTH + L, 26, 32)])
        with ExitStack() as s:
            uh = sb(s, "hidden2_hi", [P, 8, TA], F32R)
            ul = sb(s, "hidden2_lo", [P, 8, TA], F32R)
            sq = sb(s, "relu_squared", [P, 4, T])
            sq_use = [Buffer(scalar), Buffer(scalar)]
            hid_use = Buffer(scalar)
            hid = [Buffer(tensor) for _ in range(4)]
            all_done(vector, scalar)
            h_ready.update({k: before_loop([t]) for k, t in h_ready.items()})
            with b.loop(DFF // D, [*ALLBUF, *sq_use, *hid, hid_use]) as chunk:
                b.acquire(hid_use)
                with b.loop(2, [*ALLBUF, *sq_use, *hid]) as i:
                    for q in range(2):
                        slot = matrix(a["w_mlp1_2"], L, chunk * D + i * 512 + q * 256, 256)
                        for c in range(2):
                            banks = [(2 * q + c) * len(segs) + n for n in range(len(segs))]
                            t = transposed(slot, c * P, h2, segs, banks)
                            for bk, (c0, c1) in zip(banks, segs):
                                sb_ = bk % 2
                                y = sq[:, sb_, 0:c1 - c0]
                                square = sq[:, 2 + sb_, 0:c1 - c0]
                                dst = i * 4 + (2 * q + c)
                                hi, lo = (g_[:, bass.ds(dst, 1), c0:c1].rearrange("p a n -> p (a n)") for g_ in (uh, ul))
                                b.wait(scalar, t)
                                b.acquire(sq_use[sb_])
                                tk = act.after(scalar.activation(y, bank[bk][:, 0:c1 - c0], ACT.Relu))
                                bank_use[bk].last = [tk]
                                b.wait(vector, tk)
                                b.wait(scalar, tk)
                                t_s = dve.after(vector.tensor_tensor(square, y, y, ALU.mult))
                                tk = act.after(scalar.activation(hi, y, ACT.Square))
                                b.wait(vector, tk, t_s)
                                tk = dve.after(vector.tensor_tensor(lo, square, hi.bitcast(F32), ALU.subtract))
                                sq_use[sb_].last = [tk]
                            hid[2 * q + c].last = [tk]
                out_segs = [(x0, x1, m, 5, h0) for x0, x1, m, _, h0 in out_segs]
                residual(a["w_mlp2_2"], L, lambda k: (uh[:, k, :], ul[:, k, :]), KT, chunk * D, out_segs,
                         [h_.last for h_ in hid])
                hid_use.last = [(pe, pe.count, pe.steps)]
            all_done(vector, scalar, tensor)

    load_t = [load(cos2[:], a["cos2"]), load(sin2[:], a["sin2"]), load(perm2[:], a["perm2"]), load(edge[:], a["edge"])]
    b.wait(vector, *load_t)
    b.wait(tensor, *load_t)
    for L in range(n_second):
        second_layer(L, L == DEPTH - 1)
    second.close()

    scaled = scale_norm(a["g_final_cols"])
    out = a["out"].rearrange("(k p) t -> k p t", p=P)
    stores = b.counter("stores", step=16)
    for k in range(KT):
        b.wait(sync, scaled[k])
        t_out = stores.after(sync.dma_start(out[k], X[:, k, TC:TA]))
    b.wait(sync, t_out)
    return b


def columns(v):
    v = np.asarray(v)
    v = v.reshape(v.shape[:-1] + (v.shape[-1] // P, P))
    return np.ascontiguousarray(np.swapaxes(v, -1, -2))


def swap_matrix(half, span):
    m = np.zeros((P, P), np.float32)
    for r in range(P):
        d = r % HD
        if d < span:
            m[r, r + half if d % (2 * half) < half else r - half] = 1.0
    return m


def constants():
    ident = np.eye(P, dtype=np.float32)
    swap = swap_matrix(8, 16)
    dup = np.zeros((P, P), np.float32)
    dup[np.arange(P) % HD, np.arange(P)] = 1.0
    sel = np.zeros((P, P), np.float32)
    for g in range(4):
        sel[32 * g, 0] = sel[32 * g + 1, 1] = sel[32 * g + 2, 2] = 1.0
    consts = np.stack([ident, swap, np.full((P, P), 1.0 / D, np.float32), dup, dup @ swap, sel], 1)
    d = np.arange(P) % HD
    inv = np.where(d < 16, 500000.0 ** (-(d % 8) / 8.0), 0.0)
    sign = np.where(d < 8, -1.0, np.where(d < 16, 1.0, 0.0))
    negsel = np.zeros((HC, HC, P), np.float32)
    for h in range(HC):
        negsel[h, h] = -1.0
    causal = np.where(np.arange(P)[None, :] <= np.arange(P)[:, None], 0.0, NEG)
    t = np.arange(T)
    j = np.arange(HD // 4)
    freq = 10000.0 ** (-j / (HD // 4.0))
    angle = np.concatenate([(t // 64)[:, None] * freq, (t % 64)[:, None] * freq], -1).T
    angle = angle[np.arange(P) % (HD // 2)]
    half = np.where(np.arange(P) % HD < HD // 2, -1.0, 1.0)[:, None]
    edge = np.ones((P, 4, 16), np.float32)
    for g, w in enumerate(WINDOWS):
        for e in range(8):
            edge[:, g, e] = w / min(w, e + w // 2)
            edge[:, g, 8 + e] = w / min(w, (8 - e) + w // 2)
    second = {"cos2": np.cos(angle).astype(np.float32), "sin2": (np.sin(angle) * half).astype(np.float32),
              "perm2": swap_matrix(HD // 2, HD), "edge": edge}
    return {**second, "consts": np.ascontiguousarray(consts), "rope_cols": np.stack([inv, sign], 1).astype(np.float32),
            "negsel": negsel, "causal": causal.astype(np.float32)}


def lay_out(i):
    i = {k: np.asarray(v) for k, v in i.items()}
    b_in = i["b_in"]
    tiles = np.stack([b_in[:, o:o + P] for o in TILES], -1)
    gates = columns(b_in[:, OG:])
    rel = i["rel_bias"]
    rel = np.concatenate([rel, np.repeat(rel[:, :, -1:], REL_ROW - rel.shape[2], 2)], 2)
    a = {
        "x_t": np.ascontiguousarray(i["x"][0].T), "ctx_t": np.ascontiguousarray(i["ctx_2"][0].T),
        "positions": i["positions"], "c_cols": columns(i["c"][0]),
        "ada_w": np.concatenate([i["ada_w"], i["w_ada_2"]]), "ada_b_cols": columns(np.concatenate([i["ada_b"], i["b_ada_2"]])),
        "cols1": np.concatenate([columns(i["norm1_g"]), columns(i["norm2_g"]), tiles, gates], -1),
        "w_in": i["w_in"], "b_in": b_in, "rel": rel, "w_branch": i["w_branch"], "w_out": i["w_out"],
        "final1_cols": columns(i["final_g"]), "w_ffn_in": i["w_ffn_in"], "w_ffn_out": i["w_ffn_out"], "g_final_cols": columns(i["g_final_2"]),
    }
    a.update({
        "c2_cols": columns(i["c_2"][0]), "cctx_cols": columns(i["c_ctx_2"]),
        "cols2": np.concatenate([columns(i["g_mix_2"]), columns(i["g_mlp_2"]), columns(i["s_pool_2"]),
                                 columns(i["g_subln_2"])], -1),
        "lam": np.stack([i["lam_q1_2"], i["lam_k1_2"], i["lam_q2_2"], i["lam_k2_2"]], 1),
        "w_in_2": i["w_in_2"], "w_pool_2": i["w_pool_2"], "w_out_2": i["w_out_2"],
        "w_mlp1_2": i["w_mlp1_2"], "w_mlp2_2": i["w_mlp2_2"],
    })
    a.update(constants())
    return {k: np.ascontiguousarray(v) for k, v in a.items()}


def kernel(**inputs):
    import concourse.bacc as bacc
    from concourse.bass_utils import run_bass_kernel_spmd

    arrays = lay_out(inputs)

    def build(plan):
        nc = bacc.Bacc("TRN2", target_bir_lowering=False, num_devices=1)
        a = {n: nc.dram_tensor(f"in_{n}", v.shape, mybir.dt.from_np(v.dtype), kind="ExternalInput").ap()
             for n, v in arrays.items()}
        a["out"] = nc.dram_tensor("out_t", (D, T), F32, kind="ExternalOutput").ap()
        with program(nc, plan, a).ctx:
            pass
        return nc

    plan = {}
    build(plan)
    nc = build(plan)
    r = run_bass_kernel_spmd(nc, [{f"in_{n}": v for n, v in arrays.items()}], core_ids=[0])
    return np.ascontiguousarray(r.results[0]["out_t"].T)[None]
```
